# Optimizing a Trainium2 kernel written in Bass

```python
import functools
import jax, jax.numpy as jnp
from jax import lax
import numpy as np

D_MODEL = 1024
BATCH = 1
SEQ = 128
DEPTH = 1
DEC_BATCH = 1
DEC_SEQ = 1024
PAST_LEN = 128

GRID_W = 64
N_ATT_HEADS = 8
ATT_HEAD_DIM = 64
ATT_WIDTH = N_ATT_HEADS * ATT_HEAD_DIM
WIN_ROWS = 8
WIN_COLS = 16
N_ML_HEADS = 4
ML_HEAD_DIM = 128
ML_WIDTH = N_ML_HEADS * ML_HEAD_DIM
MIX_WIDTH = ATT_WIDTH + ML_WIDTH
N_GATES = 4 * N_ML_HEADS
PROJ_WIDTH = 3 * ATT_WIDTH + 4 * ML_WIDTH + N_GATES
ML_CHUNK = 64
D_FF = 2816
CONV_WIDTH = 3
ROPE_THETA = 10000.0
Q_BLOCK = 128
EPS = 1e-6

kernel_name = 'hybrid_natten_mlstm_prefix_dit_step'

def rmsnorm(x, g):
    xf = x.astype(jnp.float32)
    y = xf * lax.rsqrt(jnp.mean(xf * xf, axis=-1, keepdims=True) + EPS)
    return y.astype(x.dtype) * g

def adaln(cvec, w_mod, b_mod):
    mod = jax.nn.silu(cvec) @ w_mod + b_mod
    return jnp.split(mod[:, None, :], 6, axis=-1)

def axial_rope(x):
    T, Dh = x.shape[1], x.shape[-1]
    half = Dh // 2
    quarter = half // 2
    pos = jnp.arange(T)
    inv_freq = ROPE_THETA ** (-jnp.arange(quarter, dtype=jnp.float32) / quarter)

    def rot(xa, p):
        ang = p.astype(jnp.float32)[:, None] * inv_freq[None, :]
        cos = jnp.cos(ang)[None, :, None, :]
        sin = jnp.sin(ang)[None, :, None, :]
        x1, x2 = xa[..., :quarter], xa[..., quarter:]
        return jnp.concatenate([x1 * cos - x2 * sin, x1 * sin + x2 * cos], axis=-1)

    out = jnp.concatenate([rot(x[..., :half], pos // GRID_W), rot(x[..., half:], pos % GRID_W)], axis=-1)
    return out.astype(x.dtype)

def context_attention(q, k, v):
    B, S, H, Dh = q.shape
    scale = Dh ** -0.5
    qb = q.reshape(B, S // Q_BLOCK, Q_BLOCK, H, Dh).transpose(1, 0, 2, 3, 4)

    def blk(qi):
        s = jnp.einsum('bqhd,bkhd->bhqk', qi, k).astype(jnp.float32) * scale
        p = jax.nn.softmax(s, axis=-1).astype(v.dtype)
        return jnp.einsum('bhqk,bkhd->bqhd', p, v)

    out = lax.map(blk, qb)
    return out.transpose(1, 0, 2, 3, 4).reshape(B, S, H * Dh)

def neighborhood_attention(q, k, v, k_ctx, v_ctx, rpb):
    B, T, H, Dh = q.shape
    scale = Dh ** -0.5
    rows = T // GRID_W
    kr = min(WIN_ROWS, rows)
    r = jnp.arange(rows)
    rs = jnp.clip(r - kr // 2, 0, rows - kr)
    key_rows = rs[:, None] + jnp.arange(kr)[None, :]
    col = jnp.arange(GRID_W)
    cs = jnp.clip(col - WIN_COLS // 2, 0, GRID_W - WIN_COLS)
    in_win = (col[None, :] >= cs[:, None]) & (col[None, :] < cs[:, None] + WIN_COLS)
    dr_idx = key_rows - r[:, None] + (WIN_ROWS - 1)
    dc_idx = jnp.clip(col[None, :] - col[:, None] + (WIN_COLS - 1), 0, 2 * WIN_COLS - 2)
    bias = rpb.astype(jnp.float32)[:, dr_idx][:, :, :, dc_idx]
    bias = jnp.where(in_win[None, None, None], bias, -jnp.inf)
    bias = bias.transpose(1, 0, 3, 2, 4).reshape(rows, H, GRID_W, kr * GRID_W)
    kg = k.reshape(B, rows, GRID_W, H, Dh)[:, key_rows].reshape(B, rows, kr * GRID_W, H, Dh)
    vg = v.reshape(B, rows, GRID_W, H, Dh)[:, key_rows].reshape(B, rows, kr * GRID_W, H, Dh)
    qg = q.reshape(B, rows, GRID_W, H, Dh)
    n_loc = kr * GRID_W

    def row_block(args):
        qr, kb, vb, br = args
        s_loc = jnp.einsum('bqhd,bkhd->bhqk', qr, kb).astype(jnp.float32) * scale + br[None]
        s_ctx = jnp.einsum('bqhd,bphd->bhqp', qr, k_ctx).astype(jnp.float32) * scale
        p = jax.nn.softmax(jnp.concatenate([s_loc, s_ctx], axis=-1), axis=-1).astype(v.dtype)
        return (jnp.einsum('bhqk,bkhd->bqhd', p[..., :n_loc], vb)
                + jnp.einsum('bhqp,bphd->bqhd', p[..., n_loc:], v_ctx))

    out = lax.map(row_block, (qg.transpose(1, 0, 2, 3, 4), kg.transpose(1, 0, 2, 3, 4),
                              vg.transpose(1, 0, 2, 3, 4), bias))
    return out.transpose(1, 0, 2, 3, 4).reshape(B, T, H * Dh)

def mlstm_scan(q, k, v, log_i, log_f, state):
    B, T, H, D = q.shape
    nc = T // ML_CHUNK

    def chunks(a):
        return a.reshape(B, nc, ML_CHUNK, H, D).transpose(1, 0, 3, 2, 4)

    def gchunks(a):
        return a.reshape(B, nc, ML_CHUNK, H).transpose(1, 0, 3, 2)

    causal = jnp.tril(jnp.ones((ML_CHUNK, ML_CHUNK), dtype=bool))

    def step(carry, xs):
        C0, n0, m0 = carry
        qc, kc, vc, li, lf = xs
        b = jnp.cumsum(lf, axis=-1)
        dmat = jnp.where(causal, b[..., :, None] - b[..., None, :] + li[..., None, :], -jnp.inf)
        inter = b + m0[..., None]
        m = jnp.maximum(inter, jnp.max(dmat, axis=-1))
        w_inter = jnp.exp(inter - m)
        s = jnp.einsum('bhtd,bhsd->bhts', qc, kc) * jnp.exp(dmat - m[..., None])
        num = (jnp.einsum('bhts,bhse->bhte', s, vc)
               + w_inter[..., None] * jnp.einsum('bhtd,bhde->bhte', qc, C0))
        den = jnp.sum(s, axis=-1) + w_inter * jnp.einsum('bhtd,bhd->bht', qc, n0)
        h = num / jnp.maximum(jnp.abs(den), jnp.exp(-m))[..., None]
        b_last = b[..., -1]
        w_end = b_last[..., None] - b + li
        m_new = jnp.maximum(b_last + m0, jnp.max(w_end, axis=-1))
        decay = jnp.exp(b_last + m0 - m_new)
        w = jnp.exp(w_end - m_new[..., None])
        C_new = decay[..., None, None] * C0 + jnp.einsum('bhs,bhsd,bhse->bhde', w, kc, vc)
        n_new = decay[..., None] * n0 + jnp.einsum('bhs,bhsd->bhd', w, kc)
        return (C_new, n_new, m_new), h

    state, h = lax.scan(step, state, (chunks(q), chunks(k), chunks(v), gchunks(log_i), gchunks(log_f)))
    return h.transpose(1, 0, 3, 2, 4).reshape(B, T, H, D), state

def mlstm_bidir(q, k, v, gates, st_f, st_b):
    li_f, f_f, li_b, f_b = jnp.split(gates, 4, axis=-1)
    h_f, st_f = mlstm_scan(q, k, v, li_f, jax.nn.log_sigmoid(f_f), st_f)

    def rev(a):
        return jnp.flip(a, axis=1)

    h_b, st_b = mlstm_scan(rev(q), rev(k), rev(v), rev(li_b), rev(jax.nn.log_sigmoid(f_b)), st_b)
    return h_f + rev(h_b), st_f, st_b

def conv_ffn(h, w_up, conv_w, conv_b, w_down):
    u = h @ w_up
    up = jnp.pad(u, ((0, 0), (1, 1), (0, 0)))
    u = up[:, :-2] * conv_w[0] + up[:, 1:-1] * conv_w[1] + up[:, 2:] * conv_w[2] + conv_b
    gate, val = jnp.split(u, 2, axis=-1)
    return (jax.nn.silu(gate) * val) @ w_down

def mixer(h, w_in, b_gate, q_g, k_g, ml_g, w_out, attend, latent, st_f, st_b):
    B, T, _ = h.shape
    f32 = jnp.float32
    splits = [ATT_WIDTH, 2 * ATT_WIDTH, 3 * ATT_WIDTH, 3 * ATT_WIDTH + ML_WIDTH,
              3 * ATT_WIDTH + 2 * ML_WIDTH, 3 * ATT_WIDTH + 3 * ML_WIDTH, 3 * ATT_WIDTH + 4 * ML_WIDTH]
    aq, ak, av, mq, mk, mv, mo, gt = jnp.split(h @ w_in, splits, axis=-1)
    aq = rmsnorm(aq.reshape(B, T, N_ATT_HEADS, ATT_HEAD_DIM), q_g)
    ak = rmsnorm(ak.reshape(B, T, N_ATT_HEADS, ATT_HEAD_DIM), k_g)
    av = av.reshape(B, T, N_ATT_HEADS, ATT_HEAD_DIM)
    o_att = attend(aq, ak, av)
    mq = mq.reshape(B, T, N_ML_HEADS, ML_HEAD_DIM).astype(f32)
    mk = mk.reshape(B, T, N_ML_HEADS, ML_HEAD_DIM).astype(f32) * ML_HEAD_DIM ** -0.5
    mv = mv.reshape(B, T, N_ML_HEADS, ML_HEAD_DIM).astype(f32)
    if latent:
        mq = axial_rope(mq)
        mk = axial_rope(mk)
    gates = gt.astype(f32) + b_gate.astype(f32)
    h_ml, st_f, st_b = mlstm_bidir(mq, mk, mv, gates, st_f, st_b)
    o_gate = jax.nn.sigmoid(mo.astype(f32)).reshape(B, T, N_ML_HEADS, ML_HEAD_DIM)
    o_ml = rmsnorm(h_ml, ml_g.reshape(N_ML_HEADS, ML_HEAD_DIM).astype(f32)) * o_gate
    o = jnp.concatenate([o_att, o_ml.reshape(B, T, ML_WIDTH).astype(h.dtype)], axis=-1)
    return o @ w_out, ak, av, st_f, st_b

def layer(x, cvec, attend, latent, st_f, st_b, w_mod, b_mod, norm1_g, norm2_g, w_in, b_gate,
          q_g, k_g, ml_g, w_out, w_up, conv_w, conv_b, w_down):
    sh1, sc1, g1, sh2, sc2, g2 = adaln(cvec, w_mod, b_mod)
    h = rmsnorm(x, norm1_g) * (1 + sc1) + sh1
    out, ak, av, st_f, st_b = mixer(h, w_in, b_gate, q_g, k_g, ml_g, w_out, attend, latent, st_f, st_b)
    x = x + g1 * out
    h = rmsnorm(x, norm2_g) * (1 + sc2) + sh2
    x = x + g2 * conv_ffn(h, w_up, conv_w, conv_b, w_down)
    return x, ak, av, st_f, st_b

def setup_inputs(seed: int = 0) -> dict:
    key = jax.random.key(seed)
    ks = jax.random.split(key, 26)
    f32 = jnp.float32

    def nrm(k, shape, s=1.0):
        return jax.random.normal(k, shape, f32) * s

    L = DEPTH
    i_bias = nrm(ks[0], (L, 2, 1, N_ML_HEADS), 0.1)
    f_bias = jnp.linspace(3.0, 6.0, N_ML_HEADS, dtype=f32) + nrm(ks[1], (L, 2, 1, N_ML_HEADS), 0.1)
    b_gate = jnp.concatenate([i_bias, f_bias], axis=2).reshape(L, N_GATES)
    return {
        'x_prompt': nrm(ks[2], (BATCH, SEQ, D_MODEL)),
        'x_sample': nrm(ks[3], (DEC_BATCH, DEC_SEQ, D_MODEL)),
        'cache_k': nrm(ks[4], (DEC_BATCH, L, PAST_LEN, N_ATT_HEADS, ATT_HEAD_DIM)),
        'cache_v': nrm(ks[5], (DEC_BATCH, L, PAST_LEN, N_ATT_HEADS, ATT_HEAD_DIM)),
        'state_C': nrm(ks[6], (DEC_BATCH, L, 2, N_ML_HEADS, ML_HEAD_DIM, ML_HEAD_DIM), 0.1),
        'state_n': nrm(ks[7], (DEC_BATCH, L, 2, N_ML_HEADS, ML_HEAD_DIM), 0.1),
        'state_m': nrm(ks[8], (DEC_BATCH, L, 2, N_ML_HEADS), 0.5),
        'c': nrm(ks[9], (DEC_BATCH, D_MODEL)),
        'c_ctx': nrm(ks[10], (D_MODEL,)),
        'w_mod': nrm(ks[11], (L, D_MODEL, 6 * D_MODEL), 0.5 * D_MODEL ** -0.5),
        'b_mod': nrm(ks[12], (L, 6 * D_MODEL), 0.02),
        'norm1_g': 1.0 + nrm(ks[13], (L, D_MODEL), 0.02),
        'norm2_g': 1.0 + nrm(ks[14], (L, D_MODEL), 0.02),
        'w_in': nrm(ks[15], (L, D_MODEL, PROJ_WIDTH), D_MODEL ** -0.5),
        'b_gate': b_gate,
        'q_norm_g': 1.0 + nrm(ks[16], (L, ATT_HEAD_DIM), 0.02),
        'k_norm_g': 1.0 + nrm(ks[17], (L, ATT_HEAD_DIM), 0.02),
        'rpb': nrm(ks[18], (L, N_ATT_HEADS, 2 * WIN_ROWS - 1, 2 * WIN_COLS - 1), 0.1),
        'ml_norm_g': 1.0 + nrm(ks[19], (L, ML_WIDTH), 0.02),
        'w_out': nrm(ks[20], (L, MIX_WIDTH, D_MODEL), MIX_WIDTH ** -0.5),
        'w_up': nrm(ks[21], (L, D_MODEL, 2 * D_FF), D_MODEL ** -0.5),
        'conv_w': nrm(ks[22], (L, CONV_WIDTH, 2 * D_FF), CONV_WIDTH ** -0.5),
        'conv_b': nrm(ks[23], (L, 2 * D_FF), 0.02),
        'w_down': nrm(ks[24], (L, D_FF, D_MODEL), D_FF ** -0.5),
    }

def reference(x_prompt, x_sample, cache_k, cache_v, state_C, state_n, state_m, c, c_ctx,
              w_mod, b_mod, norm1_g, norm2_g, w_in, b_gate, q_norm_g, k_norm_g, rpb, ml_norm_g,
              w_out, w_up, conv_w, conv_b, w_down):
    f32 = jnp.float32
    x = x_prompt
    B = x_prompt.shape[0]
    zero_state = (jnp.zeros((B, N_ML_HEADS, ML_HEAD_DIM, ML_HEAD_DIM), f32),
                  jnp.zeros((B, N_ML_HEADS, ML_HEAD_DIM), f32),
                  jnp.zeros((B, N_ML_HEADS), f32))
    ks_, vs_, Cs_, ns_, ms_ = [], [], [], [], []
    for l in range(DEPTH):
        x, ak, av, st_f, st_b = layer(
            x, c_ctx[None, :], context_attention, False, zero_state, zero_state,
            w_mod[l], b_mod[l], norm1_g[l], norm2_g[l], w_in[l], b_gate[l], q_norm_g[l], k_norm_g[l],
            ml_norm_g[l], w_out[l], w_up[l], conv_w[l], conv_b[l], w_down[l])
        ks_.append(ak)
        vs_.append(av)
        Cs_.append(jnp.stack([st_f[0], st_b[0]], axis=1))
        ns_.append(jnp.stack([st_f[1], st_b[1]], axis=1))
        ms_.append(jnp.stack([st_f[2], st_b[2]], axis=1))
    y_prompt = x
    new_cache_k = jnp.stack(ks_, axis=1)
    new_cache_v = jnp.stack(vs_, axis=1)
    new_state_C = jnp.stack(Cs_, axis=1)
    new_state_n = jnp.stack(ns_, axis=1)
    new_state_m = jnp.stack(ms_, axis=1)
    x = x_sample
    for l in range(DEPTH):
        attend = functools.partial(neighborhood_attention, k_ctx=cache_k[:, l], v_ctx=cache_v[:, l], rpb=rpb[l])
        st_f = (state_C[:, l, 0].astype(f32), state_n[:, l, 0].astype(f32), state_m[:, l, 0].astype(f32))
        st_b = (state_C[:, l, 1].astype(f32), state_n[:, l, 1].astype(f32), state_m[:, l, 1].astype(f32))
        x, _, _, _, _ = layer(
            x, c, attend, True, st_f, st_b,
            w_mod[l], b_mod[l], norm1_g[l], norm2_g[l], w_in[l], b_gate[l], q_norm_g[l], k_norm_g[l],
            ml_norm_g[l], w_out[l], w_up[l], conv_w[l], conv_b[l], w_down[l])
    y_sample = x
    return (y_prompt, y_sample, new_cache_k, new_cache_v, new_state_C, new_state_n, new_state_m)


_drawn_inputs = setup_inputs


def setup_inputs(seed=0):
    import zlib

    import numpy as np

    out = dict(_drawn_inputs(seed))
    spreads = {}
    factors = {'cache_k': 4.542,
     'cache_v': 3.4,
     'state_C': 8.0,
     'state_n': 8.0,
     'state_m': 8.0,
     'norm2_g': 8.0,
     'q_norm_g': 8.0,
     'k_norm_g': 8.203,
     'rpb': 49.611,
     'ml_norm_g': 25.117,
     'conv_b': 8.0}
    for name, (base, spread) in spreads.items():
        noise = np.random.default_rng([zlib.crc32(name.encode()), seed]).standard_normal(out[name].shape)
        drawn = base * np.exp(spread * noise) if base else spread * noise
        out[name] = __import__('jax').numpy.asarray(drawn.astype(out[name].dtype))
    for name, factor in factors.items():
        out[name] = (out[name] * factor).astype(out[name].dtype)
    return out
```

```python
from contextlib import ExitStack

import concourse.bass as bass
from concourse import mybir

F32 = mybir.dt.float32
ALU = mybir.AluOpType
ACT = mybir.ActivationFunctionType
AX = mybir.AxisListType

P = 128
D = 1024
KT = D // P
CTX = 128
LAT = 1024
NT = (CTX + LAT) // P
GRID_W = 64
AH, AD = 8, 64
AW = AH * AD
MH, MD = 4, 128
MW = MH * MD
NG = 4 * MH
MIX = AW + MW
PW = 3 * AW + 4 * MW
FF = 2816
FT = FF // P
EPS = 1e-6
NEG = -1e30
BLK = 512
AQ, AK, AV, MQ, MK, MV, MO = range(7)
MOD = 6 * D


class Links:

    def __init__(self, eng, sem):
        self.eng, self.sem, self.base, self.k = eng, sem, 0, 0

    def start(self, base):
        self.base, self.k = base, 0

    def tick(self, ins):
        ins.then_inc(self.sem, 1)
        self.k += 1
        return self.base + self.k

    def wait(self, ins):
        self.eng.wait_ge(self.sem, self.tick(ins))


def tile_rows(rows, t):
    return rows[bass.ds(t, 1)].rearrange("a p n -> (a p) n")


def modulation(nc, io, keep):
    NB = MOD // BLK
    with ExitStack() as ctx:
        def sb(name, shape):
            return ctx.enter_context(nc.sbuf_tensor(name, shape, F32))

        def ps(name, shape):
            return ctx.enter_context(nc.psum_tensor(name, shape, F32))

        def sem(name):
            return ctx.enter_context(nc.semaphore(name))

        ring = [sb(f"mod_w{j}", [P, KT, BLK]) for j in range(4)]
        cvec = sb("mod_c", [P, KT, 2])
        cexp = sb("mod_cexp", [P, KT, 2])
        csilu = sb("mod_csilu", [P, KT, 2])
        brow = sb("mod_bias", [2, MOD])
        row = sb("mod_row", [2, MOD])
        sel = sb("mod_sel", [2, 2, P])
        gains = sb("mod_gains", [P, 2, KT])
        acc = [ps(f"mod_acc{j}", [P, BLK]) for j in range(4)]
        cols = ps("mod_cols", [P, BLK])
        gate = [ps(f"mod_gate{j}", [P, BLK]) for j in range(2)]
        small_in = sem("mod_small_in")
        w_in = [sem(f"mod_w_in{j}") for j in range(4)]
        c_exp = sem("mod_c_exp")
        c_silu = sem("mod_c_silu")
        acc_done = sem("mod_acc_done")
        row_done = sem("mod_row_done")
        cols_done = sem("mod_cols_done")
        gate_done = sem("mod_gate_done")
        gate_read = sem("mod_gate_read")
        vec_link = sem("mod_vec_link")
        block = ctx.enter_context(nc.Block())

        @block.sync
        def _(sp):
            sp.dma_start(cvec[:, :, :], io["cT"]).then_inc(small_in, 16)
            sp.dma_start(keep["ident"][:, :], io["ident"]).then_inc(small_in, 16)
            sp.dma_start(brow[:, :], io["b_mod2"]).then_inc(small_in, 16)
            sp.dma_start(sel[:, :, :], io["sel"]).then_inc(small_in, 16)
            sp.dma_start(gains[:, :, :], io["gains"]).then_inc(small_in, 16)

            def load(n, j):
                sp.dma_start(ring[j][:, :, :], io["w_mod"][n]).then_inc(w_in[j], 16)

            for j in range(4):
                load(j, j)
            with sp.Fori(1, NB // 4) as u:
                for j in range(4):
                    n = u * 4
                    sp.wait_ge(acc_done, n + j - 3)
                    load(n + j, j)

        @block.scalar
        def _(act):
            act.wait_ge(small_in, 80)
            act.activation(cexp[:, :, :], cvec[:, :, :], ACT.Exp, scale=-1.0).then_inc(c_exp, 1)

        @block.tensor
        def _(pe):
            pe.wait_ge(c_silu, 1)
            pe.wait_ge(small_in, 80)

            def mul(n, j, first):
                pe.wait_ge(w_in[j], n * 4 + 16 - 4 * j)
                if not first:
                    pe.wait_ge(row_done, n - 3)
                for k in range(KT):
                    mm = pe.matmul(acc[j][0:2, :], csilu[:, k, :], ring[j][:, k, :], start=(k == 0), stop=(k == KT - 1))
                mm.then_inc(acc_done, 1)

            for j in range(4):
                mul(j, j, True)
            with pe.Fori(1, NB // 4) as u:
                for j in range(4):
                    mul(u * 4 + j, j, False)
            pe.wait_ge(row_done, NB)
            for j in range(MOD // P):
                mm = pe.transpose(cols[:, 2 * j:2 * j + 2], row[:, j * P:(j + 1) * P], keep["ident"][0:2, 0:2])
            mm.then_inc(cols_done, 1)
            for v in range(2):
                for h in range(2):
                    i = 2 * v + h
                    if i >= 2:
                        pe.wait_ge(gate_read, i - 1)
                    pe.matmul(gate[h][:, :], sel[:, v, :], row[:, 2 * D + h * BLK:2 * D + (h + 1) * BLK],
                              start=True, stop=True).then_inc(gate_done, 1)

        @block.vector
        def _(dve):
            link = Links(dve, vec_link)
            dve.wait_ge(c_exp, 1)
            link.wait(dve.tensor_scalar(cexp[:, :, :], cexp[:, :, :], 1.0, None, ALU.add))
            link.wait(dve.reciprocal(cexp[:, :, :], cexp[:, :, :]))
            dve.tensor_tensor(csilu[:, :, :], cvec[:, :, :], cexp[:, :, :], ALU.mult).then_inc(c_silu, 1)

            def add_bias(n, j):
                dve.wait_ge(acc_done, n + 1)
                at = bass.ds(n * BLK, BLK)
                dve.tensor_tensor(row[:, at], acc[j][0:2, :], brow[:, at], ALU.add).then_inc(row_done, 1)

            with dve.Fori(0, NB // 4) as u:
                for j in range(4):
                    add_bias(u * 4 + j, j)
            dve.wait_ge(cols_done, 1)
            link.wait(dve.tensor_copy(keep["mod"][:, :, :], cols[:, 0:2 * (MOD // P)].rearrange("p (j v) -> p j v", v=2)))
            for norm in range(2):
                sc = keep["mod"][:, (3 * norm + 1) * KT:(3 * norm + 2) * KT, :]
                link.wait(dve.tensor_scalar(keep["gain"][:, norm, :, :], sc, 1.0, None, ALU.add))
                for v in range(2):
                    dve.tensor_tensor(keep["gain"][:, norm, :, v], keep["gain"][:, norm, :, v], gains[:, norm, :], ALU.mult)
            for i in range(4):
                dve.wait_ge(gate_done, i + 1)
                dve.tensor_copy(keep["g1"][:, i // 2, (i % 2) * BLK:(i % 2 + 1) * BLK], gate[i % 2][:, :])\
                   .then_inc(gate_read, 1)


def projection(nc, io, keep):
    with ExitStack() as ctx:
        def sb(name, shape):
            return ctx.enter_context(nc.sbuf_tensor(name, shape, F32))

        def ps(name, shape):
            return ctx.enter_context(nc.psum_tensor(name, shape, F32))

        def sem(name):
            return ctx.enter_context(nc.semaphore(name))

        w = sb("pj_w", [P, 7, KT, BLK])
        wg = sb("pj_wg", [P, KT, NG])
        xt = [sb(f"pj_x{j}", [P, D]) for j in range(2)]
        xn = sb("pj_xn", [P, D])
        junk = sb("pj_junk", [P, D])
        stat = sb("pj_stat", [P, 2])
        hT = [sb(f"pj_hT{j}", [P, KT, P]) for j in range(2)]
        out = [sb(f"pj_out{j}", [P, 7, BLK]) for j in range(2)]
        raw = sb("pj_raw", [P, 2, BLK])
        tmp = sb("pj_tmp", [P, 2, BLK])
        hs = sb("pj_hs", [P, 2, AH])
        half = sb("pj_half", [P, AH])
        qkg = sb("pj_qkg", [P, 2, AD])
        bg = sb("pj_bg", [P, NG])
        cos = sb("pj_cos", [P, NT, P])
        sin = sb("pj_sin", [P, NT, P])
        acc = [ps(f"pj_acc{j}", [P, BLK]) for j in range(4)]
        tp = [ps(f"pj_tp{j}", [P, BLK]) for j in range(2)]
        small_in = sem("pj_small_in")
        w_in = [sem(f"pj_w_in{j}") for j in range(8)]
        x_in = [sem(f"pj_x_in{j}") for j in range(2)]
        squares = sem("pj_squares")
        mean_sq = sem("pj_mean_sq")
        rstd = sem("pj_rstd")
        xn_done = sem("pj_xn_done")
        tp_done = sem("pj_tp_done")
        tp_read = sem("pj_tp_read")
        acc_done = sem("pj_acc_done")
        acc_read = sem("pj_acc_read")
        head_sq = sem("pj_head_sq")
        head_rstd = sem("pj_head_rstd")
        vec_out = sem("pj_vec_out")
        rows_out = [sem(f"pj_rows_out{j}") for j in range(2)]
        cache_out = sem("pj_cache_out")
        gates_read = sem("pj_gates_read")
        raw_read = sem("pj_raw_read")
        pool_link = sem("pj_pool_link")
        vec_link = sem("pj_vec_link")
        block = ctx.enter_context(nc.Block())

        def done(t, n):
            return t * 8 + n + 1

        def evicted(t, n):
            return t * 7 + n + 1

        @block.sync
        def _(sp):
            def load_x(t, j):
                sp.dma_start(xt[j][:, :], tile_rows(io["x"], t)).then_inc(x_in[j], 16)

            load_x(0, 0)
            sp.dma_start(qkg[:, :, :], io["qkg"]).then_inc(small_in, 16)
            sp.dma_start(bg[:, :], io["bg"]).then_inc(small_in, 16)
            sp.dma_start(cos[:, :, :], io["cos"]).then_inc(small_in, 16)
            sp.dma_start(sin[:, :, :], io["sin"]).then_inc(small_in, 16)
            load_x(1, 1)
            for n in range(7):
                sp.dma_start(w[:, n, :, :], io["w_in"][n]).then_inc(w_in[n], 16)
            sp.dma_start(wg[:, :, :], io["w_gate"]).then_inc(w_in[7], 16)
            for t in range(2, NT):
                sp.wait_ge(xn_done, t - 1)
                load_x(t, t % 2)

        @block.gpsimd
        def _(pool):
            pool.memset(half[:, :], -0.5).then_inc(pool_link, 1)
            pool.wait_ge(pool_link, 1)
            pool.wait_ge(small_in, 64)

            def norm(t):
                pool.wait_ge(mean_sq, t + 1)
                pool.tensor_tensor(stat[:, 1:2], stat[:, 1:2], half[:, 0:1], ALU.pow).then_inc(rstd, 1)

            def heads(t, j, n):
                pool.wait_ge(head_sq, 2 * t + n + 1)
                pool.tensor_tensor(hs[:, n, :], hs[:, n, :], half[:, :], ALU.pow).then_inc(head_rstd, 1)

            def store(t, j):
                pool.wait_ge(vec_out, t + 1)
                pool.wait_ge(acc_read, evicted(t, MO))
                pool.dma_start(tile_rows(io["proj"], t), out[j][:, :, :].rearrange("p b n -> p (b n)")).then_inc(rows_out[j], 16)

            def tile(t, j, more):
                heads(t, j, AQ)
                heads(t, j, AK)
                if more:
                    norm(t + 1)
                store(t, j)

            norm(0)
            tile(0, 0, True)
            pool.dma_start(io["new_k"], out[0][:, AK, :]).then_inc(cache_out, 16)
            pool.dma_start(io["new_v"], out[0][:, AV, :]).then_inc(cache_out, 16)
            with pool.Fori(0, (NT - 3) // 2) as u:
                t = u * 2 + 1
                tile(t, 1, True)
                tile(t + 1, 0, True)
            tile(NT - 2, 1, True)
            tile(NT - 1, 0, False)
            pool.wait_ge(rows_out[0], 16 * ((NT + 1) // 2))
            pool.wait_ge(rows_out[1], 16 * (NT // 2))
            pool.wait_ge(cache_out, 32)

        @block.scalar
        def _(act):
            def square(t, j):
                act.wait_ge(x_in[j], 8 * t + 16 - 8 * j)
                if not isinstance(t, int) or t > 0:
                    act.wait_ge(xn_done, t)
                act.activation(junk[:, :], xt[j][:, :], ACT.Square, accum_out=stat[:, 0:1]).then_inc(squares, 1)

            def evict(t, j, n, warm):
                act.wait_ge(acc_done, done(t, n))
                src = acc[n % 4][:, :]
                if n in (MQ, MK):
                    if warm:
                        act.wait_ge(raw_read, t)
                    act.activation(raw[:, n - MQ, :], src, ACT.Copy, scale=1.0 if n == MQ else MD ** -0.5)\
                       .then_inc(acc_read, 1)
                elif n == MO:
                    act.activation(out[j][:, n, :], src, ACT.Exp, scale=-1.0).then_inc(acc_read, 1)
                else:
                    act.activation(out[j][:, n, :], src, ACT.Copy).then_inc(acc_read, 1)

            def tile(t, j, more, warm, full):
                if full:
                    act.wait_ge(rows_out[j], 8 * (t - j))
                for n in range(7):
                    evict(t, j, n, warm)
                    if n == 3 and more:
                        square(t + 1, 1 - j)

            square(0, 0)
            tile(0, 0, True, False, False)
            tile(1, 1, True, True, False)
            act.wait_ge(cache_out, 32)
            with act.Fori(1, (NT - 1) // 2) as u:
                t = u * 2
                tile(t, 0, True, True, True)
                tile(t + 1, 1, True, True, True)
            tile(NT - 1, 0, False, True, True)

        @block.tensor
        def _(pe):
            def turn(t, warm):
                pe.wait_ge(xn_done, t + 1)
                for k in range(KT):
                    if k % 4 == 0 and warm:
                        pe.wait_ge(tp_read, 2 * t + k // 4 - 1)
                    mm = pe.transpose(tp[k // 4][:, (k % 4) * P:(k % 4 + 1) * P], xn[:, k * P:(k + 1) * P], keep["ident"][:, :])
                    if k % 4 == 3:
                        mm.then_inc(tp_done, 1)

            def tile(t, j, more, warm):
                pe.wait_ge(tp_read, 2 * t + 2)
                for n in range(8):
                    if n >= 4:
                        pe.wait_ge(acc_read, evicted(t, n - 4))
                    elif warm and n == 3:
                        pe.wait_ge(gates_read, t)
                    elif warm:
                        pe.wait_ge(acc_read, evicted(t, n) - 3)
                    if not warm:
                        pe.wait_ge(w_in[n], 16)
                    for k in range(KT):
                        rhs = w[:, n, k, :] if n < 7 else wg[:, k, :]
                        dst = acc[n % 4][:, :] if n < 7 else acc[3][:, 0:NG]
                        mm = pe.matmul(dst, hT[j][:, k, :], rhs, start=(k == 0), stop=(k == KT - 1))
                    mm.then_inc(acc_done, 1)
                    if n == 5 and more:
                        turn(t + 1, True)

            turn(0, False)
            tile(0, 0, True, False)
            with pe.Fori(0, (NT - 3) // 2) as u:
                t = u * 2 + 1
                tile(t, 1, True, True)
                tile(t + 1, 0, True, True)
            tile(NT - 2, 1, True, True)
            tile(NT - 1, 0, False, True)

        @block.vector
        def _(dve):
            link = Links(dve, vec_link)
            dve.wait_ge(small_in, 64)

            def mean_square(t):
                dve.wait_ge(squares, t + 1)
                dve.tensor_scalar(stat[:, 1:2], stat[:, 0:1], 1.0 / D, EPS, ALU.mult, ALU.add).then_inc(mean_sq, 1)

            def normalise(t, j, warm):
                dve.wait_ge(rstd, t + 1)
                if warm:
                    dve.wait_ge(tp_done, 2 * t)
                dve.tensor_scalar(xn[:, :], xt[j][:, :], stat[:, 1:2], None, ALU.mult).then_inc(xn_done, 1)

            def modulate(t, j, v):
                if not isinstance(t, int) or t >= 2:
                    dve.wait_ge(acc_done, done(t - 2, 7))
                for k in range(KT):
                    if k % 4 == 0:
                        dve.wait_ge(tp_done, 2 * t + k // 4 + 1)
                    op = dve.tensor_scalar(hT[j][:, k, :], tp[k // 4][:, (k % 4) * P:(k % 4 + 1) * P],
                                           keep["gain"][:, 0, k, v:v + 1], keep["mod"][:, k, v:v + 1], ALU.mult, ALU.add)
                    if k % 4 == 3:
                        op.then_inc(tp_read, 1)

            def heads(t, j, n):
                dve.wait_ge(acc_read, evicted(t, n))
                q = out[j][:, n, :]
                link.wait(dve.tensor_tensor(tmp[:, 0, :], q, q, ALU.mult))
                link.wait(dve.tensor_reduce(hs[:, n, :], tmp[:, 0, :].rearrange("p (h d) -> p h d", h=AH), AX.X, ALU.add))
                dve.tensor_scalar(hs[:, n, :], hs[:, n, :], 1.0 / AD, EPS, ALU.mult, ALU.add).then_inc(head_sq, 1)

            def head_scale(t, j, n):
                dve.wait_ge(head_rstd, 2 * t + n + 1)
                q = out[j][:, n, :].rearrange("p (h d) -> p h d", h=AH)
                link.wait(dve.tensor_tensor(q, q, hs[:, n, :].rearrange("p (h a) -> p h a", a=1).to_broadcast([P, AH, AD]), ALU.mult))
                link.wait(dve.tensor_tensor(q, q, qkg[:, n:n + 1, :].to_broadcast([P, AH, AD]), ALU.mult))

            def rotary(t, j):
                dve.wait_ge(acc_read, evicted(t, MK))
                x = raw[:, :, :].rearrange("p b (h d) -> p (b h) d", h=MH)
                at = bass.ds(t, 1)
                c = cos[:, at, :].to_broadcast([P, 2 * MH, P])
                dst = out[j][:, MQ:MK + 1, :].rearrange("p b (h d) -> p (b h) d", h=MH)
                dve.tensor_tensor(dst, x, c, ALU.mult)
                xs = raw[:, :, :].rearrange("p b (h g a f) -> p (b h) g a f", h=MH, g=2, a=2)
                ss = sin[:, at, :].rearrange("p t (g a f) -> p t g a f", g=2, a=2)
                ts = tmp[:, :, :].rearrange("p b (h g a f) -> p (b h) g a f", h=MH, g=2, a=2)
                for a in range(2):
                    for g in range(2):
                        op = dve.tensor_tensor(ts[:, :, g, a, :], xs[:, :, g, 1 - a, :],
                                               ss[:, :, g, a, :].to_broadcast([P, 2 * MH, 32]), ALU.mult)
                op.then_inc(raw_read, 1)
                dve.wait_ge(raw_read, t + 1)
                y = out[j][:, MQ:MK + 1, :]
                link.wait(dve.tensor_tensor(y, y, tmp[:, :, :], ALU.add))

            def sigmoid(t, j):
                dve.wait_ge(acc_read, evicted(t, MO))
                o = out[j][:, MO, :]
                link.wait(dve.tensor_scalar(o, o, 1.0, None, ALU.add))
                dve.reciprocal(o, o).then_inc(vec_out, 1)

            def gates(t):
                dve.wait_ge(acc_done, done(t, 7))
                dve.tensor_tensor(keep["gates"][:, bass.ds(t, 1), :].rearrange("p a g -> p (a g)"), acc[3][:, 0:NG], bg[:, :], ALU.add).then_inc(gates_read, 1)

            def tile(t, j, more):
                link.start(PERV * t)
                for n in (AQ, AK):
                    heads(t, j, n)
                if more:
                    mean_square(t + 1)
                for n in (AQ, AK):
                    head_scale(t, j, n)
                if more:
                    normalise(t + 1, 1 - j, True)
                rotary(t, j)
                if more:
                    modulate(t + 1, 1 - j, 1)
                gates(t)
                sigmoid(t, j)
                assert link.k == PERV, link.k

            PERV = 10
            mean_square(0)
            normalise(0, 0, False)
            modulate(0, 0, 0)
            tile(0, 0, True)
            with dve.Fori(0, (NT - 3) // 2) as u:
                t = u * 2 + 1
                tile(t, 1, True)
                tile(t + 1, 0, True)
            tile(NT - 2, 1, True)
            tile(NT - 1, 0, False)



def mlstm(nc, io, keep):
    L = P - 1
    HD = MD + 1
    with ExitStack() as ctx:
        def sb(name, shape):
            return ctx.enter_context(nc.sbuf_tensor(name, shape, F32))

        def ps(name, shape):
            return ctx.enter_context(nc.psum_tensor(name, shape, F32))

        def sem(name):
            return ctx.enter_context(nc.semaphore(name))

        causal = sb("ml_causal", [P, 2, P])
        gsrc = sb("ml_gsrc", [P, 2, P])
        lf = sb("ml_lf", [P, P])
        ones = sb("ml_ones", [P, P])
        zeros = sb("ml_zeros", [P, P])
        scan_in = sb("ml_scan_in", [P, 2, P])
        bsum = sb("ml_bsum", [P, P])
        asc = sb("ml_asc", [P, P])
        mloc = sb("ml_mloc", [P, P])
        nat = sb("ml_nat", [P, 3, P])
        rows = sb("ml_rows", [1, 4, P])
        stm = sb("ml_stm", [1, 2 * MH])
        m0 = sb("ml_m0", [P, 1])
        mb = sb("ml_mb", [P, P])
        absf = sb("ml_absf", [P, P])
        nml = sb("ml_nml", [P, 1])
        quant = sb("ml_quant", [P, 4, P])
        negm = sb("ml_negm", [P, P])
        decay = sb("ml_decay", [P, 1])
        ddiag = sb("ml_ddiag", [P, P])
        cols = sb("ml_cols", [P, 3, P])
        decays = sb("ml_decays", [P, P])
        half = sb("ml_half", [P, NT])
        mlg = sb("ml_gain", [P, MW])
        nat_in = [sb(f"ml_nat_in{j}", [P, 3, NT, MD]) for j in range(2)]
        v_in = [sb(f"ml_v_in{j}", [P, NT, HD]) for j in range(2)]
        bc_in = [sb(f"ml_bc_in{j}", [P, 2, 2, NT, P]) for j in range(2)]
        st = [sb(f"ml_st{j}", [P, 2, 2, HD]) for j in range(2)]
        qkT = sb("ml_qkT", [P, 2, NT, P])
        s_raw = sb("ml_s_raw", [P, NT, P])
        qTw = sb("ml_qTw", [P, 2, NT, P])
        kw = sb("ml_kw", [P, 2, NT, MD])
        st_ctx = [sb(f"ml_st_ctx{j}", [P, 2, HD]) for j in range(2)]
        den = sb("ml_den", [P, NT, 2])
        hid = [sb(f"ml_hid{j}", [P, 2, NT, MD]) for j in range(2)]
        sq = sb("ml_sq", [P, NT, MD])
        rs = sb("ml_rs", [P, NT])
        tq = [ps(f"ml_tq{j}", [P, 4, P]) for j in range(2)]
        num = [ps(f"ml_num{j}", [P, 2, HD]) for j in range(4)]
        upd = [ps(f"ml_upd{j}", [P, 2, HD]) for j in range(2)]

        const_in = sem("ml_const_in")
        gv = sem("ml_gate_vec")
        ga = sem("ml_gate_act")
        gp = sem("ml_gate_pe")
        rows_out = sem("ml_rows_out")
        m_out = sem("ml_m_out")
        consts = sem("ml_consts")
        head_in = [sem(f"ml_head_in{j}") for j in range(2)]
        bc_landed = [sem(f"ml_bc_landed{j}") for j in range(2)]
        turned = sem("ml_turned")
        turned_read = sem("ml_turned_read")
        shifted = sem("ml_shifted")
        masked = sem("ml_masked")
        weights = sem("ml_weights")
        scores = sem("ml_scores")
        keyw = sem("ml_keyw")
        qw = sem("ml_qw")
        upd_done = sem("ml_upd_done")
        st_new = sem("ml_st_new")
        num_done = sem("ml_num_done")
        den_done = sem("ml_den_done")
        num_read = sem("ml_num_read")
        added = sem("ml_added")
        squared = sem("ml_squared")
        mean_sq = sem("ml_mean_sq")
        rstd = sem("ml_rstd")
        scaled = sem("ml_scaled")
        gated = sem("ml_gated")
        head_out = [sem(f"ml_head_out{j}") for j in range(2)]
        state_out = [sem(f"ml_state_out{j}") for j in range(2)]
        vec_link = sem("ml_vec_link")
        block = ctx.enter_context(nc.Block())

        ident = keep["ident"]
        UPDATES = NT - 1
        GROUPS = [(i, t) for i in range(3) for t in range(0, NT, 4)]

        def tiles_of(s):
            return (s, NT - s if s else 0)

        def row_of(r, t, h):
            return 64 * r + MH * t + h

        @block.sync
        def _(sp):
            sp.dma_start(causal[:, :, :], io["causal"]).then_inc(const_in, 16)
            sp.dma_start(stm[:, :], io["stm"]).then_inc(const_in, 16)
            sp.dma_start(mlg[:, :], io["mlg"]).then_inc(const_in, 16)

            def load_rows(h, j):
                for i, b in enumerate((MQ, MK, MO)):
                    at = b * BLK + h * MD
                    sp.dma_start(nat_in[j][:, i, :, :], io["proj"][:, :, at:at + MD].rearrange("t p d -> p t d"))\
                      .then_inc(head_in[j], 16)
                at = MV * BLK + h * MD
                sp.dma_start(v_in[j][:, :, 0:MD], io["proj"][:, :, at:at + MD].rearrange("t p d -> p t d")).then_inc(head_in[j], 16)
                sp.dma_start(st[j][:, 0, :, :], io["stC"][:, h].rearrange("r d e -> d r e")).then_inc(head_in[j], 16)

            def load_bc(h, j):
                for k in range(2):
                    for r in range(2):
                        src = io["mrows"][k:k + 1, r, 0:NT, h, :].to_broadcast([P, NT, P])
                        sp.dma_start(bc_in[j][:, k, r, :, :], src).then_inc(bc_landed[j], 16)

            load_rows(0, 0)
            load_rows(1, 1)
            sp.wait_ge(ga, 6)
            sp.wait_ge(gv, 4)
            sp.dma_start(io["mrows"][0].rearrange("r t h n -> (r t h) n"), negm[:, :]).then_inc(rows_out, 16)
            sp.dma_start(io["mrows"][1].rearrange("r t h n -> (r t h) n"), quant[:, 3, :]).then_inc(rows_out, 16)
            for r in range(2):
                sp.dma_start(io["new_m"][r:r + 1, :], rows[:, 2, 64 * r:64 * r + MH]).then_inc(m_out, 16)
            sp.wait_ge(rows_out, 32)
            load_bc(0, 0)
            load_bc(1, 1)
            for h in range(2, MH):
                j = h % 2
                sp.wait_ge(head_out[j], 16)
                load_rows(h, j)
                load_bc(h, j)
            sp.wait_ge(m_out, 32)

        @block.tensor
        def _(pe):
            pe.wait_ge(gv, 1)
            pe.transpose(tq[0][:, 0, :], gsrc[:, 0, :], ident[:, :])
            pe.transpose(tq[0][:, 1, :], lf[:, :], ident[:, :]).then_inc(gp, 1)
            pe.wait_ge(gv, 2)
            pe.matmul(tq[1][0:1, 0, :], bsum[:, L:P], ident[:, :], start=True, stop=True)
            pe.matmul(tq[1][0:1, 1, :], mloc[:, L:P], ident[:, :], start=True, stop=True).then_inc(gp, 1)
            pe.wait_ge(gv, 3)
            pe.matmul(tq[0][:, 0, 0:1], rows[:, 3, :], ident[0:1, 0:1], start=True, stop=True).then_inc(gp, 1)
            pe.wait_ge(gv, 5)
            pe.wait_ge(ga, 6)
            for i in range(3):
                pe.transpose(tq[1][:, i, :], quant[:, i, :], ident[:, :])
            pe.matmul(tq[0][:, 0, :], ones[:, :], ddiag[:, :], start=True, stop=True).then_inc(gp, 1)
            pe.wait_ge(gv, 6)

            for h in range(MH):
                j = h % 2
                pe.wait_ge(head_in[j], 80 * (h // 2 + 1))
                for g, (i, t0) in enumerate(GROUPS):
                    n = len(GROUPS) * h + g
                    if n >= 2:
                        pe.wait_ge(turned_read, n - 1)
                    if i == 2:
                        pe.wait_ge(turned_read, len(GROUPS) * h + 6)
                    for t in range(t0, min(t0 + 4, NT)):
                        if i < 2:
                            mm = pe.transpose(tq[n % 2][:, t - t0, :], nat_in[j][:, i, t, :], ident[:, :])
                        else:
                            mm = pe.matmul(tq[n % 2][:, t - t0, :], qkT[:, 1, t, :], qkT[:, 0, t, :], start=True, stop=True)
                    mm.then_inc(turned, 1)
                pe.wait_ge(keyw, h + 1)
                for s in range(NT):
                    if s < UPDATES:
                        u = UPDATES * h + s
                        if u >= 2:
                            pe.wait_ge(st_new, u - 1)
                        for r, t in enumerate(tiles_of(s)):
                            mm = pe.matmul(upd[s % 2][:, r, :], kw[:, r, t, :], v_in[j][:, t, :], start=True, stop=True)
                        mm.then_inc(upd_done, 1)
                    if s == 0:
                        pe.wait_ge(scores, h + 1)
                        pe.wait_ge(qw, h + 1)
                    if s > 1:
                        pe.wait_ge(st_new, UPDATES * h + s)
                    n = NT * h + s
                    if n >= 4:
                        pe.wait_ge(num_read, n - 3)
                    for r, t in enumerate(tiles_of(s)):
                        mm = pe.matmul(num[n % 4][:, r, :], bc_in[j][:, 0, r, t, :], v_in[j][:, t, :], start=True, stop=(s == 0))
                        if s:
                            mm = pe.matmul(num[n % 4][:, r, :], qTw[:, r, t, :], st[j][:, (s - 1) % 2, r, :], start=False, stop=True)
                    mm.then_inc(num_done, 1)

        @block.scalar
        def _(act):
            act.wait_ge(consts, 1)
            act.activation(lf[:, :], absf[:, :], ACT.Exp, scale=-1.0).then_inc(ga, 1)
            act.wait_ge(ga, 1)
            act.activation(lf[:, :], lf[:, :], ACT.Ln, bias=1.0).then_inc(ga, 1)
            act.wait_ge(gv, 4)
            act.activation(quant[:, 1, :], nat[:, 0, :], ACT.Exp, bias=nml[:, 0:1]).then_inc(ga, 1)
            act.activation(quant[:, 2, :], mb[:, :], ACT.Exp, scale=-1.0).then_inc(ga, 1)
            act.activation(quant[:, 3, :], nat[:, 1, :], ACT.Exp, scale=-1.0, bias=m0[:, 0:1]).then_inc(ga, 1)
            act.activation(decay[:, :], m0[:, :], ACT.Exp, bias=nml[:, 0:1]).then_inc(ga, 1)
            for h in range(MH):
                j = h % 2
                for g, (i, t0) in enumerate(GROUPS):
                    n = len(GROUPS) * h + g
                    nt = min(4, NT - t0)
                    act.wait_ge(turned, n + 1)
                    if h and g == 0:
                        act.wait_ge(qw, h)
                    if h and i == 2 and t0 == 0:
                        act.wait_ge(scores, h)
                    dst = s_raw[:, t0:t0 + nt, :] if i == 2 else qkT[:, i, t0:t0 + nt, :]
                    act.activation(dst, tq[n % 2][:, 0:nt, :], ACT.Copy).then_inc(turned_read, 1)
                    if g == 3:
                        act.wait_ge(masked, h + 1)
                        w = bc_in[j][:, 0, :, :, :]
                        act.activation(w, w, ACT.Exp).then_inc(weights, 1)
                if h >= 2:
                    act.wait_ge(head_out[j], 16 * (h // 2))
                for s in range(NT):
                    n = NT * h + s
                    act.wait_ge(den_done, n + 1)
                    for r, t in enumerate(tiles_of(s)):
                        op = act.activation(hid[j][:, r, t, :], num[n % 4][:, r, 0:MD], ACT.Copy, scale=den[:, s, r:r + 1])
                    op.then_inc(num_read, 1)
                act.wait_ge(added, h + 1)
                act.activation(sq[:, :, :], hid[j][:, 0, :, :], ACT.Square).then_inc(squared, 1)

        @block.gpsimd
        def _(pool):
            pool.memset(half[:, :], -0.5)
            for h in range(MH):
                j = h % 2
                pool.wait_ge(shifted, h + 1)
                pool.wait_ge(const_in, 48)
                for r in range(2):
                    w = bc_in[j][:, 0, r, :, :]
                    op = pool.tensor_tensor(w, w, causal[:, r:r + 1, :].to_broadcast([P, NT, P]), ALU.add)
                op.then_inc(masked, 1)
                pool.wait_ge(num_read, NT * (h + 1))
                pool.tensor_tensor(hid[j][:, 0, :, :], hid[j][:, 0, :, :], hid[j][:, 1, :, :], ALU.add).then_inc(added, 1)
                pool.wait_ge(mean_sq, h + 1)
                pool.tensor_tensor(rs[:, :], rs[:, :], half[:, :], ALU.pow).then_inc(rstd, 1)
                pool.wait_ge(scaled, h + 1)
                pool.tensor_tensor(hid[j][:, 0, :, :], hid[j][:, 0, :, :], nat_in[j][:, 2, :, :], ALU.mult).then_inc(gated, 1)
                pool.wait_ge(gated, h + 1)
                at = AW + h * MD
                pool.dma_start(io["mix"][:, :, at:at + MD].rearrange("t p d -> p t d"), hid[j][:, 0, :, :]).then_inc(head_out[j], 16)
                pool.wait_ge(st_new, UPDATES * h + 1)
                pool.dma_start(io["new_st"][:, h].rearrange("r d e -> d r e"), st_ctx[j][:, :, :]).then_inc(state_out[j], 16)
            for j in range(2):
                pool.wait_ge(head_out[j], 16 * MH // 2)
                pool.wait_ge(state_out[j], 16 * MH // 2)

        @block.vector
        def _(dve):
            link = Links(dve, vec_link)
            dve.wait_ge(const_in, 48)
            for x in (gsrc, zeros, rows):
                dve.memset(x[:], 0.0)
            for j in range(2):
                dve.memset(v_in[j][:, :, MD:HD], 1.0)
            link.wait(dve.memset(ones[:, :], 1.0))
            for r in range(2):
                for i in range(2):
                    op = dve.tensor_copy(gsrc[:, i, 64 * r:64 * r + NT * MH].rearrange("p (t h) -> p t h", h=MH),
                                         keep["gates"][:, :, 8 * r + 4 * i:8 * r + 4 * i + 4])
            link.wait(op)
            f = gsrc[:, 1, :]
            link.wait(dve.tensor_scalar(absf[:, :], f, -1.0, None, ALU.mult))
            dve.tensor_tensor(absf[:, :], absf[:, :], f, ALU.max).then_inc(consts, 1)
            dve.wait_ge(ga, 2)
            dve.scalar_tensor_tensor(out=lf[:, :], in0=f, scalar=0.0, in1=lf[:, :], op0=ALU.min, op1=ALU.subtract).then_inc(gv, 1)
            dve.wait_ge(gp, 1)
            dve.tensor_copy(scan_in[0:64, :, :], tq[0][0:64, 0:2, :])
            link.wait(dve.tensor_copy(scan_in[64:P, :, :], tq[0][64:P, 0:2, ::-1]))
            link.wait(dve.tensor_tensor_scan(bsum[:, :], scan_in[:, 1, :], zeros[:, :], 0.0, ALU.add, ALU.add))
            link.wait(dve.tensor_tensor(asc[:, :], scan_in[:, 0, :], bsum[:, :], ALU.subtract))
            dve.tensor_tensor_scan(mloc[:, :], asc[:, :], asc[:, :], -3e38, ALU.max, ALU.max).then_inc(gv, 1)
            dve.wait_ge(gp, 2)
            link.wait(dve.tensor_copy(rows[:, 0:2, :], tq[1][0:1, 0:2, :]))
            for r in range(2):
                for h in range(MH):
                    a = 64 * r + MH + h
                    cut = slice(a, a + MH * 7 + 1, MH) if r == 0 else slice(a + MH * 7, a - 1, -MH)
                    dve.tensor_tensor_scan(rows[:, 2, cut], rows[:, 1, cut], rows[:, 0, cut], stm[:, MH * r + h:MH * r + h + 1],
                                           ALU.max, ALU.add)
                c = slice(64 * r, 64 * r + MH)
                op = dve.scalar_tensor_tensor(out=rows[:, 2, c], in0=rows[:, 1, c], scalar=0.0, in1=rows[:, 0, c],
                                              op0=ALU.max, op1=ALU.add)
            link.wait(op)
            dve.tensor_copy(rows[:, 3, 8:36], rows[:, 2, 4:32])
            dve.tensor_copy(rows[:, 3, 68:96], rows[:, 2, 72:100])
            dve.tensor_copy(rows[:, 3, 4:8], stm[:, 0:MH])
            dve.tensor_copy(rows[:, 3, 96:100], stm[:, MH:2 * MH]).then_inc(gv, 1)
            dve.wait_ge(gp, 3)
            link.wait(dve.tensor_copy(m0[:, :], tq[0][:, 0, 0:1]))
            link.wait(dve.tensor_scalar(mloc[:, :], mloc[:, :], m0[:, 0:1], None, ALU.max))
            dve.tensor_scalar(nml[:, :], mloc[:, L:P], -1.0, None, ALU.mult)
            for i, x in enumerate((asc, mloc, bsum)):
                dve.tensor_copy(nat[0:64, i, :], x[0:64, :])
                op = dve.tensor_copy(nat[64:P, i, :], x[64:P, ::-1])
            link.wait(op)
            dve.tensor_tensor(mb[:, :], nat[:, 1, :], nat[:, 2, :], ALU.add)
            dve.tensor_scalar(negm[:, :], nat[:, 1, :], -1.0, None, ALU.mult).then_inc(gv, 1)
            dve.tensor_copy(quant[:, 0, :], nat[:, 0, :])
            dve.wait_ge(ga, 6)
            dve.tensor_scalar(ddiag[:, :], ident[:, :], decay[:, 0:1], None, ALU.mult).then_inc(gv, 1)
            dve.wait_ge(gp, 4)
            dve.tensor_copy(cols[:, :, :], tq[1][:, 0:3, :])
            dve.tensor_copy(decays[:, :], tq[0][:, 0, :]).then_inc(gv, 1)
            dve.wait_ge(gv, 6)

            def by_tile(i, h, n):
                c = cols[:, i, :].rearrange("p (r t h) -> p r t h", r=2, h=MH)[:, :, 0:NT, h:h + 1]
                return c.to_broadcast([P, 2, NT, n])

            for h in range(MH):
                j = h % 2
                dve.wait_ge(bc_landed[j], 64 * (h // 2 + 1))
                dve.wait_ge(head_in[j], 80 * (h // 2 + 1))
                w = bc_in[j][:, 0, :, :, :]
                dve.tensor_tensor(w, w, by_tile(0, h, P), ALU.add).then_inc(shifted, 1)
                if h:
                    dve.wait_ge(num_done, NT * h)
                for r in range(2):
                    c = cols[:, 1, :].rearrange("p (r t h) -> p r t h", r=2, h=MH)[:, r, 0:NT, h:h + 1]
                    op = dve.tensor_tensor(kw[:, r, :, :], nat_in[j][:, 1, :, :], c.to_broadcast([P, NT, MD]), ALU.mult)
                op.then_inc(keyw, 1)
                dve.wait_ge(turned_read, len(GROUPS) * h + 3)
                for r in range(2):
                    op = dve.tensor_tensor(qTw[:, r, :, :], qkT[:, 0, :, :], bc_in[j][:, 1, r, :, :], ALU.mult)
                op.then_inc(qw, 1)
                dve.wait_ge(turned_read, len(GROUPS) * (h + 1))
                dve.wait_ge(weights, h + 1)
                for r in range(2):
                    w = bc_in[j][:, 0, r, :, :]
                    op = dve.tensor_tensor(w, w, s_raw[:, :, :], ALU.mult)
                op.then_inc(scores, 1)
                for s in range(NT):
                    n = NT * h + s
                    if s < UPDATES:
                        dve.wait_ge(upd_done, UPDATES * h + s + 1)
                        if s == 0:
                            if h >= 2:
                                dve.wait_ge(state_out[j], 16 * (h // 2))
                            dve.tensor_copy(st_ctx[j][:, :, :], upd[0][:, :, :]).then_inc(st_new, 1)
                        else:
                            if s > 1:
                                dve.wait_ge(num_done, n)
                            dve.wait_ge(st_new, UPDATES * h + s)
                            for r, t in enumerate(tiles_of(s)):
                                c = row_of(r, t, h)
                                op = dve.scalar_tensor_tensor(out=st[j][:, s % 2, r, :], in0=st[j][:, (s - 1) % 2, r, :],
                                                              scalar=decays[:, c:c + 1], in1=upd[s % 2][:, r, :],
                                                              op0=ALU.mult, op1=ALU.add)
                            op.then_inc(st_new, 1)
                    dve.wait_ge(num_done, n + 1)
                    if n >= 1 and s == 0 and h:
                        dve.wait_ge(num_read, n)
                    for r, t in enumerate(tiles_of(s)):
                        c = row_of(r, t, h)
                        op = dve.tensor_scalar(den[:, s, r:r + 1], num[n % 4][:, r, MD:HD], -1.0, cols[:, 2, c:c + 1],
                                               ALU.mult, ALU.max)
                    link.wait(op)
                    op = dve.tensor_tensor(den[:, s, :], den[:, s, :], num[n % 4][:, :, MD], ALU.max)
                    link.wait(op)
                    dve.reciprocal(den[:, s, :], den[:, s, :]).then_inc(den_done, 1)
                dve.wait_ge(squared, h + 1)
                link.wait(dve.tensor_reduce(rs[:, :], sq[:, :, :], AX.X, ALU.add))
                dve.tensor_scalar(rs[:, :], rs[:, :], 1.0 / MD, EPS, ALU.mult, ALU.add).then_inc(mean_sq, 1)
                dve.wait_ge(rstd, h + 1)
                y = hid[j][:, 0, :, :]
                link.wait(dve.tensor_tensor(y, y, rs[:, :].rearrange("p (t a) -> p t a", a=1).to_broadcast([P, NT, MD]), ALU.mult))
                dve.tensor_tensor(y, y, mlg[:, h * MD:(h + 1) * MD].rearrange("p (a d) -> p a d", a=1).to_broadcast([P, NT, MD]),
                                  ALU.mult).then_inc(scaled, 1)



def attention(nc, io, keep):
    SCALE = AD ** -0.5
    WR = 8
    JR = 14
    HP = AH // 2
    LT = NT - 1
    WINDOWS = []
    for i in range(LT):
        first = [min(max(r - WR // 2, 0), LAT // GRID_W - WR) for r in (2 * i, 2 * i + 1)]
        WINDOWS.append((first[0], first[1] + WR - first[0], first[0] - 2 * i + 7 - 1, first[1] != first[0]))
    with ExitStack() as ctx:
        def sb(name, shape):
            return ctx.enter_context(nc.sbuf_tensor(name, shape, F32))

        def ps(name, shape):
            return ctx.enter_context(nc.psum_tensor(name, shape, F32))

        def sem(name):
            return ctx.enter_context(nc.semaphore(name))

        qk_nat = sb("at_qk_nat", [P, NT + 1, 2, AW])
        v_nat = sb("at_v_nat", [P, NT + 1, AW])
        qT = sb("at_qT", [P, HP, NT, P])
        kT = sb("at_kT", [P, HP, NT + 1, P])
        window = sb("at_window", [P, GRID_W])
        rowmask = sb("at_rowmask", [P, WR + 1])
        zeros = sb("at_zeros", [P, P])
        table = [sb(f"at_table{j}", [P, JR, GRID_W]) for j in range(2)]
        inner = [sb(f"at_inner{j}", [P, WR + 1, GRID_W]) for j in range(2)]
        prob = [sb(f"at_prob{j}", [P, 11 * GRID_W]) for j in range(3)]
        probT = [sb(f"at_probT{j}", [P, 6, P]) for j in range(2)]
        low = sb("at_low", [P, 9 * AH, 2])
        total = sb("at_total", [P, 9 * AH])
        heads = [sb(f"at_heads{j}", [P, LT, 2, AD]) for j in range(2)]
        first_rows = sb("at_first_rows", [P, AH, AD])
        score = [ps(f"at_score{j}", [P, 2 * BLK]) for j in range(2)]
        turn = [ps(f"at_turn{j}", [P, 4, P]) for j in range(2)]
        outp = [ps(f"at_out{j}", [P, 8, AD]) for j in range(2)]

        const_in = sem("at_const_in")
        tile_in = [sem(f"at_tile_in{j}") for j in range(NT + 1)]
        table_in = [sem(f"at_table_in{j}") for j in range(2)]
        table_ready = sem("at_table_ready")
        spread = sem("at_spread")
        laid = sem("at_laid")
        laid_vec = sem("at_laid_vec")
        laid_act = sem("at_laid_act")
        scored = sem("at_scored")
        biased = sem("at_biased")
        expd = sem("at_expd")
        turned = [sem(f"at_turned{j}") for j in range(2)]
        taken = [sem(f"at_taken{j}") for j in range(2)]
        summed = sem("at_summed")
        scaled = sem("at_scaled")
        out_free = sem("at_out_free")
        pair_out = [sem(f"at_pair_out{j}") for j in range(2)]
        first_out = sem("at_first_out")
        vec_link = sem("at_vec_link")
        pool_link = sem("at_pool_link")
        block = ctx.enter_context(nc.Block())

        units = []
        for h in range(AH):
            units.append((h, 0))
        for h in range(AH):
            for i in range(LT):
                units.append((h, i + 1))
        N = len(units)

        def local_cols(t):
            return GRID_W * WINDOWS[t - 1][1] if t else 0

        def pieces(h, t):
            rows = slice(AD * (h % 2), AD * (h % 2) + AD)
            if t == 0:
                return [(0, P, kT[rows, h // 2, 0, :])]
            u0, nr, _, _ = WINDOWS[t - 1]
            keys = kT[rows, h // 2, 1:, :].rearrange("p t n -> p (t n)")
            out = [(0, BLK, keys[:, GRID_W * u0:GRID_W * u0 + BLK])]
            n = GRID_W * nr
            if n > BLK:
                out.append((BLK, n - BLK, keys[:, GRID_W * u0 + BLK:GRID_W * u0 + n]))
            return out + [(n, P, kT[rows, h // 2, NT, :])]

        def blocks(h, t):
            cols = slice(AD * h, AD * h + AD)
            if t == 0:
                return [(0, P, v_nat[:, 0, cols])]
            u0, nr, _, _ = WINDOWS[t - 1]
            n, out = GRID_W * nr, []
            for c in range(0, n, P):
                k = min(P, n - c)
                out.append((c, k, v_nat[0:k, 1 + (GRID_W * u0 + c) // P, cols]))
            return out + [(n, P, v_nat[:, NT, cols])]

        LAY = [(0, hp, t) for hp in range(HP) for t in range(NT)] + [(1, hp, t) for hp in range(HP) for t in range(NT + 1)]
        GROUPS = [LAY[g:g + 4] for g in range(0, len(LAY), 4)]

        def lay_dst(i, hp, t):
            return (qT if i == 0 else kT)[:, hp, t, :]

        def store(eng, hp):
            eng.wait_ge(scaled, 2 * hp + 3)
            eng.dma_start(io["mix"][1:NT, :, hp * P:(hp + 1) * P].rearrange("t p d -> p t d"),
                          heads[hp % 2][:, :, :, :].rearrange("p t b d -> p t (b d)")).then_inc(pair_out[hp % 2], 16)

        @block.sync
        def _(sp):
            for h in range(AH):
                sp.dma_start(io["bias_rows"][h], io["toeplitz"][h:h + 1, :].to_broadcast([GRID_W, 15 * 127])).then_inc(spread, 16)
            sp.dma_start(window[:, :], io["window"]).then_inc(const_in, 16)
            sp.dma_start(rowmask[:, :], io["rowmask"]).then_inc(const_in, 16)
            for t in range(NT):
                sp.dma_start(qk_nat[:, t, :, :], io["proj"][t, :, 0:2 * AW].rearrange("p (b n) -> p b n", b=2)).then_inc(tile_in[t], 16)
                sp.dma_start(v_nat[:, t, :], io["proj"][t, :, 2 * AW:3 * AW]).then_inc(tile_in[t], 16)
            sp.dma_start(qk_nat[:, NT, 1, :], io["ck"]).then_inc(tile_in[NT], 16)
            sp.dma_start(v_nat[:, NT, :], io["cv"]).then_inc(tile_in[NT], 16)
            sp.wait_ge(spread, 16 * AH)
            for h in range(AH):
                if h >= 2:
                    sp.wait_ge(biased, AH + LT * (h - 1))
                rows = io["bias_rows"]
                for half in range(2):
                    src = bass.AP(tensor=rows.tensor, offset=h * GRID_W * 15 * 127 + (1 - half) * 127 + GRID_W - 1,
                                  ap=[[15 * 127 - 1, GRID_W], [127, JR], [1, GRID_W]])
                    sp.dma_start(table[h % 2][GRID_W * half:GRID_W * (half + 1), :, :], src).then_inc(table_in[h % 2], 16)

        @block.gpsimd
        def _(pool):
            pool.wait_ge(const_in, 32)
            link = Links(pool, pool_link)
            for h in range(AH):
                b, s = table[h % 2], inner[h % 2]
                pool.wait_ge(table_in[h % 2], 32 * (h // 2 + 1))
                link.wait(pool.tensor_scalar(b[:, :, :], b[:, :, :], 1 / SCALE, None, ALU.mult))
                link.wait(pool.tensor_tensor(b[:, :, :], b[:, :, :],
                                             window[:, :].rearrange("p (a n) -> p a n", a=1).to_broadcast([P, JR, GRID_W]), ALU.add))
                pool.tensor_tensor(s[:, :, :], b[:, 2:2 + WR + 1, :],
                                   rowmask[:, :].rearrange("p (r a) -> p r a", a=1).to_broadcast([P, WR + 1, GRID_W]), ALU.add)\
                    .then_inc(table_ready, 1)
                if h == 0:
                    pool.wait_ge(scaled, 1)
                    pool.dma_start(io["mix"][0, :, 0:AW], first_rows[:, :, :].rearrange("p h d -> p (h d)")).then_inc(first_out, 16)
                elif h % 2 == 1 and h >= 3:
                    store(pool, (h - 3) // 2)
            store(pool, 3)
            pool.wait_ge(first_out, 16)
            pool.wait_ge(pair_out[0], 32)
            pool.wait_ge(pair_out[1], 32)

        @block.tensor
        def _(pe):
            ident = keep["ident"]
            for g, group in enumerate(GROUPS):
                if g < 4:
                    bank = (score[g // 2])[:, (g % 2) * BLK:(g % 2 + 1) * BLK]
                if g >= 4:
                    bank = (score[g % 4 // 2])[:, (g % 2) * BLK:(g % 2 + 1) * BLK]
                    pe.wait_ge((laid_vec, laid_act)[g % 2], g // 2 - 1)
                for m, (i, hp, t) in enumerate(group):
                    pe.wait_ge(tile_in[t], 32)
                    mm = pe.transpose(bank[:, m * P:(m + 1) * P], qk_nat[:, t, i, hp * P:(hp + 1) * P], ident[:, :])
                mm.then_inc(laid, 1)
            pe.wait_ge(laid_vec, (len(GROUPS) + 1) // 2)
            pe.wait_ge(laid_act, len(GROUPS) // 2)

            def raw_scores(n):
                h, t = units[n]
                if n >= 2:
                    pe.wait_ge(biased, n - 1)
                q = qT[AD * (h % 2):AD * (h % 2) + AD, h // 2, t, :]
                for c, k, keys in pieces(h, t):
                    mm = pe.matmul(score[n % 2][:, c:c + k], q, keys, start=True, stop=True)
                mm.then_inc(scored, 1)

            def turn_probs(n):
                h, t = units[n]
                pe.wait_ge(expd, n + 1)
                if n >= 1:
                    pe.wait_ge(taken[0], n)
                bl = blocks(h, t)
                for b, (c, k, _) in enumerate(bl):
                    if b == 4:
                        pe.wait_ge(taken[1], n)
                    mm = pe.transpose(turn[b // 4][0:k, b % 4, :], prob[n % 3][:, c:c + k], ident[:, :])
                    if b == min(3, len(bl) - 1):
                        mm.then_inc(turned[0], 1)
                if len(bl) > 4:
                    mm.then_inc(turned[1], 1)

            def values(n):
                h, t = units[n]
                bank = 0 if n < AH else (h + 1) % 2
                slot = h if n < AH else t - 1
                if n >= AH and slot == 0 and h >= 1:
                    pe.wait_ge(scaled, h)
                pe.wait_ge(taken[0], n + 1)
                pe.wait_ge(taken[1], n + 1)
                bl = blocks(h, t)
                for b, (c, k, v) in enumerate(bl):
                    mm = pe.matmul(outp[bank][:, slot, :], probT[n % 2][0:k, b, :], v, start=(b == 0), stop=(b == len(bl) - 1))
                mm.then_inc(summed, 1)

            for n in range(N + 2):
                if n < N:
                    raw_scores(n)
                if 1 <= n <= N:
                    turn_probs(n - 1)
                if n >= 2:
                    values(n - 2)

        @block.scalar
        def _(act):
            for g in range(1, len(GROUPS), 2):
                act.wait_ge(laid, g + 1)
                for m, (i, hp, t) in enumerate(GROUPS[g]):
                    op = act.activation(lay_dst(i, hp, t), score[g % 4 // 2][:, (g % 2) * BLK + m * P:(g % 2) * BLK + (m + 1) * P], ACT.Copy)
                op.then_inc(laid_act, 1)

            def exps(n):
                h, t = units[n]
                w = local_cols(t) + P
                act.wait_ge(biased, n + 1)
                p = prob[n % 3][:, 0:w]
                act.activation(p, p, ACT.Exp, scale=-1.0, bias=low[:, n, 1:2], accum_out=total[:, n:n + 1]).then_inc(expd, 1)

            def take(n):
                h, t = units[n]
                if t == 0:
                    act.wait_ge(expd, n + 1)
                    act.activation(low[0:1, n, 0:1], low[0:1, n, 1:2], ACT.Copy).then_inc(taken[1], 1)
                    return
                act.wait_ge(turned[1], n - AH + 1)
                if n >= 2:
                    act.wait_ge(summed, n - 1)
                bl = blocks(h, t)[4:]
                for b, (c, k, _) in enumerate(bl):
                    if len(bl) == 1 or k < P:
                        op = act.activation(probT[n % 2][0:k, 4 + b, :], turn[1][0:k, b, :], ACT.Copy)
                    else:
                        op = act.activation(probT[n % 2][:, 4 + b, :], turn[1][:, b, :], ACT.Copy)
                op.then_inc(taken[1], 1)

            for n in range(N + 1):
                if n < N:
                    exps(n)
                if n >= 1:
                    take(n - 1)

        @block.vector
        def _(dve):
            link = Links(dve, vec_link)
            link.wait(dve.memset(zeros[:, :], 0.0))
            for g in range(0, len(GROUPS), 2):
                dve.wait_ge(laid, g + 1)
                for m, (i, hp, t) in enumerate(GROUPS[g]):
                    op = dve.tensor_copy(lay_dst(i, hp, t), score[g % 4 // 2][:, m * P:(m + 1) * P])
                op.then_inc(laid_vec, 1)

            def bias(n):
                h, t = units[n]
                dve.wait_ge(scored, n + 1)
                if n >= 3:
                    dve.wait_ge(turned[0], n - 2)
                    if n - 3 >= AH:
                        dve.wait_ge(turned[1], n - 2 - AH)
                w = local_cols(t)
                s, p = score[n % 2], prob[n % 3]
                start = 3e38
                if t:
                    _, nr, j0, differ = WINDOWS[t - 1]
                    if t == 1:
                        dve.wait_ge(table_ready, h + 1)
                    tab = inner[h % 2][:, 0:nr, :] if differ else table[h % 2][:, j0:j0 + nr, :]
                    link.wait(dve.tensor_tensor_reduce(p[:, 0:w], s[:, 0:w], tab.rearrange("p r n -> p (r n)"), -SCALE, start,
                                                       ALU.add, ALU.min, low[:, n, 0:1]))
                    start = low[:, n, 0:1]
                dve.tensor_tensor_reduce(p[:, w:w + P], s[:, w:w + P], zeros[:, :], -SCALE, start,
                                         ALU.add, ALU.min, low[:, n, 1:2]).then_inc(biased, 1)

            def take(n):
                h, t = units[n]
                dve.wait_ge(turned[0], n + 1)
                if n >= 2:
                    dve.wait_ge(summed, n - 1)
                nb = 4 if t else 1
                dve.tensor_copy(probT[n % 2][:, 0:nb, :], turn[0][:, 0:nb, :]).then_inc(taken[0], 1)

            def scale(g):
                c = slice(8 * g, 8 * g + 8)
                link.wait(dve.reciprocal(total[:, c], total[:, c]))
                dve.wait_ge(summed, 8 * g + 8)
                h = g - 1
                dst = first_rows[:, :, :] if g == 0 else heads[h // 2 % 2][:, :, h % 2, :]
                if g and h // 2 >= 2:
                    dve.wait_ge(pair_out[h // 2 % 2], 16)
                dve.tensor_tensor(dst, outp[g % 2][:, :, :], total[:, c].rearrange("p (t a) -> p t a", a=1).to_broadcast([P, 8, AD]),
                                  ALU.mult).then_inc(scaled, 1)

            for n in range(N + 2):
                if n < N:
                    bias(n)
                if 1 <= n <= N:
                    take(n - 1)
                if n >= 9 and (n - 9) % 8 == 1:
                    scale((n - 10) // 8)
            scale(N // 8 - 1) if (N + 1 - 9) % 8 != 1 else None



GAP = 2
TW = CTX + GAP + LAT
CUTS = [(0, CTX + GAP + 2 * P), (CTX + GAP + 2 * P, 3 * P), (CTX + GAP + 5 * P, 3 * P)]


def column_of(t):
    return t * P + (GAP if t else 0)


def output_projection(nc, io, keep):
    with ExitStack() as ctx:
        def sb(name, shape):
            return ctx.enter_context(nc.sbuf_tensor(name, shape, F32))

        def ps(name, shape):
            return ctx.enter_context(nc.psum_tensor(name, shape, F32))

        def sem(name):
            return ctx.enter_context(nc.semaphore(name))

        w = sb("op_w", [P, KT, D])
        mt = [sb(f"op_mix{j}", [P, MIX]) for j in range(2)]
        xt = [sb(f"op_x{j}", [P, D]) for j in range(2)]
        mT = [sb(f"op_mixT{j}", [P, KT, P]) for j in range(2)]
        x1 = [sb(f"op_x1{j}", [P, D]) for j in range(2)]
        xn = [sb(f"op_xn{j}", [P, D]) for j in range(2)]
        junk = sb("op_junk", [P, D])
        stat = sb("op_stat", [P, NT, 2])
        half = sb("op_half", [P, 1])
        tp = [ps(f"op_tp{j}", [P, 4, P]) for j in range(4)]
        acc = [ps(f"op_acc{j}", [P, BLK]) for j in range(4)]
        w_in = sem("op_w_in")
        half_set = sem("op_half_set")
        t_in = [sem(f"op_t_in{j}") for j in range(2)]
        turned = sem("op_turned")
        turned_read = sem("op_turned_read")
        acc_done = sem("op_acc_done")
        gated = sem("op_gated")
        x1_done = sem("op_x1_done")
        squares = sem("op_squares")
        mean_sq = sem("op_mean_sq")
        rstd = sem("op_rstd")
        xn_done = sem("op_xn_done")
        xn_turned = sem("op_xn_turned")
        xn_read = sem("op_xn_read")
        x1_out = [sem(f"op_x1_out{j}") for j in range(2)]
        block = ctx.enter_context(nc.Block())

        @block.sync
        def _(sp):
            for t in range(NT):
                if t >= 2:
                    sp.wait_ge(x1_done, t - 1)
                    sp.wait_ge(turned, 2 * t - 2)
                sp.dma_start(mt[t % 2][:, :], io["mix"][t]).then_inc(t_in[t % 2], 16)
                sp.dma_start(xt[t % 2][:, :], io["x"][t]).then_inc(t_in[t % 2], 16)
                if t == 0:
                    sp.dma_start(w[:, :, :], io["w_out"]).then_inc(w_in, 16)

        @block.gpsimd
        def _(pool):
            pool.memset(half[:, :], -0.5).then_inc(half_set, 1)
            pool.wait_ge(half_set, 1)
            for t in range(NT):
                pool.wait_ge(x1_done, t + 1)
                pool.dma_start(io["x1"][t], x1[t % 2][:, :]).then_inc(x1_out[t % 2], 16)
                pool.wait_ge(mean_sq, t + 1)
                pool.tensor_tensor(stat[:, t, 1:2], stat[:, t, 1:2], half[:, :], ALU.pow).then_inc(rstd, 1)
            pool.wait_ge(x1_out[0], 16 * ((NT + 1) // 2))
            pool.wait_ge(x1_out[1], 16 * (NT // 2))

        @block.tensor
        def _(pe):
            def turn(t):
                pe.wait_ge(t_in[t % 2], 32 * (t // 2 + 1))
                for g in range(2):
                    if t:
                        pe.wait_ge(turned_read, 2 * (t - 1) + g + 1)
                    for k in range(4):
                        mm = pe.transpose(tp[g][:, k, :], mt[t % 2][:, (4 * g + k) * P:(4 * g + k + 1) * P], keep["ident"][:, :])
                    mm.then_inc(turned, 1)

            def turn_xn(t):
                pe.wait_ge(xn_done, t + 1)
                for g in range(2):
                    if t:
                        pe.wait_ge(xn_read, 2 * (t - 1) + g + 1)
                    for k in range(4):
                        mm = pe.transpose(tp[2 + g][:, k, :], xn[t % 2][:, (4 * g + k) * P:(4 * g + k + 1) * P], keep["ident"][:, :])
                    mm.then_inc(xn_turned, 1)

            turn(0)
            pe.wait_ge(w_in, 16)
            for t in range(NT):
                if t + 1 < NT:
                    turn(t + 1)
                pe.wait_ge(turned_read, 2 * t + 2)
                for b in range(2):
                    n = 2 * t + b
                    if n >= 4:
                        pe.wait_ge(gated, n - 3)
                    for k in range(KT):
                        mm = pe.matmul(acc[n % 4][:, :], mT[t % 2][:, k, :], w[:, k, b * BLK:(b + 1) * BLK], start=(k == 0), stop=(k == KT - 1))
                    mm.then_inc(acc_done, 1)
                if t:
                    turn_xn(t - 1)
            turn_xn(NT - 1)

        @block.scalar
        def _(act):
            def square(t):
                act.wait_ge(x1_done, t + 1)
                act.activation(junk[:, :], x1[t % 2][:, :], ACT.Square, accum_out=stat[:, t, 0:1]).then_inc(squares, 1)

            for t in range(NT):
                for g in range(2):
                    act.wait_ge(turned, 2 * t + g + 1)
                    if t >= 2:
                        act.wait_ge(acc_done, 2 * t - 2)
                    act.activation(mT[t % 2][:, 4 * g:4 * g + 4, :], tp[g][:, :, :], ACT.Copy).then_inc(turned_read, 1)
                if t:
                    square(t - 1)
            square(NT - 1)

        @block.vector
        def _(dve):
            h2T = keep["h2T"]
            dve.memset(h2T[:, :, CTX:CTX + GAP], 0.0)

            def modulate(t):
                v = 1 if t else 0
                for k in range(KT):
                    if k % 4 == 0:
                        dve.wait_ge(xn_turned, 2 * t + k // 4 + 1)
                    op = dve.tensor_scalar(h2T[:, k, column_of(t):column_of(t) + P], tp[2 + k // 4][:, k % 4, :],
                                           keep["gain"][:, 1, k, v:v + 1], keep["mod"][:, 3 * KT + k, v:v + 1], ALU.mult, ALU.add)
                    if k % 4 == 3:
                        op.then_inc(xn_read, 1)

            for t in range(NT):
                j, v = t % 2, 1 if t else 0
                dve.wait_ge(t_in[j], 32 * (t // 2 + 1))
                if t >= 2:
                    dve.wait_ge(x1_out[j], 16 * (t // 2))
                    dve.wait_ge(squares, t - 1)
                for b in range(2):
                    n, at = 2 * t + b, slice(b * BLK, (b + 1) * BLK)
                    dve.wait_ge(acc_done, n + 1)
                    dve.tensor_tensor(x1[j][:, at], acc[n % 4][:, :], keep["g1"][:, v, at], ALU.mult).then_inc(gated, 1)
                dve.wait_ge(gated, 2 * t + 2)
                dve.tensor_tensor(x1[j][:, :], x1[j][:, :], xt[j][:, :], ALU.add).then_inc(x1_done, 1)
                if t:
                    modulate(t - 1)
                dve.wait_ge(squares, t + 1)
                dve.tensor_scalar(stat[:, t, 1:2], stat[:, t, 0:1], 1.0 / D, EPS, ALU.mult, ALU.add).then_inc(mean_sq, 1)
                dve.wait_ge(rstd, t + 1)
                if t >= 2:
                    dve.wait_ge(xn_turned, 2 * t - 2)
                dve.tensor_scalar(xn[j][:, :], x1[j][:, :], stat[:, t, 1:2], None, ALU.mult).then_inc(xn_done, 1)
            modulate(NT - 1)


def mlp_up(nc, io, keep):
    with ExitStack() as ctx:
        def sb(name, shape):
            return ctx.enter_context(nc.sbuf_tensor(name, shape, F32))

        def ps(name, shape):
            return ctx.enter_context(nc.psum_tensor(name, shape, F32))

        def sem(name):
            return ctx.enter_context(nc.semaphore(name))

        w = [sb(f"up_w{j}", [P, KT, 2, P]) for j in range(2)]
        cw = sb("up_convw", [P, FT, 2, 3])
        cb = sb("up_convb", [P, FT, 2])
        u = [sb(f"up_u{j}", [P, TW + 2]) for j in range(2)]
        conv = [sb(f"up_conv{j}", [P, TW]) for j in range(2)]
        acc = [[ps(f"up_acc{i}_{c}", [P, BLK]) for c in range(3)] for i in range(2)]
        const_in = sem("up_const_in")
        w_in = [sem(f"up_w_in{j}") for j in range(2)]
        acc_done = sem("up_acc_done")
        acc_read = sem("up_acc_read")
        conv_done = sem("up_conv_done")
        silu_done = sem("up_silu_done")
        g_done = sem("up_g_done")
        edges = sem("up_edges")
        vec_link = sem("up_vec_link")
        block = ctx.enter_context(nc.Block())
        h2T, gT = keep["h2T"], keep["gT"]

        @block.sync
        def _(sp):
            def load(f, j):
                sp.dma_start(w[j][:, :, :, :], io["w_up"][bass.ds(f, 1)].rearrange("a p k b n -> (a p) k b n")).then_inc(w_in[j], 16)

            load(0, 0)
            load(1, 1)
            sp.dma_start(cw[:, :, :, :], io["convw"]).then_inc(const_in, 16)
            sp.dma_start(cb[:, :, :], io["convb"]).then_inc(const_in, 16)
            with sp.Fori(1, FT // 2) as v:
                for j in range(2):
                    f = v * 2 + j
                    sp.wait_ge(acc_done, 6 * f - 6)
                    load(f, j)

        @block.tensor
        def _(pe):
            def tile(f, j, warm):
                pe.wait_ge(w_in[j], f * 8 + 16 - 8 * j)
                for i in range(2):
                    for c, (c0, cn) in enumerate(CUTS):
                        if warm:
                            pe.wait_ge(acc_read, 6 * f - 6 + 3 * i + c + 1)
                        for k in range(KT):
                            mm = pe.matmul(acc[i][c][:, 0:cn], w[j][:, k, i, :], h2T[:, k, c0:c0 + cn], start=(k == 0), stop=(k == KT - 1))
                        mm.then_inc(acc_done, 1)

            tile(0, 0, False)
            tile(1, 1, True)
            with pe.Fori(1, FT // 2) as v:
                for j in range(2):
                    tile(v * 2 + j, j, True)

        @block.scalar
        def _(act):
            act.wait_ge(edges, 1)

            def tile(f, warm):
                for i in range(2):
                    for c, (c0, cn) in enumerate(CUTS):
                        act.wait_ge(acc_done, 6 * f + 3 * i + c + 1)
                        if warm and c == 0:
                            act.wait_ge(conv_done, 2 * f - 1 + i)
                        act.activation(u[i][:, 1 + c0:1 + c0 + cn], acc[i][c][:, 0:cn], ACT.Copy).then_inc(acc_read, 1)
                act.wait_ge(conv_done, 2 * f + 1)
                act.activation(conv[0][:, :], conv[0][:, :], ACT.Silu).then_inc(silu_done, 1)

            tile(0, False)
            with act.Fori(1, FT) as f:
                tile(f, True)

        @block.vector
        def _(dve):
            for i in range(2):
                dve.memset(u[i][:, 0:1], 0.0)
                op = dve.memset(u[i][:, TW + 1:TW + 2], 0.0)
            op.then_inc(edges, 1)
            dve.wait_ge(const_in, 32)
            link = Links(dve, vec_link)
            PER = 4

            def tile(f, warm):
                link.start(PER * f)
                for i in range(2):
                    dve.wait_ge(acc_read, 6 * f + 3 * i + 3)
                    if warm:
                        dve.wait_ge(g_done, f)
                    at = bass.ds(f, 1)

                    def tap(n):
                        return cw[:, at, i, n:n + 1].rearrange("p a n -> p (a n)")

                    link.wait(dve.tensor_scalar(conv[i][:, :], u[i][:, 1:TW + 1], tap(1), cb[:, at, i], ALU.mult, ALU.add))
                    link.wait(dve.scalar_tensor_tensor(out=conv[i][:, :], in0=u[i][:, 0:TW], scalar=tap(0), in1=conv[i][:, :],
                                                       op0=ALU.mult, op1=ALU.add))
                    dve.scalar_tensor_tensor(out=conv[i][:, :], in0=u[i][:, 2:TW + 2], scalar=tap(2), in1=conv[i][:, :],
                                             op0=ALU.mult, op1=ALU.add).then_inc(conv_done, 1)
                assert link.k == PER
                dve.wait_ge(silu_done, f + 1)
                dve.wait_ge(conv_done, 2 * f + 2)
                dve.tensor_tensor(gT[:, bass.ds(f, 1), :].rearrange("p a n -> p (a n)"), conv[0][:, :], conv[1][:, :], ALU.mult)\
                   .then_inc(g_done, 1)

            tile(0, False)
            with dve.Fori(1, FT) as f:
                tile(f, True)


def mlp_down(nc, io, keep):
    with ExitStack() as ctx:
        def sb(name, shape):
            return ctx.enter_context(nc.sbuf_tensor(name, shape, F32))

        def ps(name, shape):
            return ctx.enter_context(nc.psum_tensor(name, shape, F32))

        def sem(name):
            return ctx.enter_context(nc.semaphore(name))

        w = [sb(f"dn_w{j}", [P, FT, P]) for j in range(2)]
        yT = [sb(f"dn_yT{j}", [P, TW]) for j in range(2)]
        x1 = [sb(f"dn_x1{j}", [P, NT, P]) for j in range(2)]
        acc = [ps(f"dn_acc{c}", [P, BLK]) for c in range(3)]
        tp = [ps(f"dn_tp{g}", [P, 4, P]) for g in range(3)]
        w_in = [sem(f"dn_w_in{j}") for j in range(2)]
        x_in = [sem(f"dn_x_in{j}") for j in range(2)]
        acc_done = sem("dn_acc_done")
        gated = sem("dn_gated")
        turned = sem("dn_turned")
        added = sem("dn_added")
        y_out = [sem(f"dn_y_out{j}") for j in range(2)]
        block = ctx.enter_context(nc.Block())
        gT = keep["gT"]
        TG = [(0, 4), (4, 4), (8, 1)]

        def slab(rows, n):
            return rows[:, bass.ds(n, 1)].rearrange("t a p d -> (a p) t d")

        @block.sync
        def _(sp):
            def load(n, j):
                sp.dma_start(w[j][:, :, :], io["w_down"][bass.ds(n, 1)].rearrange("a p f n -> (a p) f n")).then_inc(w_in[j], 16)
                sp.dma_start(x1[j][:, :, :], io["x1"][:, :, bass.ds(n * P, P)].rearrange("t p d -> p t d")).then_inc(x_in[j], 16)

            def store(n, j):
                sp.wait_ge(added, 3 * n + 3)
                sp.dma_start(io["y"][:, :, bass.ds(n * P, P)].rearrange("t p d -> p t d"), x1[j][:, :, :]).then_inc(y_out[j], 16)

            load(0, 0)
            load(1, 1)
            with sp.Fori(1, KT // 2) as v:
                for j in range(2):
                    n = v * 2 + j
                    store(n - 2, j)
                    sp.wait_ge(y_out[j], 8 * (n - j))
                    load(n, j)
            for j in range(2):
                store(KT - 2 + j, j)
            for j in range(2):
                sp.wait_ge(y_out[j], 8 * KT)

        @block.tensor
        def _(pe):
            def multiply(n, j, warm):
                pe.wait_ge(w_in[j], n * 8 + 16 - 8 * j)
                for c, (c0, cn) in enumerate(CUTS):
                    if warm:
                        pe.wait_ge(gated, 3 * n - 2 + c)
                    for f in range(FT):
                        mm = pe.matmul(acc[c][:, 0:cn], w[j][:, f, :], gT[:, f, c0:c0 + cn], start=(f == 0), stop=(f == FT - 1))
                    mm.then_inc(acc_done, 1)

            def turn(n, j, warm):
                pe.wait_ge(gated, 3 * n + 3)
                for g, (t0, nt) in enumerate(TG):
                    if warm:
                        pe.wait_ge(added, 3 * n - 2 + g)
                    for t in range(t0, t0 + nt):
                        mm = pe.transpose(tp[g][:, t - t0, :], yT[j][:, column_of(t):column_of(t) + P], keep["ident"][:, :])
                    mm.then_inc(turned, 1)

            multiply(0, 0, False)
            multiply(1, 1, True)
            turn(0, 0, False)
            with pe.Fori(1, KT // 2) as v:
                for j in range(2):
                    n = v * 2 + j
                    multiply(n, j, True)
                    turn(n - 1, 1 - j, True)
            turn(KT - 1, 1, True)

        @block.vector
        def _(dve):
            def gate(n, j, warm):
                for c, (c0, cn) in enumerate(CUTS):
                    dve.wait_ge(acc_done, 3 * n + c + 1)
                    if warm and c == 0:
                        dve.wait_ge(turned, 3 * n - 3)
                    if c == 0:
                        dve.tensor_scalar(yT[j][:, 0:CTX], acc[0][:, 0:CTX], g2(n, 0), None, ALU.mult)
                        a = CTX + GAP
                    else:
                        a = c0
                    dve.tensor_scalar(yT[j][:, a:c0 + cn], acc[c][:, a - c0:cn], g2(n, 1), None, ALU.mult).then_inc(gated, 1)

            def g2(n, v):
                return keep["mod"][:, bass.ds(n + 5 * KT, 1), v]

            def add(n, j):
                for g, (t0, nt) in enumerate(TG):
                    dve.wait_ge(turned, 3 * n + g + 1)
                    if g == 0:
                        dve.wait_ge(x_in[j], n * 8 + 16 - 8 * j)
                    dve.tensor_tensor(x1[j][:, t0:t0 + nt, :], x1[j][:, t0:t0 + nt, :], tp[g][:, 0:nt, :], ALU.add).then_inc(added, 1)

            gate(0, 0, False)
            gate(1, 1, False)
            add(0, 0)
            with dve.Fori(1, KT // 2) as v:
                for j in range(2):
                    n = v * 2 + j
                    gate(n, j, True)
                    add(n - 1, 1 - j)
            add(KT - 1, 1)



def shape_constants():
    import numpy as np
    f = np.float32
    tri = np.tril(np.ones((P, P), bool))
    pos = np.arange(LAT)
    quarter = MD // 4
    freq = (10000.0 ** (-np.arange(quarter, dtype=f) / f(quarter))).astype(f)
    cos = np.ones((P, NT, 2, 2, quarter), f)
    sin = np.zeros((P, NT, 2, 2, quarter), f)
    for g, p in enumerate((pos // GRID_W, pos % GRID_W)):
        ang = (p.astype(f)[:, None] * freq[None, :]).reshape(NT - 1, P, quarter).transpose(1, 0, 2)
        for a in range(2):
            cos[:, 1:, g, a] = np.cos(ang)
            sin[:, 1:, g, a] = np.sin(ang) * (1 if a else -1)
    sel = np.zeros((2, 2, P), f)
    sel[0, 0] = sel[1, 1] = 1
    col = np.arange(GRID_W)
    cs = np.clip(col - 8, 0, GRID_W - 16)
    inside = (col[None, :] >= cs[:, None]) & (col[None, :] < cs[:, None] + 16)
    window = np.tile(np.where(inside, f(0), f(NEG)), (2, 1))
    rowmask = np.zeros((P, 9), f)
    rowmask[:GRID_W, 8] = NEG
    rowmask[GRID_W:, 0] = NEG
    return {"ident": np.eye(P, dtype=f), "flip": np.eye(P, dtype=f)[::-1].copy(),
            "cos": cos.reshape(P, NT, MD), "sin": sin.reshape(P, NT, MD), "sel": sel,
            "causal": np.stack([np.where(tri.T, f(0), f(NEG)), np.where(tri, f(0), f(NEG))], axis=1),
            "window": window, "rowmask": rowmask}


def lay_out(inp):
    import numpy as np
    a = {k: np.asarray(v) for k, v in inp.items()}
    w_in = a["w_in"][0].reshape(KT, P, -1).transpose(1, 0, 2)
    rep = lambda v: np.broadcast_to(v, (P,) + v.shape)
    toe = np.zeros((AH, 15, 127), np.float32)
    toe[:, :, 48:79] = a["rpb"][0]
    out = dict(shape_constants())
    out.update({
        "x": np.concatenate([a["x_prompt"][0], a["x_sample"][0]]).reshape(NT, P, D),
        "cT": np.stack([a["c_ctx"], a["c"][0]], -1).reshape(KT, P, 2).transpose(1, 0, 2),
        "w_mod": a["w_mod"][0].reshape(KT, P, MOD // BLK, BLK).transpose(2, 1, 0, 3),
        "b_mod2": np.broadcast_to(a["b_mod"], (2, MOD)),
        "gains": np.stack([a["norm1_g"][0].reshape(KT, P).T, a["norm2_g"][0].reshape(KT, P).T], 1),
        "w_in": w_in[:, :, :7 * BLK].reshape(P, KT, 7, BLK).transpose(2, 0, 1, 3),
        "w_gate": w_in[:, :, 7 * BLK:],
        "bg": rep(a["b_gate"][0]),
        "qkg": rep(np.stack([a["q_norm_g"][0], a["k_norm_g"][0]])),
        "ck": a["cache_k"][0, 0].reshape(P, AW), "cv": a["cache_v"][0, 0].reshape(P, AW),
        "toeplitz": toe.reshape(AH, 15 * 127),
        "stC": np.concatenate([a["state_C"][0, 0], a["state_n"][0, 0][..., None]], -1),
        "stm": a["state_m"][0, 0].reshape(1, 2 * MH),
        "mlg": rep(a["ml_norm_g"][0]),
        "w_out": a["w_out"][0].reshape(KT, P, D).transpose(1, 0, 2),
        "w_up": a["w_up"][0].reshape(KT, P, 2, FT, P).transpose(3, 1, 0, 2, 4),
        "convw": a["conv_w"][0].reshape(3, 2, FT, P).transpose(3, 2, 1, 0),
        "convb": a["conv_b"][0].reshape(2, FT, P).transpose(2, 1, 0),
        "w_down": a["w_down"][0].reshape(FT, P, KT, P).transpose(2, 1, 0, 3),
    })
    return out



_OUTS = {"y": (NT, P, D), "new_k": (P, AW), "new_v": (P, AW), "new_st": (2, MH, MD, MD + 1), "new_m": (2, MH)}
_SCRATCH = {"proj": (NT, P, 7 * BLK), "mix": (NT, P, MIX), "x1": (NT, P, D), "mrows": (2, 2, 16, MH, P),
            "bias_rows": (AH, GRID_W, 15 * 127)}


def program(nc, io):
    with ExitStack() as ctx:
        def keeping(name, shape):
            keep[name] = ctx.enter_context(nc.sbuf_tensor("keep_" + name, shape, F32))

        keep = {}
        keeping("ident", [P, P])
        keeping("mod", [P, MOD // P, 2])
        keeping("gain", [P, 2, KT, 2])
        keeping("g1", [P, 2, D])
        keeping("gates", [P, NT, NG])
        modulation(nc, io, keep)
        projection(nc, io, keep)
        mlstm(nc, io, keep)
        attention(nc, io, keep)
        keeping("h2T", [P, KT, TW])
        output_projection(nc, io, keep)
        keeping("gT", [P, FT, TW])
        mlp_up(nc, io, keep)
        mlp_down(nc, io, keep)


def kernel(**inputs):
    import numpy as _np
    import concourse.bacc as _bacc
    from concourse import mybir as _mybir
    from concourse.bass_utils import run_bass_kernel_spmd as _run

    nc = _bacc.Bacc("TRN2", target_bir_lowering=False, num_devices=1)
    arrays, io = {}, {}
    for name, a in lay_out(inputs).items():
        a = _np.ascontiguousarray(a)
        arrays[f"in_{name}"] = a
        io[name] = nc.dram_tensor(f"in_{name}", a.shape, _mybir.dt.from_np(a.dtype), kind="ExternalInput").ap()
    for name, shape in _OUTS.items():
        io[name] = nc.dram_tensor(f"out_{name}", shape, _mybir.dt.float32, kind="ExternalOutput").ap()
    for name, shape in _SCRATCH.items():
        io[name] = nc.dram_tensor(f"scratch_{name}", shape, _mybir.dt.float32, kind="Internal").ap()
    program(nc, io)
    got = _run(nc, [arrays], core_ids=[0]).results[0]
    y = got["out_y"].reshape(CTX + LAT, D)
    st = got["out_new_st"]
    return (y[None, :CTX], y[None, CTX:], got["out_new_k"].reshape(1, 1, CTX, AH, AD), got["out_new_v"].reshape(1, 1, CTX, AH, AD),
            st[None, None, ..., :MD], st[None, None, ..., MD], got["out_new_m"].reshape(1, 1, 2, MH))
```

```python
from contextlib import ExitStack

import concourse.bass as bass
from concourse import mybir

F32 = mybir.dt.float32
F32R = mybir.dt.float32r
ALU = mybir.AluOpType
ACT = mybir.ActivationFunctionType
AX = mybir.AxisListType

P = 128
D = 1024
KT = D // P
CTX = 128
LAT = 1024
NT = (CTX + LAT) // P
GRID_W = 64
AH, AD = 8, 64
AW = AH * AD
MH, MD = 4, 128
MW = MH * MD
NG = 4 * MH
MIX = AW + MW
PW = 3 * AW + 4 * MW
FF = 2816
FT = FF // P
EPS = 1e-6
NEG = -1e30
BLK = 512
AQ, AK, AV, MQ, MK, MV, MO = range(7)
MOD = 6 * D


class Links:

    def __init__(self, eng, sem):
        self.eng, self.sem, self.base, self.k = eng, sem, 0, 0

    def start(self, base):
        self.base, self.k = base, 0

    def tick(self, ins):
        ins.then_inc(self.sem, 1)
        self.k += 1
        return self.base + self.k

    def wait(self, ins):
        self.eng.wait_ge(self.sem, self.tick(ins))


def tile_rows(rows, t):
    return rows[bass.ds(t, 1)].rearrange("a p n -> (a p) n")


def modulation(nc, io, keep):
    NB = MOD // BLK
    GATES = [(r, v, h) for r in (5, 2) for v in range(2) for h in range(2)]
    with ExitStack() as ctx:
        def sb(name, shape):
            return ctx.enter_context(nc.sbuf_tensor(name, shape, F32))

        def ps(name, shape):
            return ctx.enter_context(nc.psum_tensor(name, shape, F32))

        def sem(name):
            return ctx.enter_context(nc.semaphore(name))

        ring = [sb(f"mod_w{j}", [P, KT, BLK]) for j in range(4)]
        cvec = sb("mod_c", [P, KT, 2])
        cexp = sb("mod_cexp", [P, KT, 2])
        csilu = sb("mod_csilu", [P, KT, 2])
        brow = sb("mod_bias", [2, MOD])
        row = sb("mod_row", [2, MOD])
        sel = sb("mod_sel", [2, 2, P])
        gains = sb("mod_gains", [P, 2, KT])
        gate2 = sb("mod_gate2", [P, 2, D])
        acc = [ps(f"mod_acc{j}", [P, BLK]) for j in range(4)]
        cols = ps("mod_cols", [P, BLK])
        gate = [ps(f"mod_gate{j}", [P, BLK]) for j in range(2)]
        small_in = sem("mod_small_in")
        w_in = [sem(f"mod_w_in{j}") for j in range(4)]
        c_exp = sem("mod_c_exp")
        c_silu = sem("mod_c_silu")
        acc_done = sem("mod_acc_done")
        row_done = sem("mod_row_done")
        cols_done = sem("mod_cols_done")
        gate_done = sem("mod_gate_done")
        gate_read = sem("mod_gate_read")
        gate_out = sem("mod_gate_out")
        vec_link = sem("mod_vec_link")
        block = ctx.enter_context(nc.Block())

        @block.sync
        def _(sp):
            sp.dma_start(cvec[:, :, :], io["cT"]).then_inc(small_in, 16)
            sp.dma_start(keep["ident"][:, :], io["ident"]).then_inc(small_in, 16)
            sp.dma_start(brow[:, :], io["b_mod2"]).then_inc(small_in, 16)
            sp.dma_start(sel[:, :, :], io["sel"]).then_inc(small_in, 16)
            sp.dma_start(gains[:, :, :], io["gains"]).then_inc(small_in, 16)

            def load(n, j):
                sp.dma_start(ring[j][:, :, :], io["w_mod"][n]).then_inc(w_in[j], 16)

            for j in range(4):
                load(j, j)
            with sp.Fori(1, NB // 4) as u:
                for j in range(4):
                    n = u * 4
                    sp.wait_ge(acc_done, n + j - 3)
                    load(n + j, j)
            sp.wait_ge(gate_read, 4)
            sp.dma_start(io["gate2"], gate2[:, :, :]).then_inc(gate_out, 16)
            sp.wait_ge(gate_out, 16)

        @block.scalar
        def _(act):
            act.wait_ge(small_in, 80)
            act.activation(cexp[:, :, :], cvec[:, :, :], ACT.Exp, scale=-1.0).then_inc(c_exp, 1)

        @block.tensor
        def _(pe):
            pe.wait_ge(c_silu, 1)
            pe.wait_ge(small_in, 80)

            def mul(n, j, first):
                pe.wait_ge(w_in[j], n * 4 + 16 - 4 * j)
                if not first:
                    pe.wait_ge(row_done, n - 3)
                for k in range(KT):
                    mm = pe.matmul(acc[j][0:2, :], csilu[:, k, :], ring[j][:, k, :], start=(k == 0), stop=(k == KT - 1))
                mm.then_inc(acc_done, 1)

            for j in range(4):
                mul(j, j, True)
            with pe.Fori(1, NB // 4) as u:
                for j in range(4):
                    mul(u * 4 + j, j, False)
            pe.wait_ge(row_done, NB)
            for j in range(MOD // P):
                mm = pe.transpose(cols[:, 2 * j:2 * j + 2], row[:, j * P:(j + 1) * P], keep["ident"][0:2, 0:2])
            mm.then_inc(cols_done, 1)
            for i, (r, v, h) in enumerate(GATES):
                if i >= 2:
                    pe.wait_ge(gate_read, i - 1)
                pe.matmul(gate[h][:, :], sel[:, v, :], row[:, r * D + h * BLK:r * D + (h + 1) * BLK],
                          start=True, stop=True).then_inc(gate_done, 1)

        @block.vector
        def _(dve):
            link = Links(dve, vec_link)
            dve.wait_ge(c_exp, 1)
            link.wait(dve.tensor_scalar(cexp[:, :, :], cexp[:, :, :], 1.0, None, ALU.add))
            link.wait(dve.reciprocal(cexp[:, :, :], cexp[:, :, :]))
            dve.tensor_tensor(csilu[:, :, :], cvec[:, :, :], cexp[:, :, :], ALU.mult).then_inc(c_silu, 1)

            def add_bias(n, j):
                dve.wait_ge(acc_done, n + 1)
                at = bass.ds(n * BLK, BLK)
                dve.tensor_tensor(row[:, at], acc[j][0:2, :], brow[:, at], ALU.add).then_inc(row_done, 1)

            with dve.Fori(0, NB // 4) as u:
                for j in range(4):
                    add_bias(u * 4 + j, j)
            dve.wait_ge(cols_done, 1)
            link.wait(dve.tensor_copy(keep["mod"][:, :, :], cols[:, 0:2 * (MOD // P)].rearrange("p (j v) -> p j v", v=2)))
            for norm in range(2):
                sc = keep["mod"][:, (3 * norm + 1) * KT:(3 * norm + 2) * KT, :]
                link.wait(dve.tensor_scalar(keep["gain"][:, norm, :, :], sc, 1.0, None, ALU.add))
                for v in range(2):
                    dve.tensor_tensor(keep["gain"][:, norm, :, v], keep["gain"][:, norm, :, v], gains[:, norm, :], ALU.mult)
            for i, (r, v, h) in enumerate(GATES):
                dve.wait_ge(gate_done, i + 1)
                to = gate2 if r == 5 else keep["gate"]
                dve.tensor_copy(to[:, v, h * BLK:(h + 1) * BLK], gate[h][:, :]).then_inc(gate_read, 1)


def projection(nc, io, keep):
    with ExitStack() as ctx:
        def sb(name, shape):
            return ctx.enter_context(nc.sbuf_tensor(name, shape, F32))

        def ps(name, shape):
            return ctx.enter_context(nc.psum_tensor(name, shape, F32))

        def sem(name):
            return ctx.enter_context(nc.semaphore(name))

        w = sb("pj_w", [P, 7, KT, BLK])
        wg = sb("pj_wg", [P, KT, NG])
        xt = [sb(f"pj_x{j}", [P, D]) for j in range(2)]
        xn = sb("pj_xn", [P, D])
        junk = sb("pj_junk", [P, D])
        stat = sb("pj_stat", [P, 2])
        hT = [sb(f"pj_hT{j}", [P, KT, P]) for j in range(2)]
        out = [sb(f"pj_out{j}", [P, 7, BLK]) for j in range(2)]
        raw = sb("pj_raw", [P, 2, BLK])
        tmp = sb("pj_tmp", [P, 2, BLK])
        hs = sb("pj_hs", [P, 2, AH])
        half = sb("pj_half", [P, AH])
        qkg = sb("pj_qkg", [P, 2, AD])
        bg = sb("pj_bg", [P, NG])
        cos = sb("pj_cos", [P, NT, P])
        sin = sb("pj_sin", [P, NT, P])
        acc = [ps(f"pj_acc{j}", [P, BLK]) for j in range(4)]
        tp = [ps(f"pj_tp{j}", [P, BLK]) for j in range(2)]
        small_in = sem("pj_small_in")
        w_in = [sem(f"pj_w_in{j}") for j in range(4)]
        x_in = [sem(f"pj_x_in{j}") for j in range(2)]
        squares = sem("pj_squares")
        mean_sq = sem("pj_mean_sq")
        rstd = sem("pj_rstd")
        xn_done = sem("pj_xn_done")
        tp_done = sem("pj_tp_done")
        tp_read = sem("pj_tp_read")
        acc_done = sem("pj_acc_done")
        acc_read = sem("pj_acc_read")
        head_sq = sem("pj_head_sq")
        head_rstd = sem("pj_head_rstd")
        vec_out = sem("pj_vec_out")
        rows_out = [sem(f"pj_rows_out{j}") for j in range(2)]
        cache_out = sem("pj_cache_out")
        spread = sem("pj_spread")
        gates_read = sem("pj_gates_read")
        raw_read = sem("pj_raw_read")
        pool_link = sem("pj_pool_link")
        vec_link = sem("pj_vec_link")
        block = ctx.enter_context(nc.Block())

        def done(t, n):
            return t * 8 + n + 1

        def evicted(t, n):
            return t * 7 + n + 1

        @block.sync
        def _(sp):
            def load_x(t, j):
                sp.dma_start(xt[j][:, :], tile_rows(io["x"], t)).then_inc(x_in[j], 16)

            load_x(0, 0)
            sp.dma_start(qkg[:, :, :], io["qkg"]).then_inc(small_in, 16)
            sp.dma_start(bg[:, :], io["bg"]).then_inc(small_in, 16)
            sp.dma_start(cos[:, :, :], io["cos"]).then_inc(small_in, 16)
            sp.dma_start(sin[:, :, :], io["sin"]).then_inc(small_in, 16)
            load_x(1, 1)
            for n in range(7):
                sp.dma_start(w[:, n, :, :], io["w_in"][n]).then_inc(w_in[(n + 1) // 2], 16)
            sp.dma_start(wg[:, :, :], io["w_gate"]).then_inc(w_in[3], 16)
            for t in range(2, NT):
                sp.wait_ge(xn_done, t - 1)
                load_x(t, t % 2)
            for h in range(AH):
                sp.dma_start(io["bias_rows"][h], io["toeplitz"][h:h + 1, :].to_broadcast([GRID_W, 15 * 127])).then_inc(spread, 16)
            sp.wait_ge(spread, 16 * AH)

        @block.gpsimd
        def _(pool):
            pool.memset(half[:, :], -0.5).then_inc(pool_link, 1)
            pool.wait_ge(pool_link, 1)
            pool.wait_ge(small_in, 64)

            def norm(t):
                pool.wait_ge(mean_sq, t + 1)
                pool.tensor_tensor(stat[:, 1:2], stat[:, 1:2], half[:, 0:1], ALU.pow).then_inc(rstd, 1)

            def heads(t, j, n):
                pool.wait_ge(head_sq, 2 * t + n + 1)
                pool.tensor_tensor(hs[:, n, :], hs[:, n, :], half[:, :], ALU.pow).then_inc(head_rstd, 1)

            def store(t, j):
                pool.wait_ge(vec_out, t + 1)
                pool.wait_ge(acc_read, evicted(t, MO))
                pool.dma_start(tile_rows(io["proj"], t), out[j][:, :, :].rearrange("p b n -> p (b n)")).then_inc(rows_out[j], 16)

            def tile(t, j, more):
                heads(t, j, AQ)
                heads(t, j, AK)
                if more:
                    norm(t + 1)
                store(t, j)

            norm(0)
            tile(0, 0, True)
            pool.dma_start(io["new_k"], out[0][:, AK, :]).then_inc(cache_out, 16)
            pool.dma_start(io["new_v"], out[0][:, AV, :]).then_inc(cache_out, 16)
            with pool.Fori(0, (NT - 3) // 2) as u:
                t = u * 2 + 1
                tile(t, 1, True)
                tile(t + 1, 0, True)
            tile(NT - 2, 1, True)
            tile(NT - 1, 0, False)
            pool.wait_ge(rows_out[0], 16 * ((NT + 1) // 2))
            pool.wait_ge(rows_out[1], 16 * (NT // 2))
            pool.wait_ge(cache_out, 32)

        @block.scalar
        def _(act):
            def square(t, j):
                act.wait_ge(x_in[j], 8 * t + 16 - 8 * j)
                if not isinstance(t, int) or t > 0:
                    act.wait_ge(xn_done, t)
                act.activation(junk[:, :], xt[j][:, :], ACT.Square, accum_out=stat[:, 0:1]).then_inc(squares, 1)

            def evict(t, j, n, warm):
                act.wait_ge(acc_done, done(t, n))
                src = acc[n % 4][:, :]
                if n in (MQ, MK):
                    if warm:
                        act.wait_ge(raw_read, t)
                    act.activation(raw[:, n - MQ, :], src, ACT.Copy, scale=1.0 if n == MQ else MD ** -0.5)\
                       .then_inc(acc_read, 1)
                elif n == MO:
                    act.activation(out[j][:, n, :], src, ACT.Exp, scale=-1.0).then_inc(acc_read, 1)
                else:
                    act.activation(out[j][:, n, :], src, ACT.Copy).then_inc(acc_read, 1)

            def tile(t, j, more, warm, full):
                if full:
                    act.wait_ge(rows_out[j], 8 * (t - j))
                for n in range(7):
                    evict(t, j, n, warm)
                    if n == 3 and more:
                        square(t + 1, 1 - j)

            square(0, 0)
            tile(0, 0, True, False, False)
            tile(1, 1, True, True, False)
            act.wait_ge(cache_out, 32)
            with act.Fori(1, (NT - 1) // 2) as u:
                t = u * 2
                tile(t, 0, True, True, True)
                tile(t + 1, 1, True, True, True)
            tile(NT - 1, 0, False, True, True)

        @block.tensor
        def _(pe):
            def turn(t, warm):
                pe.wait_ge(xn_done, t + 1)
                for k in range(KT):
                    if k % 4 == 0 and warm:
                        pe.wait_ge(tp_read, 2 * t + k // 4 - 1)
                    mm = pe.transpose(tp[k // 4][:, (k % 4) * P:(k % 4 + 1) * P], xn[:, k * P:(k + 1) * P], keep["ident"][:, :])
                    if k % 4 == 3:
                        mm.then_inc(tp_done, 1)

            def tile(t, j, more, warm):
                pe.wait_ge(tp_read, 2 * t + 2)
                for n in range(8):
                    if n >= 4:
                        pe.wait_ge(acc_read, evicted(t, n - 4))
                    elif warm and n == 3:
                        pe.wait_ge(gates_read, t)
                    elif warm:
                        pe.wait_ge(acc_read, evicted(t, n) - 3)
                    if not warm:
                        pe.wait_ge(w_in[min((n + 1) // 2, 3)], (16, 32, 32, 48)[min((n + 1) // 2, 3)])
                    for k in range(KT):
                        rhs = w[:, n, k, :] if n < 7 else wg[:, k, :]
                        dst = acc[n % 4][:, :] if n < 7 else acc[3][:, 0:NG]
                        mm = pe.matmul(dst, hT[j][:, k, :], rhs, start=(k == 0), stop=(k == KT - 1))
                    mm.then_inc(acc_done, 1)
                    if n == 5 and more:
                        turn(t + 1, True)

            turn(0, False)
            tile(0, 0, True, False)
            with pe.Fori(0, (NT - 3) // 2) as u:
                t = u * 2 + 1
                tile(t, 1, True, True)
                tile(t + 1, 0, True, True)
            tile(NT - 2, 1, True, True)
            tile(NT - 1, 0, False, True)

        @block.vector
        def _(dve):
            link = Links(dve, vec_link)
            dve.wait_ge(small_in, 64)

            def mean_square(t):
                dve.wait_ge(squares, t + 1)
                dve.tensor_scalar(stat[:, 1:2], stat[:, 0:1], 1.0 / D, EPS, ALU.mult, ALU.add).then_inc(mean_sq, 1)

            def normalise(t, j, warm):
                dve.wait_ge(rstd, t + 1)
                if warm:
                    dve.wait_ge(tp_done, 2 * t)
                dve.tensor_scalar(xn[:, :], xt[j][:, :], stat[:, 1:2], None, ALU.mult).then_inc(xn_done, 1)

            def modulate(t, j, v):
                if not isinstance(t, int) or t >= 2:
                    dve.wait_ge(acc_done, done(t - 2, 7))
                for k in range(KT):
                    if k % 4 == 0:
                        dve.wait_ge(tp_done, 2 * t + k // 4 + 1)
                    op = dve.tensor_scalar(hT[j][:, k, :], tp[k // 4][:, (k % 4) * P:(k % 4 + 1) * P],
                                           keep["gain"][:, 0, k, v:v + 1], keep["mod"][:, k, v:v + 1], ALU.mult, ALU.add)
                    if k % 4 == 3:
                        op.then_inc(tp_read, 1)

            def heads(t, j, n):
                dve.wait_ge(acc_read, evicted(t, n))
                q = out[j][:, n, :]
                link.wait(dve.tensor_tensor(tmp[:, 0, :], q, q, ALU.mult))
                link.wait(dve.tensor_reduce(hs[:, n, :], tmp[:, 0, :].rearrange("p (h d) -> p h d", h=AH), AX.X, ALU.add))
                dve.tensor_scalar(hs[:, n, :], hs[:, n, :], 1.0 / AD, EPS, ALU.mult, ALU.add).then_inc(head_sq, 1)

            def head_scale(t, j, n):
                dve.wait_ge(head_rstd, 2 * t + n + 1)
                q = out[j][:, n, :].rearrange("p (h d) -> p h d", h=AH)
                link.wait(dve.tensor_tensor(q, q, hs[:, n, :].rearrange("p (h a) -> p h a", a=1).to_broadcast([P, AH, AD]), ALU.mult))
                link.wait(dve.tensor_tensor(q, q, qkg[:, n:n + 1, :].to_broadcast([P, AH, AD]), ALU.mult))

            def rotary(t, j):
                dve.wait_ge(acc_read, evicted(t, MK))
                x = raw[:, :, :].rearrange("p b (h d) -> p (b h) d", h=MH)
                at = bass.ds(t, 1)
                c = cos[:, at, :].to_broadcast([P, 2 * MH, P])
                dst = out[j][:, MQ:MK + 1, :].rearrange("p b (h d) -> p (b h) d", h=MH)
                dve.tensor_tensor(dst, x, c, ALU.mult)
                xs = raw[:, :, :].rearrange("p b (h g a f) -> p (b h) g a f", h=MH, g=2, a=2)
                ss = sin[:, at, :].rearrange("p t (g a f) -> p t g a f", g=2, a=2)
                ts = tmp[:, :, :].rearrange("p b (h g a f) -> p (b h) g a f", h=MH, g=2, a=2)
                for a in range(2):
                    for g in range(2):
                        op = dve.tensor_tensor(ts[:, :, g, a, :], xs[:, :, g, 1 - a, :],
                                               ss[:, :, g, a, :].to_broadcast([P, 2 * MH, 32]), ALU.mult)
                op.then_inc(raw_read, 1)
                dve.wait_ge(raw_read, t + 1)
                y = out[j][:, MQ:MK + 1, :]
                link.wait(dve.tensor_tensor(y, y, tmp[:, :, :], ALU.add))

            def sigmoid(t, j):
                dve.wait_ge(acc_read, evicted(t, MO))
                o = out[j][:, MO, :]
                link.wait(dve.tensor_scalar(o, o, 1.0, None, ALU.add))
                dve.reciprocal(o, o).then_inc(vec_out, 1)

            def gates(t):
                dve.wait_ge(acc_done, done(t, 7))
                dve.tensor_tensor(keep["gates"][:, bass.ds(t, 1), :].rearrange("p a g -> p (a g)"), acc[3][:, 0:NG], bg[:, :], ALU.add).then_inc(gates_read, 1)

            def tile(t, j, more):
                link.start(PERV * t)
                for n in (AQ, AK):
                    heads(t, j, n)
                if more:
                    mean_square(t + 1)
                for n in (AQ, AK):
                    head_scale(t, j, n)
                if more:
                    normalise(t + 1, 1 - j, True)
                rotary(t, j)
                if more:
                    modulate(t + 1, 1 - j, 1)
                gates(t)
                sigmoid(t, j)
                assert link.k == PERV, link.k

            PERV = 10
            mean_square(0)
            normalise(0, 0, False)
            modulate(0, 0, 0)
            tile(0, 0, True)
            with dve.Fori(0, (NT - 3) // 2) as u:
                t = u * 2 + 1
                tile(t, 1, True)
                tile(t + 1, 0, True)
            tile(NT - 2, 1, True)
            tile(NT - 1, 0, False)



def mlstm(nc, io, keep):
    L = P - 1
    HD = MD + 1
    with ExitStack() as ctx:
        def sb(name, shape):
            return ctx.enter_context(nc.sbuf_tensor(name, shape, F32))

        def ps(name, shape):
            return ctx.enter_context(nc.psum_tensor(name, shape, F32))

        def sem(name):
            return ctx.enter_context(nc.semaphore(name))

        causal = sb("ml_causal", [P, 2, P])
        gsrc = sb("ml_gsrc", [P, 2, P])
        lf = sb("ml_lf", [P, P])
        ones = sb("ml_ones", [P, P])
        zeros = sb("ml_zeros", [P, P])
        scan_in = sb("ml_scan_in", [P, 2, P])
        bsum = sb("ml_bsum", [P, P])
        asc = sb("ml_asc", [P, P])
        mloc = sb("ml_mloc", [P, P])
        nat = sb("ml_nat", [P, 3, P])
        rows = sb("ml_rows", [1, 4, P])
        stm = sb("ml_stm", [1, 2 * MH])
        m0 = sb("ml_m0", [P, 1])
        mb = sb("ml_mb", [P, P])
        absf = sb("ml_absf", [P, P])
        nml = sb("ml_nml", [P, 1])
        quant = sb("ml_quant", [P, 4, P])
        negm = sb("ml_negm", [P, P])
        decay = sb("ml_decay", [P, 1])
        ddiag = sb("ml_ddiag", [P, P])
        cols = sb("ml_cols", [P, 3, P])
        decays = sb("ml_decays", [P, P])
        half = sb("ml_half", [P, NT])
        mlg = sb("ml_gain", [P, MW])
        nat_in = [sb(f"ml_nat_in{j}", [P, 3, NT, MD]) for j in range(2)]
        v_in = [sb(f"ml_v_in{j}", [P, NT, HD]) for j in range(2)]
        bc_in = [sb(f"ml_bc_in{j}", [P, 2, 2, NT, P]) for j in range(2)]
        st = [sb(f"ml_st{j}", [P, 2, 2, HD]) for j in range(2)]
        qkT = sb("ml_qkT", [P, 2, NT, P])
        s_raw = sb("ml_s_raw", [P, NT, P])
        qTw = [sb(f"ml_qTw{j}", [P, 2, NT, P]) for j in range(2)]
        kw = [sb(f"ml_kw{j}", [P, 2, NT, MD]) for j in range(2)]
        st_ctx = [sb(f"ml_st_ctx{j}", [P, 2, HD]) for j in range(2)]
        den = sb("ml_den", [P, NT, 2])
        hid = [sb(f"ml_hid{j}", [P, 2, NT, MD]) for j in range(2)]
        sq = sb("ml_sq", [P, NT, MD])
        rs = sb("ml_rs", [P, NT])
        tq = [ps(f"ml_tq{j}", [P, 4, P]) for j in range(2)]
        num = [ps(f"ml_num{j}", [P, 2, HD]) for j in range(4)]
        upd = [ps(f"ml_upd{j}", [P, 2, HD]) for j in range(2)]

        const_in = sem("ml_const_in")
        gv = sem("ml_gate_vec")
        ga = sem("ml_gate_act")
        gp = sem("ml_gate_pe")
        rows_out = sem("ml_rows_out")
        m_out = sem("ml_m_out")
        consts = sem("ml_consts")
        qk_in = [sem(f"ml_qk_in{j}") for j in range(2)]
        rest_in = [sem(f"ml_rest_in{j}") for j in range(2)]
        bc_landed = [sem(f"ml_bc_landed{j}") for j in range(2)]
        turned = sem("ml_turned")
        turned_read = sem("ml_turned_read")
        shifted = sem("ml_shifted")
        masked = sem("ml_masked")
        weights = sem("ml_weights")
        scores = sem("ml_scores")
        keyw = sem("ml_keyw")
        qw = sem("ml_qw")
        upd_done = sem("ml_upd_done")
        st_new = sem("ml_st_new")
        num_done = sem("ml_num_done")
        den_done = sem("ml_den_done")
        num_read = sem("ml_num_read")
        added = sem("ml_added")
        squared = sem("ml_squared")
        mean_sq = sem("ml_mean_sq")
        rstd = sem("ml_rstd")
        scaled = sem("ml_scaled")
        gated = sem("ml_gated")
        head_out = [sem(f"ml_head_out{j}") for j in range(2)]
        state_out = [sem(f"ml_state_out{j}") for j in range(2)]
        vec_link = sem("ml_vec_link")
        block = ctx.enter_context(nc.Block())

        ident = keep["ident"]
        UPDATES = NT - 1
        GROUPS = [(i, t) for i in range(3) for t in range(0, NT, 4)]

        def tiles_of(s):
            return (s, NT - s if s else 0)

        def row_of(r, t, h):
            return 64 * r + MH * t + h

        @block.sync
        def _(sp):
            sp.dma_start(causal[:, :, :], io["causal"]).then_inc(const_in, 16)
            sp.dma_start(stm[:, :], io["stm"]).then_inc(const_in, 16)
            sp.dma_start(mlg[:, :], io["mlg"]).then_inc(const_in, 16)

            def load_tiles(to, b, h):
                at = b * BLK + h * MD
                return sp.dma_start(to, io["proj"][:, :, at:at + MD].rearrange("t p d -> p t d"))

            def load_qk(h, j):
                load_tiles(nat_in[j][:, 0, :, :], MQ, h).then_inc(qk_in[j], 16)
                load_tiles(nat_in[j][:, 1, :, :], MK, h).then_inc(qk_in[j], 16)

            def load_rest(h, j):
                load_tiles(nat_in[j][:, 2, :, :], MO, h).then_inc(rest_in[j], 16)
                load_tiles(v_in[j][:, :, 0:MD], MV, h).then_inc(rest_in[j], 16)
                sp.dma_start(st[j][:, 0, :, :], io["stC"][:, h].rearrange("r d e -> d r e")).then_inc(rest_in[j], 16)

            def load_bc(h, j):
                for k in range(2):
                    for r in range(2):
                        src = io["mrows"][k:k + 1, r, 0:NT, h, :].to_broadcast([P, NT, P])
                        sp.dma_start(bc_in[j][:, k, r, :, :], src).then_inc(bc_landed[j], 16)

            load_qk(0, 0)
            load_rest(0, 0)
            sp.wait_ge(ga, 6)
            sp.wait_ge(gv, 4)
            sp.dma_start(io["mrows"][0].rearrange("r t h n -> (r t h) n"), negm[:, :]).then_inc(rows_out, 16)
            sp.dma_start(io["mrows"][1].rearrange("r t h n -> (r t h) n"), quant[:, 3, :]).then_inc(rows_out, 16)
            for r in range(2):
                sp.dma_start(io["new_m"][r:r + 1, :], rows[:, 2, 64 * r:64 * r + MH]).then_inc(m_out, 16)
            sp.wait_ge(rows_out, 32)
            load_bc(0, 0)
            load_qk(1, 1)
            load_bc(1, 1)
            load_rest(1, 1)
            for h in range(2, MH):
                j = h % 2
                sp.wait_ge(keyw, h - 1)
                sp.wait_ge(turned, len(GROUPS) * (h - 2) + 6)
                load_qk(h, j)
                sp.wait_ge(num_done, NT * (h - 1))
                load_bc(h, j)
                sp.wait_ge(head_out[j], 16 * (h // 2))
                load_rest(h, j)
            sp.wait_ge(m_out, 32)

        @block.tensor
        def _(pe):
            pe.wait_ge(gv, 1)
            pe.transpose(tq[0][:, 0, :], gsrc[:, 0, :], ident[:, :])
            pe.transpose(tq[0][:, 1, :], lf[:, :], ident[:, :]).then_inc(gp, 1)
            pe.wait_ge(gv, 2)
            pe.matmul(tq[1][0:1, 0, :], bsum[:, L:P], ident[:, :], start=True, stop=True)
            pe.matmul(tq[1][0:1, 1, :], mloc[:, L:P], ident[:, :], start=True, stop=True).then_inc(gp, 1)
            pe.wait_ge(gv, 3)
            pe.matmul(tq[0][:, 0, 0:1], rows[:, 3, :], ident[0:1, 0:1], start=True, stop=True).then_inc(gp, 1)
            pe.wait_ge(gv, 5)
            pe.wait_ge(ga, 6)
            for i in range(3):
                pe.transpose(tq[1][:, i, :], quant[:, i, :], ident[:, :])
            pe.matmul(tq[0][:, 0, :], ones[:, :], ddiag[:, :], start=True, stop=True).then_inc(gp, 1)
            pe.wait_ge(gv, 6)

            def group(h, g):
                j, (i, t0) = h % 2, GROUPS[g]
                n = len(GROUPS) * h + g
                if g == 0:
                    pe.wait_ge(qk_in[j], 32 * (h // 2 + 1))
                if n >= 2:
                    pe.wait_ge(turned_read, n - 1)
                if i == 2:
                    pe.wait_ge(turned_read, len(GROUPS) * h + 6)
                for t in range(t0, min(t0 + 4, NT)):
                    if i < 2:
                        mm = pe.transpose(tq[n % 2][:, t - t0, :], nat_in[j][:, i, t, :], ident[:, :])
                    else:
                        mm = pe.matmul(tq[n % 2][:, t - t0, :], qkT[:, 1, t, :], qkT[:, 0, t, :], start=True, stop=True)
                mm.then_inc(turned, 1)

            def step(h, s):
                j = h % 2
                if s == 0:
                    pe.wait_ge(rest_in[j], 48 * (h // 2 + 1))
                    pe.wait_ge(keyw, h + 1)
                if s < UPDATES:
                    u = UPDATES * h + s
                    if u >= 2:
                        pe.wait_ge(st_new, u - 1)
                    for r, t in enumerate(tiles_of(s)):
                        mm = pe.matmul(upd[s % 2][:, r, :], kw[j][:, r, t, :], v_in[j][:, t, :], start=True, stop=True)
                    mm.then_inc(upd_done, 1)
                if s == 0:
                    pe.wait_ge(scores, h + 1)
                    pe.wait_ge(qw, h + 1)
                n = NT * h + s
                if n >= 4:
                    pe.wait_ge(num_read, n - 3)
                if s > 1:
                    pe.wait_ge(st_new, UPDATES * h + s)
                for r, t in enumerate(tiles_of(s)):
                    mm = pe.matmul(num[n % 4][:, r, :], bc_in[j][:, 0, r, t, :], v_in[j][:, t, :], start=True, stop=(s == 0))
                    if s:
                        mm = pe.matmul(num[n % 4][:, r, :], qTw[j][:, r, t, :], st[j][:, (s - 1) % 2, r, :], start=False, stop=True)
                mm.then_inc(num_done, 1)

            for g in range(len(GROUPS)):
                group(0, g)
            for h in range(MH):
                for s in range(NT):
                    step(h, s)
                    if h + 1 < MH:
                        group(h + 1, s)

        @block.scalar
        def _(act):
            act.wait_ge(consts, 1)
            act.activation(lf[:, :], absf[:, :], ACT.Exp, scale=-1.0).then_inc(ga, 1)
            act.wait_ge(ga, 1)
            act.activation(lf[:, :], lf[:, :], ACT.Ln, bias=1.0).then_inc(ga, 1)
            act.wait_ge(gv, 4)
            act.activation(quant[:, 1, :], nat[:, 0, :], ACT.Exp, bias=nml[:, 0:1]).then_inc(ga, 1)
            act.activation(quant[:, 2, :], mb[:, :], ACT.Exp, scale=-1.0).then_inc(ga, 1)
            act.activation(quant[:, 3, :], nat[:, 1, :], ACT.Exp, scale=-1.0, bias=m0[:, 0:1]).then_inc(ga, 1)
            act.activation(decay[:, :], m0[:, :], ACT.Exp, bias=nml[:, 0:1]).then_inc(ga, 1)
            def take(h, g):
                i, t0 = GROUPS[g]
                n = len(GROUPS) * h + g
                nt = min(4, NT - t0)
                act.wait_ge(turned, n + 1)
                if h and g == 0:
                    act.wait_ge(qw, h)
                if h and g == 6:
                    act.wait_ge(scores, h)
                dst = s_raw[:, t0:t0 + nt, :] if i == 2 else qkT[:, i, t0:t0 + nt, :]
                act.activation(dst, tq[n % 2][:, 0:nt, :], ACT.Copy).then_inc(turned_read, 1)

            def exps(h):
                act.wait_ge(masked, h + 1)
                w = bc_in[h % 2][:, 0, :, :, :]
                act.activation(w, w, ACT.Exp).then_inc(weights, 1)

            def square(h):
                act.wait_ge(added, h + 1)
                act.activation(sq[:, :, :], hid[h % 2][:, 0, :, :], ACT.Square).then_inc(squared, 1)

            def step(h, s):
                j, n = h % 2, NT * h + s
                if h >= 2 and s == 0:
                    act.wait_ge(head_out[j], 16 * (h // 2))
                act.wait_ge(den_done, n + 1)
                for r, t in enumerate(tiles_of(s)):
                    op = act.activation(hid[j][:, r, t, :], num[n % 4][:, r, 0:MD], ACT.Copy, scale=den[:, s, r:r + 1])
                op.then_inc(num_read, 1)

            for g in range(len(GROUPS)):
                take(0, g)
            exps(0)
            for h in range(MH):
                for s in range(NT):
                    step(h, s)
                    if h and s == 1:
                        square(h - 1)
                    if h + 1 < MH:
                        take(h + 1, s)
                if h + 1 < MH:
                    exps(h + 1)
            square(MH - 1)

        @block.gpsimd
        def _(pool):
            pool.memset(half[:, :], -0.5)
            pool.wait_ge(const_in, 48)

            def mask(h):
                pool.wait_ge(shifted, h + 1)
                for r in range(2):
                    w = bc_in[h % 2][:, 0, r, :, :]
                    op = pool.tensor_tensor(w, w, causal[:, r:r + 1, :].to_broadcast([P, NT, P]), ALU.add)
                op.then_inc(masked, 1)

            def finish(h):
                j = h % 2
                pool.wait_ge(num_read, NT * (h + 1))
                pool.tensor_tensor(hid[j][:, 0, :, :], hid[j][:, 0, :, :], hid[j][:, 1, :, :], ALU.add).then_inc(added, 1)
                pool.wait_ge(mean_sq, h + 1)
                pool.tensor_tensor(rs[:, :], rs[:, :], half[:, :], ALU.pow).then_inc(rstd, 1)
                pool.wait_ge(scaled, h + 1)
                pool.tensor_tensor(hid[j][:, 0, :, :], hid[j][:, 0, :, :], nat_in[j][:, 2, :, :], ALU.mult).then_inc(gated, 1)
                pool.wait_ge(gated, h + 1)
                at = AW + h * MD
                pool.dma_start(io["mix"][:, :, at:at + MD].rearrange("t p d -> p t d"), hid[j][:, 0, :, :]).then_inc(head_out[j], 16)
                pool.wait_ge(st_new, UPDATES * h + 1)
                pool.dma_start(io["new_st"][:, h].rearrange("r d e -> d r e"), st_ctx[j][:, :, :]).then_inc(state_out[j], 16)

            mask(0)
            for h in range(MH):
                if h:
                    finish(h - 1)
                if h + 1 < MH:
                    mask(h + 1)
            finish(MH - 1)
            for j in range(2):
                pool.wait_ge(head_out[j], 16 * MH // 2)
                pool.wait_ge(state_out[j], 16 * MH // 2)

        @block.vector
        def _(dve):
            link = Links(dve, vec_link)
            dve.wait_ge(const_in, 48)
            for x in (gsrc, zeros, rows):
                dve.memset(x[:], 0.0)
            for j in range(2):
                dve.memset(v_in[j][:, :, MD:HD], 1.0)
            link.wait(dve.memset(ones[:, :], 1.0))
            for r in range(2):
                for i in range(2):
                    op = dve.tensor_copy(gsrc[:, i, 64 * r:64 * r + NT * MH].rearrange("p (t h) -> p t h", h=MH),
                                         keep["gates"][:, :, 8 * r + 4 * i:8 * r + 4 * i + 4])
            link.wait(op)
            f = gsrc[:, 1, :]
            link.wait(dve.tensor_scalar(absf[:, :], f, -1.0, None, ALU.mult))
            dve.tensor_tensor(absf[:, :], absf[:, :], f, ALU.max).then_inc(consts, 1)
            dve.wait_ge(ga, 2)
            dve.scalar_tensor_tensor(out=lf[:, :], in0=f, scalar=0.0, in1=lf[:, :], op0=ALU.min, op1=ALU.subtract).then_inc(gv, 1)
            dve.wait_ge(gp, 1)
            dve.tensor_copy(scan_in[0:64, :, :], tq[0][0:64, 0:2, :])
            link.wait(dve.tensor_copy(scan_in[64:P, :, :], tq[0][64:P, 0:2, ::-1]))
            link.wait(dve.tensor_tensor_scan(bsum[:, :], scan_in[:, 1, :], zeros[:, :], 0.0, ALU.add, ALU.add))
            link.wait(dve.tensor_tensor(asc[:, :], scan_in[:, 0, :], bsum[:, :], ALU.subtract))
            dve.tensor_tensor_scan(mloc[:, :], asc[:, :], asc[:, :], -3e38, ALU.max, ALU.max).then_inc(gv, 1)
            dve.wait_ge(gp, 2)
            link.wait(dve.tensor_copy(rows[:, 0:2, :], tq[1][0:1, 0:2, :]))
            for r in range(2):
                for h in range(MH):
                    a = 64 * r + MH + h
                    cut = slice(a, a + MH * 7 + 1, MH) if r == 0 else slice(a + MH * 7, a - 1, -MH)
                    dve.tensor_tensor_scan(rows[:, 2, cut], rows[:, 1, cut], rows[:, 0, cut], stm[:, MH * r + h:MH * r + h + 1],
                                           ALU.max, ALU.add)
                c = slice(64 * r, 64 * r + MH)
                op = dve.scalar_tensor_tensor(out=rows[:, 2, c], in0=rows[:, 1, c], scalar=0.0, in1=rows[:, 0, c],
                                              op0=ALU.max, op1=ALU.add)
            link.wait(op)
            dve.tensor_copy(rows[:, 3, 8:36], rows[:, 2, 4:32])
            dve.tensor_copy(rows[:, 3, 68:96], rows[:, 2, 72:100])
            dve.tensor_copy(rows[:, 3, 4:8], stm[:, 0:MH])
            dve.tensor_copy(rows[:, 3, 96:100], stm[:, MH:2 * MH]).then_inc(gv, 1)
            dve.wait_ge(gp, 3)
            link.wait(dve.tensor_copy(m0[:, :], tq[0][:, 0, 0:1]))
            link.wait(dve.tensor_scalar(mloc[:, :], mloc[:, :], m0[:, 0:1], None, ALU.max))
            dve.tensor_scalar(nml[:, :], mloc[:, L:P], -1.0, None, ALU.mult)
            for i, x in enumerate((asc, mloc, bsum)):
                dve.tensor_copy(nat[0:64, i, :], x[0:64, :])
                op = dve.tensor_copy(nat[64:P, i, :], x[64:P, ::-1])
            link.wait(op)
            dve.tensor_tensor(mb[:, :], nat[:, 1, :], nat[:, 2, :], ALU.add)
            dve.tensor_scalar(negm[:, :], nat[:, 1, :], -1.0, None, ALU.mult).then_inc(gv, 1)
            dve.tensor_copy(quant[:, 0, :], nat[:, 0, :])
            dve.wait_ge(ga, 6)
            dve.tensor_scalar(ddiag[:, :], ident[:, :], decay[:, 0:1], None, ALU.mult).then_inc(gv, 1)
            dve.wait_ge(gp, 4)
            dve.tensor_copy(cols[:, :, :], tq[1][:, 0:3, :])
            dve.tensor_copy(decays[:, :], tq[0][:, 0, :]).then_inc(gv, 1)
            dve.wait_ge(gv, 6)

            def by_tile(i, h, n):
                c = cols[:, i, :].rearrange("p (r t h) -> p r t h", r=2, h=MH)[:, :, 0:NT, h:h + 1]
                return c.to_broadcast([P, 2, NT, n])

            def shift(h):
                dve.wait_ge(bc_landed[h % 2], 64 * (h // 2 + 1))
                w = bc_in[h % 2][:, 0, :, :, :]
                dve.tensor_tensor(w, w, by_tile(0, h, P), ALU.add).then_inc(shifted, 1)

            def keys(h, r):
                j = h % 2
                if r == 0:
                    dve.wait_ge(qk_in[j], 32 * (h // 2 + 1))
                    if h >= 2:
                        dve.wait_ge(upd_done, UPDATES * (h - 1))
                c = cols[:, 1, :].rearrange("p (r t h) -> p r t h", r=2, h=MH)[:, r, 0:NT, h:h + 1]
                op = dve.tensor_tensor(kw[j][:, r, :, :], nat_in[j][:, 1, :, :], c.to_broadcast([P, NT, MD]), ALU.mult)
                if r:
                    op.then_inc(keyw, 1)

            def queries(h, r):
                j = h % 2
                if r == 0:
                    dve.wait_ge(turned_read, len(GROUPS) * h + 3)
                    if h >= 2:
                        dve.wait_ge(num_done, NT * (h - 1))
                op = dve.tensor_tensor(qTw[j][:, r, :, :], qkT[:, 0, :, :], bc_in[j][:, 1, r, :, :], ALU.mult)
                if r:
                    op.then_inc(qw, 1)

            def weigh(h):
                dve.wait_ge(turned_read, len(GROUPS) * (h + 1))
                dve.wait_ge(weights, h + 1)
                for r in range(2):
                    w = bc_in[h % 2][:, 0, r, :, :]
                    op = dve.tensor_tensor(w, w, s_raw[:, :, :], ALU.mult)
                op.then_inc(scores, 1)

            def step(h, s):
                j, n = h % 2, NT * h + s
                if s < UPDATES:
                    dve.wait_ge(upd_done, UPDATES * h + s + 1)
                    if s == 0:
                        if h >= 2:
                            dve.wait_ge(state_out[j], 16 * (h // 2))
                        dve.tensor_copy(st_ctx[j][:, :, :], upd[0][:, :, :]).then_inc(st_new, 1)
                    else:
                        if s > 1:
                            dve.wait_ge(num_done, n)
                        dve.wait_ge(st_new, UPDATES * h + s)
                        for r, t in enumerate(tiles_of(s)):
                            c = row_of(r, t, h)
                            op = dve.scalar_tensor_tensor(out=st[j][:, s % 2, r, :], in0=st[j][:, (s - 1) % 2, r, :],
                                                          scalar=decays[:, c:c + 1], in1=upd[s % 2][:, r, :],
                                                          op0=ALU.mult, op1=ALU.add)
                        op.then_inc(st_new, 1)
                dve.wait_ge(num_done, n + 1)
                if s == 0 and h:
                    dve.wait_ge(num_read, n)
                for r, t in enumerate(tiles_of(s)):
                    c = row_of(r, t, h)
                    op = dve.tensor_scalar(den[:, s, r:r + 1], num[n % 4][:, r, MD:HD], -1.0, cols[:, 2, c:c + 1],
                                           ALU.mult, ALU.max)
                link.wait(op)
                link.wait(dve.tensor_tensor(den[:, s, :], den[:, s, :], num[n % 4][:, :, MD], ALU.max))
                dve.reciprocal(den[:, s, :], den[:, s, :]).then_inc(den_done, 1)

            def mean_square(h):
                dve.wait_ge(squared, h + 1)
                link.wait(dve.tensor_reduce(rs[:, :], sq[:, :, :], AX.X, ALU.add))
                dve.tensor_scalar(rs[:, :], rs[:, :], 1.0 / MD, EPS, ALU.mult, ALU.add).then_inc(mean_sq, 1)

            def normalise(h):
                dve.wait_ge(rstd, h + 1)
                y = hid[h % 2][:, 0, :, :]
                link.wait(dve.tensor_tensor(y, y, rs[:, :].rearrange("p (t a) -> p t a", a=1).to_broadcast([P, NT, MD]), ALU.mult))
                dve.tensor_tensor(y, y, mlg[:, h * MD:(h + 1) * MD].rearrange("p (a d) -> p a d", a=1).to_broadcast([P, NT, MD]),
                                  ALU.mult).then_inc(scaled, 1)

            shift(0)
            keys(0, 0)
            keys(0, 1)
            queries(0, 0)
            queries(0, 1)
            weigh(0)
            for h in range(MH):
                for s in range(NT):
                    step(h, s)
                    if h and s == 2:
                        mean_square(h - 1)
                    if h and s == 3:
                        normalise(h - 1)
                    if h + 1 < MH:
                        if s == 0 and h == 0 or s == 4 and h:
                            shift(h + 1)
                        if s in (1, 2):
                            keys(h + 1, s - 1)
                        if s in (5, 6):
                            queries(h + 1, s - 5)
                if h + 1 < MH:
                    weigh(h + 1)
            mean_square(MH - 1)
            normalise(MH - 1)



def attention(nc, io, keep):
    SCALE = AD ** -0.5
    WR = 8
    JR = 14
    HP = AH // 2
    LT = NT - 1
    WINDOWS = []
    for i in range(LT):
        first = [min(max(r - WR // 2, 0), LAT // GRID_W - WR) for r in (2 * i, 2 * i + 1)]
        WINDOWS.append((first[0], first[1] + WR - first[0], first[0] - 2 * i + 7 - 1, first[1] != first[0]))
    with ExitStack() as ctx:
        def sb(name, shape):
            return ctx.enter_context(nc.sbuf_tensor(name, shape, F32))

        def ps(name, shape):
            return ctx.enter_context(nc.psum_tensor(name, shape, F32))

        def sem(name):
            return ctx.enter_context(nc.semaphore(name))

        qk_nat = sb("at_qk_nat", [P, NT + 1, 2, AW])
        v_nat = sb("at_v_nat", [P, NT + 1, AW])
        qT = sb("at_qT", [P, 2, HP, NT, P])
        kT = sb("at_kT", [P, HP, NT + 1, P])
        window = sb("at_window", [P, GRID_W])
        rowmask = sb("at_rowmask", [P, WR + 1])
        zeros = sb("at_zeros", [P, P])
        table = [sb(f"at_table{j}", [P, JR, GRID_W]) for j in range(2)]
        inner = [sb(f"at_inner{j}", [P, WR + 1, GRID_W]) for j in range(2)]
        prob = [sb(f"at_prob{j}", [P, 11 * GRID_W]) for j in range(3)]
        probT = [sb(f"at_probT{j}", [P, 6, P]) for j in range(2)]
        low = sb("at_low", [P, 9 * AH, 2])
        total = sb("at_total", [P, 9 * AH])
        heads = [sb(f"at_heads{j}", [P, LT, 2, AD]) for j in range(2)]
        first_rows = sb("at_first_rows", [P, AH, AD])
        score = [ps(f"at_score{j}", [P, 2 * BLK]) for j in range(2)]
        turn = [ps(f"at_turn{j}", [P, 4, P]) for j in range(2)]
        outp = [ps(f"at_out{j}", [P, 8, AD]) for j in range(2)]

        const_in = sem("at_const_in")
        tile_in = [sem(f"at_tile_in{j}") for j in range((NT + 1) // 2)]
        table_in = [sem(f"at_table_in{j}") for j in range(2)]
        table_ready = sem("at_table_ready")
        laid = sem("at_laid")
        laid_vec = sem("at_laid_vec")
        laid_act = sem("at_laid_act")
        scored = sem("at_scored")
        biased = sem("at_biased")
        expd = sem("at_expd")
        turned = [sem(f"at_turned{j}") for j in range(2)]
        taken = [sem(f"at_taken{j}") for j in range(2)]
        summed = sem("at_summed")
        scaled = sem("at_scaled")
        out_free = sem("at_out_free")
        pair_out = [sem(f"at_pair_out{j}") for j in range(2)]
        first_out = sem("at_first_out")
        vec_link = sem("at_vec_link")
        pool_link = sem("at_pool_link")
        block = ctx.enter_context(nc.Block())

        units = []
        for h in range(AH):
            units.append((h, 0))
        for h in range(AH):
            for i in range(LT):
                units.append((h, i + 1))
        N = len(units)

        def local_cols(t):
            return GRID_W * WINDOWS[t - 1][1] if t else 0

        def pieces(h, t):
            if t == 0:
                return [(0, P, kT[:, h // 2, 0, :])]
            u0, nr, _, _ = WINDOWS[t - 1]
            keys = kT[:, h // 2, 1:, :].rearrange("p t n -> p (t n)")
            out = [(0, BLK, keys[:, GRID_W * u0:GRID_W * u0 + BLK])]
            n = GRID_W * nr
            if n > BLK:
                out.append((BLK, n - BLK, keys[:, GRID_W * u0 + BLK:GRID_W * u0 + n]))
            return out + [(n, P, kT[:, h // 2, NT, :])]

        def blocks(h, t):
            cols = slice(AD * h, AD * h + AD)
            if t == 0:
                return [(0, P, v_nat[:, 0, cols])]
            u0, nr, _, _ = WINDOWS[t - 1]
            n, out = GRID_W * nr, []
            for c in range(0, n, P):
                k = min(P, n - c)
                out.append((c, k, v_nat[0:k, 1 + (GRID_W * u0 + c) // P, cols]))
            return out + [(n, P, v_nat[:, NT, cols])]

        GROUPS = [(i, t) for t in range(NT) for i in range(2)] + [(1, NT)]

        def lay(copy, g):
            i, t = GROUPS[g]
            src = score[g % 4 // 2][:, g % 2 * BLK:g % 2 * BLK + BLK].rearrange("p (m n) -> p m n", n=P)
            if i:
                return copy(kT[:, :, t, :], src)
            for b in range(2):
                rows = slice(AD * b, AD * b + AD)
                op = copy(qT[rows, b, :, t, :], src[rows])
            return op

        def store(eng, hp):
            eng.wait_ge(scaled, 2 * hp + 3)
            eng.dma_start(io["mix"][1:NT, :, hp * P:(hp + 1) * P].rearrange("t p d -> p t d"),
                          heads[hp % 2][:, :, :, :].rearrange("p t b d -> p t (b d)")).then_inc(pair_out[hp % 2], 16)

        @block.sync
        def _(sp):
            sp.dma_start(window[:, :], io["window"]).then_inc(const_in, 16)
            sp.dma_start(rowmask[:, :], io["rowmask"]).then_inc(const_in, 16)
            for t in range(NT):
                sp.dma_start(qk_nat[:, t, :, :], io["proj"][t, :, 0:2 * AW].rearrange("p (b n) -> p b n", b=2)).then_inc(tile_in[t // 2], 16)
                sp.dma_start(v_nat[:, t, :], io["proj"][t, :, 2 * AW:3 * AW]).then_inc(tile_in[t // 2], 16)
            sp.dma_start(qk_nat[:, NT, 1, :], io["ck"]).then_inc(tile_in[NT // 2], 16)
            sp.dma_start(v_nat[:, NT, :], io["cv"]).then_inc(tile_in[NT // 2], 16)
            for h in range(AH):
                if h >= 2:
                    sp.wait_ge(biased, AH + LT * (h - 1))
                rows = io["bias_rows"]
                for half in range(2):
                    src = bass.AP(tensor=rows.tensor, offset=h * GRID_W * 15 * 127 + (1 - half) * 127 + GRID_W - 1,
                                  ap=[[15 * 127 - 1, GRID_W], [127, JR], [1, GRID_W]])
                    sp.dma_start(table[h % 2][GRID_W * half:GRID_W * (half + 1), :, :], src).then_inc(table_in[h % 2], 16)

        @block.gpsimd
        def _(pool):
            pool.wait_ge(const_in, 32)
            link = Links(pool, pool_link)
            for h in range(AH):
                b, s = table[h % 2], inner[h % 2]
                pool.wait_ge(table_in[h % 2], 32 * (h // 2 + 1))
                link.wait(pool.tensor_scalar(b[:, :, :], b[:, :, :], 1 / SCALE, None, ALU.mult))
                link.wait(pool.tensor_tensor(b[:, :, :], b[:, :, :],
                                             window[:, :].rearrange("p (a n) -> p a n", a=1).to_broadcast([P, JR, GRID_W]), ALU.add))
                pool.tensor_tensor(s[:, :, :], b[:, 2:2 + WR + 1, :],
                                   rowmask[:, :].rearrange("p (r a) -> p r a", a=1).to_broadcast([P, WR + 1, GRID_W]), ALU.add)\
                    .then_inc(table_ready, 1)
                if h == 0:
                    pool.wait_ge(scaled, 1)
                    pool.dma_start(io["mix"][0, :, 0:AW], first_rows[:, :, :].rearrange("p h d -> p (h d)")).then_inc(first_out, 16)
                elif h % 2 == 1 and h >= 3:
                    store(pool, (h - 3) // 2)
            store(pool, 3)
            pool.wait_ge(first_out, 16)
            pool.wait_ge(pair_out[0], 32)
            pool.wait_ge(pair_out[1], 32)

        @block.tensor
        def _(pe):
            ident = keep["ident"]
            for g, (i, t) in enumerate(GROUPS):
                bank = score[g % 4 // 2][:, (g % 2) * BLK:(g % 2 + 1) * BLK]
                if g >= 4:
                    pe.wait_ge((laid_vec, laid_act)[g % 2], g // 2 - 1)
                pe.wait_ge(tile_in[t // 2], 64)
                for hp in range(HP):
                    mm = pe.transpose(bank[:, hp * P:(hp + 1) * P], qk_nat[:, t, i, hp * P:(hp + 1) * P], ident[:, :])
                mm.then_inc(laid, 1)
            pe.wait_ge(laid_vec, (len(GROUPS) + 1) // 2)
            pe.wait_ge(laid_act, len(GROUPS) // 2)

            def raw_scores(n):
                h, t = units[n]
                if n >= 2:
                    pe.wait_ge(biased, n - 1)
                q = qT[:, h % 2, h // 2, t, :]
                for c, k, keys in pieces(h, t):
                    mm = pe.matmul(score[n % 2][:, c:c + k], q, keys, start=True, stop=True)
                mm.then_inc(scored, 1)

            def turn_probs(n):
                h, t = units[n]
                pe.wait_ge(expd, n + 1)
                if n >= 1:
                    pe.wait_ge(taken[0], n)
                bl = blocks(h, t)
                for b, (c, k, _) in enumerate(bl):
                    if b == 4:
                        pe.wait_ge(taken[1], n)
                    mm = pe.transpose(turn[b // 4][0:k, b % 4, :], prob[n % 3][:, c:c + k], ident[:, :])
                    if b == min(3, len(bl) - 1):
                        mm.then_inc(turned[0], 1)
                if len(bl) > 4:
                    mm.then_inc(turned[1], 1)

            def values(n):
                h, t = units[n]
                bank = 0 if n < AH else (h + 1) % 2
                slot = h if n < AH else t - 1
                if n >= AH and slot == 0 and h >= 1:
                    pe.wait_ge(scaled, h)
                pe.wait_ge(taken[0], n + 1)
                pe.wait_ge(taken[1], n + 1)
                bl = blocks(h, t)
                for b, (c, k, v) in enumerate(bl):
                    mm = pe.matmul(outp[bank][:, slot, :], probT[n % 2][0:k, b, :], v, start=(b == 0), stop=(b == len(bl) - 1))
                mm.then_inc(summed, 1)

            for n in range(N + 2):
                if n < N:
                    raw_scores(n)
                if 1 <= n <= N:
                    turn_probs(n - 1)
                if n >= 2:
                    values(n - 2)

        @block.scalar
        def _(act):
            for g in range(1, len(GROUPS), 2):
                act.wait_ge(laid, g + 1)
                lay(lambda to, src: act.activation(to, src, ACT.Copy), g).then_inc(laid_act, 1)

            def exps(n):
                h, t = units[n]
                w = local_cols(t) + P
                act.wait_ge(biased, n + 1)
                p = prob[n % 3][:, 0:w]
                act.activation(p, p, ACT.Exp, scale=-1.0, bias=low[:, n, 1:2], accum_out=total[:, n:n + 1]).then_inc(expd, 1)

            def take(n):
                h, t = units[n]
                if t == 0:
                    act.wait_ge(expd, n + 1)
                    act.activation(low[0:1, n, 0:1], low[0:1, n, 1:2], ACT.Copy).then_inc(taken[1], 1)
                    return
                act.wait_ge(turned[1], n - AH + 1)
                if n >= 2:
                    act.wait_ge(summed, n - 1)
                bl = blocks(h, t)[4:]
                for b, (c, k, _) in enumerate(bl):
                    if len(bl) == 1 or k < P:
                        op = act.activation(probT[n % 2][0:k, 4 + b, :], turn[1][0:k, b, :], ACT.Copy)
                    else:
                        op = act.activation(probT[n % 2][:, 4 + b, :], turn[1][:, b, :], ACT.Copy)
                op.then_inc(taken[1], 1)

            for n in range(N + 1):
                if n < N:
                    exps(n)
                if n >= 1:
                    take(n - 1)

        @block.vector
        def _(dve):
            link = Links(dve, vec_link)
            link.wait(dve.memset(zeros[:, :], 0.0))
            dve.memset(qT[AD:P, 0, :, :, :], 0.0)
            dve.memset(qT[0:AD, 1, :, :, :], 0.0)
            for g in range(0, len(GROUPS), 2):
                dve.wait_ge(laid, g + 1)
                lay(dve.tensor_copy, g).then_inc(laid_vec, 1)

            def bias(n):
                h, t = units[n]
                dve.wait_ge(scored, n + 1)
                if n >= 3:
                    dve.wait_ge(turned[0], n - 2)
                    if n - 3 >= AH:
                        dve.wait_ge(turned[1], n - 2 - AH)
                w = local_cols(t)
                s, p = score[n % 2], prob[n % 3]
                start = 3e38
                if t:
                    _, nr, j0, differ = WINDOWS[t - 1]
                    if t == 1:
                        dve.wait_ge(table_ready, h + 1)
                    tab = inner[h % 2][:, 0:nr, :] if differ else table[h % 2][:, j0:j0 + nr, :]
                    link.wait(dve.tensor_tensor_reduce(p[:, 0:w], s[:, 0:w], tab.rearrange("p r n -> p (r n)"), -SCALE, start,
                                                       ALU.add, ALU.min, low[:, n, 0:1]))
                    start = low[:, n, 0:1]
                dve.tensor_tensor_reduce(p[:, w:w + P], s[:, w:w + P], zeros[:, :], -SCALE, start,
                                         ALU.add, ALU.min, low[:, n, 1:2]).then_inc(biased, 1)

            def take(n):
                h, t = units[n]
                dve.wait_ge(turned[0], n + 1)
                if n >= 2:
                    dve.wait_ge(summed, n - 1)
                nb = 4 if t else 1
                dve.tensor_copy(probT[n % 2][:, 0:nb, :], turn[0][:, 0:nb, :]).then_inc(taken[0], 1)

            def scale(g):
                c = slice(8 * g, 8 * g + 8)
                link.wait(dve.reciprocal(total[:, c], total[:, c]))
                dve.wait_ge(summed, 8 * g + 8)
                h = g - 1
                dst = first_rows[:, :, :] if g == 0 else heads[h // 2 % 2][:, :, h % 2, :]
                if g and h // 2 >= 2:
                    dve.wait_ge(pair_out[h // 2 % 2], 16)
                dve.tensor_tensor(dst, outp[g % 2][:, :, :], total[:, c].rearrange("p (t a) -> p t a", a=1).to_broadcast([P, 8, AD]),
                                  ALU.mult).then_inc(scaled, 1)

            for n in range(N + 2):
                if n < N:
                    bias(n)
                if 1 <= n <= N:
                    take(n - 1)
                if n >= 9 and (n - 9) % 8 == 1:
                    scale((n - 10) // 8)
            scale(N // 8 - 1) if (N + 1 - 9) % 8 != 1 else None



GAP = 2
TW = CTX + GAP + LAT
CUTS = [(0, CTX + GAP + 2 * P), (CTX + GAP + 2 * P, 3 * P), (CTX + GAP + 5 * P, 3 * P)]


def column_of(t):
    return t * P + (GAP if t else 0)


def output_projection(nc, io, keep):
    with ExitStack() as ctx:
        def sb(name, shape):
            return ctx.enter_context(nc.sbuf_tensor(name, shape, F32))

        def ps(name, shape):
            return ctx.enter_context(nc.psum_tensor(name, shape, F32))

        def sem(name):
            return ctx.enter_context(nc.semaphore(name))

        w = sb("op_w", [P, KT, D])
        mt = [sb(f"op_mix{j}", [P, MIX]) for j in range(3)]
        xt = [sb(f"op_x{j}", [P, D]) for j in range(3)]
        mT = [sb(f"op_mixT{j}", [P, KT, P]) for j in range(2)]
        x1 = [sb(f"op_x1{j}", [P, D]) for j in range(2)]
        xn = [sb(f"op_xn{j}", [P, D]) for j in range(2)]
        junk = sb("op_junk", [P, D])
        h2 = [sb(f"op_h2{g}", [P, 4, P]) for g in range(2)]
        stat = sb("op_stat", [P, NT, 2])
        half = sb("op_half", [P, 1])
        zeros = sb("op_zeros", [P, KT * GAP])
        tp = [ps(f"op_tp{j}", [P, 4, P]) for j in range(4)]
        acc = [ps(f"op_acc{j}", [P, BLK]) for j in range(4)]
        w_in = sem("op_w_in")
        half_set = sem("op_half_set")
        t_in = [sem(f"op_t_in{j}") for j in range(3)]
        turned = sem("op_turned")
        turned_read = sem("op_turned_read")
        acc_done = sem("op_acc_done")
        gated = sem("op_gated")
        x1_done = sem("op_x1_done")
        squares = sem("op_squares")
        mean_sq = sem("op_mean_sq")
        rstd = sem("op_rstd")
        xn_done = sem("op_xn_done")
        xn_turned = sem("op_xn_turned")
        xn_read = sem("op_xn_read")
        h2_hi = sem("op_h2_hi")
        h2_lo = sem("op_h2_lo")
        x1_out = [sem(f"op_x1_out{j}") for j in range(2)]
        block = ctx.enter_context(nc.Block())

        @block.sync
        def _(sp):
            for t in range(NT):
                if t >= 3:
                    sp.wait_ge(x1_done, t - 2)
                    sp.wait_ge(turned, 2 * t - 4)
                sp.dma_start(mt[t % 3][:, :], io["mix"][t]).then_inc(t_in[t % 3], 16)
                sp.dma_start(xt[t % 3][:, :], io["x"][t]).then_inc(t_in[t % 3], 16)
                if t == 0:
                    sp.dma_start(w[:, :, :], io["w_out"]).then_inc(w_in, 16)

        @block.gpsimd
        def _(pool):
            pool.memset(half[:, :], -0.5).then_inc(half_set, 1)
            pool.wait_ge(half_set, 1)
            for t in range(NT):
                pool.wait_ge(x1_done, t + 1)
                pool.dma_start(io["x1"][t], x1[t % 2][:, :]).then_inc(x1_out[t % 2], 16)
                pool.wait_ge(mean_sq, t + 1)
                pool.tensor_tensor(stat[:, t, 1:2], stat[:, t, 1:2], half[:, :], ALU.pow).then_inc(rstd, 1)
            pool.wait_ge(x1_out[0], 16 * ((NT + 1) // 2))
            pool.wait_ge(x1_out[1], 16 * (NT // 2))

        @block.tensor
        def _(pe):
            def turn(t):
                pe.wait_ge(t_in[t % 3], 32 * (t // 3 + 1))
                for g in range(2):
                    if t:
                        pe.wait_ge(turned_read, 2 * (t - 1) + g + 1)
                    for k in range(4):
                        mm = pe.transpose(tp[g][:, k, :], mt[t % 3][:, (4 * g + k) * P:(4 * g + k + 1) * P], keep["ident"][:, :])
                    mm.then_inc(turned, 1)

            def turn_xn(t):
                pe.wait_ge(xn_done, t + 1)
                for g in range(2):
                    if t:
                        pe.wait_ge(xn_read, 2 * (t - 1) + g + 1)
                    for k in range(4):
                        mm = pe.transpose(tp[2 + g][:, k, :], xn[t % 2][:, (4 * g + k) * P:(4 * g + k + 1) * P], keep["ident"][:, :])
                    mm.then_inc(xn_turned, 1)

            turn(0)
            pe.wait_ge(w_in, 16)
            for t in range(NT):
                if t + 1 < NT:
                    turn(t + 1)
                pe.wait_ge(turned_read, 2 * t + 2)
                for b in range(2):
                    n = 2 * t + b
                    if n >= 4:
                        pe.wait_ge(gated, n - 3)
                    for k in range(KT):
                        mm = pe.matmul(acc[n % 4][:, :], mT[t % 2][:, k, :], w[:, k, b * BLK:(b + 1) * BLK], start=(k == 0), stop=(k == KT - 1))
                    mm.then_inc(acc_done, 1)
                if t:
                    turn_xn(t - 1)
            turn_xn(NT - 1)

        @block.scalar
        def _(act):
            def square(t):
                act.wait_ge(x1_done, t + 1)
                act.activation(junk[:, :], x1[t % 2][:, :], ACT.Square, accum_out=stat[:, t, 0:1]).then_inc(squares, 1)

            def high(t):
                for g in range(2):
                    act.wait_ge(xn_read, 2 * t + g + 1)
                    act.activation(keep["h2h"][:, 4 * g:4 * g + 4, column_of(t):column_of(t) + P], h2[g][:, :, :], ACT.Copy)\
                       .then_inc(h2_hi, 1)

            for t in range(NT):
                for g in range(2):
                    act.wait_ge(turned, 2 * t + g + 1)
                    if t >= 2:
                        act.wait_ge(acc_done, 2 * t - 2)
                    act.activation(mT[t % 2][:, 4 * g:4 * g + 4, :], tp[g][:, :, :], ACT.Copy).then_inc(turned_read, 1)
                if t:
                    square(t - 1)
                if t >= 2:
                    high(t - 2)
            square(NT - 1)
            high(NT - 2)
            high(NT - 1)

        @block.vector
        def _(dve):
            dve.memset(zeros[:, :], 0.0).then_inc(h2_lo, 1)
            dve.wait_ge(h2_lo, 1)
            z = zeros[:, :].rearrange("p (k n) -> p k n", k=KT)
            dve.tensor_copy(keep["h2h"][:, :, CTX:CTX + GAP], z)
            dve.tensor_copy(keep["h2l"][:, :, CTX:CTX + GAP], z)

            def modulate(t):
                v = 1 if t else 0
                for k in range(KT):
                    if k % 4 == 0:
                        if t:
                            dve.wait_ge(h2_lo, 2 * (t - 1) + k // 4 + 2)
                        dve.wait_ge(xn_turned, 2 * t + k // 4 + 1)
                    op = dve.tensor_scalar(h2[k // 4][:, k % 4, :], tp[2 + k // 4][:, k % 4, :],
                                           keep["gain"][:, 1, k, v:v + 1], keep["mod"][:, 3 * KT + k, v:v + 1], ALU.mult, ALU.add)
                    if k % 4 == 3:
                        op.then_inc(xn_read, 1)

            def low(t):
                for g in range(2):
                    dve.wait_ge(h2_hi, 2 * t + g + 1)
                    at = slice(column_of(t), column_of(t) + P)
                    dve.tensor_tensor(keep["h2l"][:, 4 * g:4 * g + 4, at], h2[g][:, :, :],
                                      keep["h2h"][:, 4 * g:4 * g + 4, at].bitcast(F32), ALU.subtract).then_inc(h2_lo, 1)

            for t in range(NT):
                j, v = t % 2, 1 if t else 0
                dve.wait_ge(t_in[t % 3], 32 * (t // 3 + 1))
                if t >= 2:
                    dve.wait_ge(x1_out[j], 16 * (t // 2))
                    dve.wait_ge(squares, t - 1)
                for b in range(2):
                    n, at = 2 * t + b, slice(b * BLK, (b + 1) * BLK)
                    dve.wait_ge(acc_done, n + 1)
                    dve.tensor_tensor(x1[j][:, at], acc[n % 4][:, :], keep["gate"][:, v, at], ALU.mult).then_inc(gated, 1)
                dve.wait_ge(gated, 2 * t + 2)
                dve.tensor_tensor(x1[j][:, :], x1[j][:, :], xt[t % 3][:, :], ALU.add).then_inc(x1_done, 1)
                if t >= 2:
                    low(t - 2)
                if t:
                    modulate(t - 1)
                dve.wait_ge(squares, t + 1)
                dve.tensor_scalar(stat[:, t, 1:2], stat[:, t, 0:1], 1.0 / D, EPS, ALU.mult, ALU.add).then_inc(mean_sq, 1)
                dve.wait_ge(rstd, t + 1)
                if t >= 2:
                    dve.wait_ge(xn_turned, 2 * t - 2)
                dve.tensor_scalar(xn[j][:, :], x1[j][:, :], stat[:, t, 1:2], None, ALU.mult).then_inc(xn_done, 1)
            low(NT - 2)
            modulate(NT - 1)
            low(NT - 1)


def mlp_up(nc, io, keep):
    with ExitStack() as ctx:
        def sb(name, shape, dt=F32):
            return ctx.enter_context(nc.sbuf_tensor(name, shape, dt))

        def ps(name, shape):
            return ctx.enter_context(nc.psum_tensor(name, shape, F32))

        def sem(name):
            return ctx.enter_context(nc.semaphore(name))

        w = [sb(f"up_w{j}", [P, KT, 2, P]) for j in range(2)]
        wh = [sb(f"up_wh{j}", [P, KT, 2, P], F32R) for j in range(2)]
        wl = [sb(f"up_wl{j}", [P, KT, 2, P], F32R) for j in range(2)]
        cw = sb("up_convw", [P, FT, 2, 3])
        cb = sb("up_convb", [P, FT, 2])
        u = [sb(f"up_u{j}", [P, TW + 2]) for j in range(2)]
        conv = [sb(f"up_conv{j}", [P, TW]) for j in range(2)]
        g = [sb(f"up_g{j}", [P, TW]) for j in range(2)]
        acc = [[ps(f"up_acc{i}_{c}", [P, BLK]) for c in range(3)] for i in range(2)]
        const_in = sem("up_const_in")
        w_in = [sem(f"up_w_in{j}") for j in range(2)]
        w_hi = sem("up_w_hi")
        w_lo = sem("up_w_lo")
        acc_done = sem("up_acc_done")
        acc_read = sem("up_acc_read")
        conv_done = sem("up_conv_done")
        silu_done = sem("up_silu_done")
        g_done = sem("up_g_done")
        g_out = [sem(f"up_g_out{j}") for j in range(2)]
        edges = sem("up_edges")
        vec_link = sem("up_vec_link")
        block = ctx.enter_context(nc.Block())
        h2h, h2l = keep["h2h"], keep["h2l"]

        @block.sync
        def _(sp):
            def load(f, j):
                sp.dma_start(w[j][:, :, :, :], io["w_up"][bass.ds(f, 1)].rearrange("a p k b n -> (a p) k b n")).then_inc(w_in[j], 16)

            def store(f, j):
                sp.wait_ge(g_done, f + 1)
                for t0, nt in ((0, 1), (1, NT - 1)):
                    at = column_of(t0)
                    sp.dma_start(io["g"][t0:t0 + nt, :, bass.ds(f, 1), :].rearrange("t p a n -> (a p) t n"),
                                 g[j][:, at:at + nt * P].rearrange("p (t n) -> p t n", n=P)).then_inc(g_out[j], 16)

            load(0, 0)
            load(1, 1)
            sp.dma_start(cw[:, :, :, :], io["convw"]).then_inc(const_in, 16)
            sp.dma_start(cb[:, :, :], io["convb"]).then_inc(const_in, 16)
            with sp.Fori(1, FT // 2) as v:
                for j in range(2):
                    f = v * 2 + j
                    sp.wait_ge(w_lo, f - 1)
                    load(f, j)
                    store(f - 2, j)
            for j in range(2):
                store(FT - 2 + j, j)
            for j in range(2):
                sp.wait_ge(g_out[j], 16 * FT)

        @block.tensor
        def _(pe):
            def tile(f, j, warm):
                pe.wait_ge(w_lo, f + 1)
                for i in range(2):
                    for c, (c0, cn) in enumerate(CUTS):
                        if warm:
                            pe.wait_ge(acc_read, 6 * f - 6 + 3 * i + c + 1)
                        for k in range(KT):
                            for part, (a, b) in enumerate(((wh, h2h), (wh, h2l), (wl, h2h))):
                                mm = pe.matmul(acc[i][c][:, 0:cn], a[j][:, k, i, :], b[:, k, c0:c0 + cn],
                                               start=(k == 0 and part == 0), stop=(k == KT - 1 and part == 2))
                        mm.then_inc(acc_done, 1)

            tile(0, 0, False)
            tile(1, 1, True)
            with pe.Fori(1, FT // 2) as v:
                for j in range(2):
                    tile(v * 2 + j, j, True)

        @block.scalar
        def _(act):
            act.wait_ge(edges, 1)

            def high(f, j, warm):
                act.wait_ge(w_in[j], f * 8 + 16 - 8 * j)
                if warm:
                    act.wait_ge(acc_done, 6 * f - 6)
                act.activation(wh[j][:, :, :, :], w[j][:, :, :, :], ACT.Copy).then_inc(w_hi, 1)

            def half_tile(f, i, warm):
                for c, (c0, cn) in enumerate(CUTS):
                    act.wait_ge(acc_done, 6 * f + 3 * i + c + 1)
                    if warm and c == 0:
                        act.wait_ge(conv_done, 2 * f - 1 + i)
                    act.activation(u[i][:, 1 + c0:1 + c0 + cn], acc[i][c][:, 0:cn], ACT.Copy).then_inc(acc_read, 1)

            def silu(f):
                act.wait_ge(conv_done, 2 * f + 1)
                act.activation(conv[0][:, :], conv[0][:, :], ACT.Silu).then_inc(silu_done, 1)

            def tile(f, j, warm, more):
                half_tile(f, 0, warm)
                if more:
                    high(f + 1, 1 - j, True)
                half_tile(f, 1, warm)
                silu(f)

            high(0, 0, False)
            high(1, 1, False)
            half_tile(0, 0, False)
            half_tile(0, 1, False)
            silu(0)
            with act.Fori(0, FT // 2 - 1) as v:
                for j in range(2):
                    f = v * 2 + 1 + j
                    tile(f, 1 - j, True, True)
            tile(FT - 1, 1, True, False)

        @block.vector
        def _(dve):
            for i in range(2):
                dve.memset(u[i][:, 0:1], 0.0)
                op = dve.memset(u[i][:, TW + 1:TW + 2], 0.0)
            op.then_inc(edges, 1)
            dve.wait_ge(const_in, 32)
            link = Links(dve, vec_link)
            PER = 4

            def low(f, j):
                dve.wait_ge(w_hi, f + 1)
                dve.tensor_tensor(wl[j][:, :, :, :], w[j][:, :, :, :], wh[j][:, :, :, :].bitcast(F32), ALU.subtract).then_inc(w_lo, 1)

            def tile(f, j, warm, more):
                link.start(PER * f)
                for i in range(2):
                    dve.wait_ge(acc_read, 6 * f + 3 * i + 3)
                    if warm:
                        dve.wait_ge(g_done, f)
                    at = bass.ds(f, 1)

                    def tap(n):
                        return cw[:, at, i, n:n + 1].rearrange("p a n -> p (a n)")

                    link.wait(dve.tensor_scalar(conv[i][:, :], u[i][:, 1:TW + 1], tap(1), cb[:, at, i], ALU.mult, ALU.add))
                    link.wait(dve.scalar_tensor_tensor(out=conv[i][:, :], in0=u[i][:, 0:TW], scalar=tap(0), in1=conv[i][:, :],
                                                       op0=ALU.mult, op1=ALU.add))
                    dve.scalar_tensor_tensor(out=conv[i][:, :], in0=u[i][:, 2:TW + 2], scalar=tap(2), in1=conv[i][:, :],
                                             op0=ALU.mult, op1=ALU.add).then_inc(conv_done, 1)
                    if i == 0 and more:
                        low(f + 1, 1 - j)
                assert link.k == PER
                dve.wait_ge(silu_done, f + 1)
                dve.wait_ge(conv_done, 2 * f + 2)
                if not isinstance(f, int) or f >= 2:
                    dve.wait_ge(g_out[j], 16 * (f - j))
                dve.tensor_tensor(g[j][:, :], conv[0][:, :], conv[1][:, :], ALU.mult).then_inc(g_done, 1)

            low(0, 0)
            low(1, 1)
            tile(0, 0, False, False)
            tile(1, 1, True, True)
            with dve.Fori(1, FT // 2 - 1) as v:
                for j in range(2):
                    tile(v * 2 + j, j, True, True)
            tile(FT - 2, 0, True, True)
            tile(FT - 1, 1, True, False)


def mlp_down(nc, io, keep):
    FS = 2
    PC = FT // FS
    with ExitStack() as ctx:
        def sb(name, shape, dt=F32):
            return ctx.enter_context(nc.sbuf_tensor(name, shape, dt))

        def sem(name):
            return ctx.enter_context(nc.semaphore(name))

        w = [sb(f"dn_w{j}", [P, FS, BLK]) for j in range(3)]
        wh = sb("dn_wh", [P, FT, BLK], F32R)
        wl = sb("dn_wl", [P, FT, BLK], F32R)
        g = [sb(f"dn_g{j}", [P, FT, P]) for j in range(2)]
        gh = [sb(f"dn_gh{j}", [P, FT, P], F32R) for j in range(2)]
        gl = [sb(f"dn_gl{j}", [P, FT, P], F32R) for j in range(2)]
        x1 = [sb(f"dn_x1{j}", [P, BLK]) for j in range(2)]
        tmp = sb("dn_tmp", [P, BLK])
        acc = [ctx.enter_context(nc.psum_tensor(f"dn_acc{j}", [P, BLK], F32)) for j in range(2)]
        gate_in = sem("dn_gate_in")
        w_in = [sem(f"dn_w_in{j}") for j in range(3)]
        g_in = [sem(f"dn_g_in{j}") for j in range(2)]
        w_hi = sem("dn_w_hi")
        w_lo = sem("dn_w_lo")
        g_hi = sem("dn_g_hi")
        g_lo = sem("dn_g_lo")
        multiplied = sem("dn_multiplied")
        gated = sem("dn_gated")
        added = sem("dn_added")
        x_in = [sem(f"dn_x_in{j}") for j in range(2)]
        y_out = [sem(f"dn_y_out{j}") for j in range(2)]
        block = ctx.enter_context(nc.Block())

        def units(eng, unit):
            for h in range(2):
                for t in range(3):
                    unit(h, t, (h + t) % 2, h == 1 or t == 2)
                with eng.Fori(1, NT // 2) as u:
                    for i in range(2):
                        unit(h, u * 2 + 1 + i, (h + 1 + i) % 2, True)

        def number(h, t):
            return t + NT * h

        def columns(h):
            return slice(h * BLK, (h + 1) * BLK)

        @block.sync
        def _(sp):
            def store(q, h, t, j):
                sp.wait_ge(added, q + 1)
                sp.dma_start(tile_rows(io["y"], t)[:, columns(h)], x1[j][:, :]).then_inc(y_out[j], 16)

            def unit(h, t, j, warm):
                q = number(h, t)
                if warm:
                    sp.wait_ge(g_lo, q - 1)
                sp.dma_start(g[j][:, :, :], io["g"][bass.ds(t, 1)].rearrange("a p f n -> (a p) f n")).then_inc(g_in[j], 16)
                if warm:
                    if isinstance(t, int) and t < 2:
                        store(q - 2, 0, NT - 2 + t, j)
                    else:
                        store(q - 2, h, t - 2, j)
                    sp.wait_ge(y_out[j], q * 8 - 8 * j)
                sp.dma_start(x1[j][:, :], tile_rows(io["x1"], t)[:, columns(h)]).then_inc(x_in[j], 16)

            units(sp, unit)
            for t in range(NT - 2, NT):
                store(NT + t, 1, t, (NT + t) % 2)
            for j in range(2):
                sp.wait_ge(y_out[j], 16 * NT)

        @block.gpsimd
        def _(pool):
            pool.dma_start(keep["gate"][:, :, :], io["gate2"]).then_inc(gate_in, 16)
            for r in range(2 * PC):
                i = r % PC
                if r >= 3:
                    pool.wait_ge(w_lo, r - 2)
                pool.dma_start(w[r % 3][:, :, :], io["w_down"][r // PC, :, FS * i:FS * i + FS]).then_inc(w_in[r % 3], 16)

        @block.tensor
        def _(pe):
            def unit(h, t, j, warm):
                q = number(h, t)
                pe.wait_ge(g_lo, q + 1)
                if warm:
                    pe.wait_ge(gated, q - 1)
                for f in range(FT):
                    if f % FS == 0 and isinstance(t, int) and t == 0:
                        pe.wait_ge(w_lo, PC * h + f // FS + 1)
                    for part, (a, b) in enumerate(((gh, wh), (gh, wl), (gl, wh))):
                        mm = pe.matmul(acc[j][:, :], a[j][:, f, :], b[:, f, :],
                                       start=(f == 0 and part == 0), stop=(f == FT - 1 and part == 2))
                    if f % FS == FS - 1:
                        mm.then_inc(multiplied, 1)

            units(pe, unit)

        @block.scalar
        def _(act):
            def high_w(h):
                for i in range(PC):
                    r = PC * h + i
                    act.wait_ge(w_in[r % 3], 16 * (r // 3 + 1))
                    if h:
                        act.wait_ge(multiplied, PC * (NT - 1) + i + 1)
                    act.activation(wh[:, FS * i:FS * i + FS, :], w[r % 3][:, :, :], ACT.Copy).then_inc(w_hi, 1)

            def unit(h, t, j, warm):
                q = number(h, t)
                act.wait_ge(g_in[j], q * 8 - 8 * j + 16)
                if warm:
                    act.wait_ge(multiplied, q * PC - PC)
                act.activation(gh[j][:, :, :], g[j][:, :, :], ACT.Copy).then_inc(g_hi, 1)
                if isinstance(t, int) and t == 0:
                    high_w(h)

            units(act, unit)

        @block.vector
        def _(dve):
            def low_w(h):
                for i in range(PC):
                    r = PC * h + i
                    dve.wait_ge(w_hi, r + 1)
                    at = slice(FS * i, FS * i + FS)
                    dve.tensor_tensor(wl[:, at, :], w[r % 3][:, :, :], wh[:, at, :].bitcast(F32), ALU.subtract).then_inc(w_lo, 1)

            def finish(q, h, v, j):
                if not isinstance(q, int) or q:
                    dve.wait_ge(added, q)
                dve.wait_ge(multiplied, q * PC + PC)
                dve.tensor_tensor(tmp[:, :], acc[j][:, :], keep["gate"][:, v, columns(h)], ALU.mult).then_inc(gated, 1)
                dve.wait_ge(gated, q + 1)
                dve.wait_ge(x_in[j], q * 8 - 8 * j + 16)
                dve.tensor_tensor(x1[j][:, :], x1[j][:, :], tmp[:, :], ALU.add).then_inc(added, 1)

            def unit(h, t, j, warm):
                q = number(h, t)
                dve.wait_ge(g_hi, q + 1)
                dve.tensor_tensor(gl[j][:, :, :], g[j][:, :, :], gh[j][:, :, :].bitcast(F32), ALU.subtract).then_inc(g_lo, 1)
                if isinstance(t, int) and t == 0:
                    low_w(h)
                if not isinstance(t, int) or t:
                    finish(q - 1, h, 0 if isinstance(t, int) and t == 1 else 1, 1 - j)
                elif h:
                    finish(q - 1, 0, 1, 1 - j)

            dve.wait_ge(gate_in, 16)
            units(dve, unit)
            finish(2 * NT - 1, 1, 1, 1)



def shape_constants():
    import numpy as np
    f = np.float32
    tri = np.tril(np.ones((P, P), bool))
    pos = np.arange(LAT)
    quarter = MD // 4
    freq = (10000.0 ** (-np.arange(quarter, dtype=f) / f(quarter))).astype(f)
    cos = np.ones((P, NT, 2, 2, quarter), f)
    sin = np.zeros((P, NT, 2, 2, quarter), f)
    for g, p in enumerate((pos // GRID_W, pos % GRID_W)):
        ang = (p.astype(f)[:, None] * freq[None, :]).reshape(NT - 1, P, quarter).transpose(1, 0, 2)
        for a in range(2):
            cos[:, 1:, g, a] = np.cos(ang)
            sin[:, 1:, g, a] = np.sin(ang) * (1 if a else -1)
    sel = np.zeros((2, 2, P), f)
    sel[0, 0] = sel[1, 1] = 1
    col = np.arange(GRID_W)
    cs = np.clip(col - 8, 0, GRID_W - 16)
    inside = (col[None, :] >= cs[:, None]) & (col[None, :] < cs[:, None] + 16)
    window = np.tile(np.where(inside, f(0), f(NEG)), (2, 1))
    rowmask = np.zeros((P, 9), f)
    rowmask[:GRID_W, 8] = NEG
    rowmask[GRID_W:, 0] = NEG
    return {"ident": np.eye(P, dtype=f), "flip": np.eye(P, dtype=f)[::-1].copy(),
            "cos": cos.reshape(P, NT, MD), "sin": sin.reshape(P, NT, MD), "sel": sel,
            "causal": np.stack([np.where(tri.T, f(0), f(NEG)), np.where(tri, f(0), f(NEG))], axis=1),
            "window": window, "rowmask": rowmask}


def lay_out(inp):
    import numpy as np
    a = {k: np.asarray(v) for k, v in inp.items()}
    w_in = a["w_in"][0].reshape(KT, P, -1).transpose(1, 0, 2)
    rep = lambda v: np.broadcast_to(v, (P,) + v.shape)
    toe = np.zeros((AH, 15, 127), np.float32)
    toe[:, :, 48:79] = a["rpb"][0]
    out = dict(shape_constants())
    out.update({
        "x": np.concatenate([a["x_prompt"][0], a["x_sample"][0]]).reshape(NT, P, D),
        "cT": np.stack([a["c_ctx"], a["c"][0]], -1).reshape(KT, P, 2).transpose(1, 0, 2),
        "w_mod": a["w_mod"][0].reshape(KT, P, MOD // BLK, BLK).transpose(2, 1, 0, 3),
        "b_mod2": np.broadcast_to(a["b_mod"], (2, MOD)),
        "gains": np.stack([a["norm1_g"][0].reshape(KT, P).T, a["norm2_g"][0].reshape(KT, P).T], 1),
        "w_in": w_in[:, :, :7 * BLK].reshape(P, KT, 7, BLK).transpose(2, 0, 1, 3),
        "w_gate": w_in[:, :, 7 * BLK:],
        "bg": rep(a["b_gate"][0]),
        "qkg": rep(np.stack([a["q_norm_g"][0], a["k_norm_g"][0]])),
        "ck": a["cache_k"][0, 0].reshape(P, AW), "cv": a["cache_v"][0, 0].reshape(P, AW),
        "toeplitz": toe.reshape(AH, 15 * 127),
        "stC": np.concatenate([a["state_C"][0, 0], a["state_n"][0, 0][..., None]], -1),
        "stm": a["state_m"][0, 0].reshape(1, 2 * MH),
        "mlg": rep(a["ml_norm_g"][0]),
        "w_out": a["w_out"][0].reshape(KT, P, D).transpose(1, 0, 2),
        "w_up": a["w_up"][0].reshape(KT, P, 2, FT, P).transpose(3, 1, 0, 2, 4),
        "convw": a["conv_w"][0].reshape(3, 2, FT, P).transpose(3, 2, 1, 0),
        "convb": a["conv_b"][0].reshape(2, FT, P).transpose(2, 1, 0),
        "w_down": a["w_down"][0].reshape(FT, P, 2, BLK).transpose(2, 1, 0, 3),
    })
    return out



_OUTS = {"y": (NT, P, D), "new_k": (P, AW), "new_v": (P, AW), "new_st": (2, MH, MD, MD + 1), "new_m": (2, MH)}
_SCRATCH = {"proj": (NT, P, 7 * BLK), "mix": (NT, P, MIX), "x1": (NT, P, D), "g": (NT, P, FT, P), "gate2": (P, 2, D), "mrows": (2, 2, 16, MH, P),
            "bias_rows": (AH, GRID_W, 15 * 127)}


def program(nc, io):
    with ExitStack() as ctx:
        def keeping(name, shape):
            keep[name] = ctx.enter_context(nc.sbuf_tensor("keep_" + name, shape, F32))

        keep = {}
        keeping("ident", [P, P])
        keeping("mod", [P, MOD // P, 2])
        keeping("gain", [P, 2, KT, 2])
        keeping("gate", [P, 2, D])
        keeping("gates", [P, NT, NG])
        modulation(nc, io, keep)
        projection(nc, io, keep)
        mlstm(nc, io, keep)
        attention(nc, io, keep)
        with ExitStack() as rows:
            for part in ("h2h", "h2l"):
                keep[part] = rows.enter_context(nc.sbuf_tensor("keep_" + part, [P, KT, TW], F32R))
            output_projection(nc, io, keep)
            mlp_up(nc, io, keep)
        mlp_down(nc, io, keep)


def kernel(**inputs):
    import numpy as _np
    import concourse.bacc as _bacc
    from concourse import mybir as _mybir
    from concourse.bass_utils import run_bass_kernel_spmd as _run

    nc = _bacc.Bacc("TRN2", target_bir_lowering=False, num_devices=1)
    arrays, io = {}, {}
    for name, a in lay_out(inputs).items():
        a = _np.ascontiguousarray(a)
        arrays[f"in_{name}"] = a
        io[name] = nc.dram_tensor(f"in_{name}", a.shape, _mybir.dt.from_np(a.dtype), kind="ExternalInput").ap()
    for name, shape in _OUTS.items():
        io[name] = nc.dram_tensor(f"out_{name}", shape, _mybir.dt.float32, kind="ExternalOutput").ap()
    for name, shape in _SCRATCH.items():
        io[name] = nc.dram_tensor(f"scratch_{name}", shape, _mybir.dt.float32, kind="Internal").ap()
    program(nc, io)
    got = _run(nc, [arrays], core_ids=[0]).results[0]
    y = got["out_y"].reshape(CTX + LAT, D)
    st = got["out_new_st"]
    return (y[None, :CTX], y[None, CTX:], got["out_new_k"].reshape(1, 1, CTX, AH, AD), got["out_new_v"].reshape(1, 1, CTX, AH, AD),
            st[None, None, ..., :MD], st[None, None, ..., MD], got["out_new_m"].reshape(1, 1, 2, MH))
```

```python
from contextlib import ExitStack

import concourse.bass as bass
from concourse import mybir

F32 = mybir.dt.float32
F32R = mybir.dt.float32r
ALU = mybir.AluOpType
ACT = mybir.ActivationFunctionType
AX = mybir.AxisListType

P = 128
D = 1024
KT = D // P
CTX = 128
LAT = 1024
NT = (CTX + LAT) // P
GRID_W = 64
AH, AD = 8, 64
AW = AH * AD
MH, MD = 4, 128
MW = MH * MD
NG = 4 * MH
MIX = AW + MW
PW = 3 * AW + 4 * MW
FF = 2816
FT = FF // P
EPS = 1e-6
NEG = -1e30
BLK = 512
AQ, AK, AV, MQ, MK, MV, MO = range(7)
MOD = 6 * D


class Links:

    def __init__(self, eng, sem):
        self.eng, self.sem, self.base, self.k = eng, sem, 0, 0

    def start(self, base):
        self.base, self.k = base, 0

    def tick(self, ins):
        ins.then_inc(self.sem, 1)
        self.k += 1
        return self.base + self.k

    def wait(self, ins):
        self.eng.wait_ge(self.sem, self.tick(ins))


def tile_rows(rows, t):
    return rows[bass.ds(t, 1)].rearrange("a p n -> (a p) n")


def modulation(nc, io, keep):
    NB = MOD // BLK
    GATES = [(r, v, h) for r in (5, 2) for v in range(2) for h in range(2)]
    with ExitStack() as ctx:
        def sb(name, shape):
            return ctx.enter_context(nc.sbuf_tensor(name, shape, F32))

        def ps(name, shape):
            return ctx.enter_context(nc.psum_tensor(name, shape, F32))

        def sem(name):
            return ctx.enter_context(nc.semaphore(name))

        ring = [sb(f"mod_w{j}", [P, KT, BLK]) for j in range(4)]
        cvec = sb("mod_c", [P, KT, 2])
        cexp = sb("mod_cexp", [P, KT, 2])
        csilu = sb("mod_csilu", [P, KT, 2])
        brow = sb("mod_bias", [2, MOD])
        row = sb("mod_row", [2, MOD])
        sel = sb("mod_sel", [2, 2, P])
        gains = sb("mod_gains", [P, 2, KT])
        gate2 = sb("mod_gate2", [P, 2, D])
        acc = [ps(f"mod_acc{j}", [P, BLK]) for j in range(4)]
        cols = ps("mod_cols", [P, BLK])
        gate = [ps(f"mod_gate{j}", [P, BLK]) for j in range(2)]
        small_in = sem("mod_small_in")
        w_in = [sem(f"mod_w_in{j}") for j in range(4)]
        c_exp = sem("mod_c_exp")
        c_silu = sem("mod_c_silu")
        acc_done = sem("mod_acc_done")
        row_done = sem("mod_row_done")
        cols_done = sem("mod_cols_done")
        gate_done = sem("mod_gate_done")
        gate_read = sem("mod_gate_read")
        gate_out = sem("mod_gate_out")
        vec_link = sem("mod_vec_link")
        block = ctx.enter_context(nc.Block())

        @block.sync
        def _(sp):
            sp.dma_start(cvec[:, :, :], io["cT"]).then_inc(small_in, 16)
            sp.dma_start(keep["ident"][:, :], io["ident"]).then_inc(small_in, 16)
            sp.dma_start(brow[:, :], io["b_mod2"]).then_inc(small_in, 16)
            sp.dma_start(sel[:, :, :], io["sel"]).then_inc(small_in, 16)
            sp.dma_start(gains[:, :, :], io["gains"]).then_inc(small_in, 16)

            def load(n, j):
                sp.dma_start(ring[j][:, :, :], io["w_mod"][n]).then_inc(w_in[j], 16)

            for j in range(4):
                load(j, j)
            with sp.Fori(1, NB // 4) as u:
                for j in range(4):
                    n = u * 4
                    sp.wait_ge(acc_done, n + j - 3)
                    load(n + j, j)
            sp.wait_ge(gate_read, 4)
            sp.dma_start(io["gate2"], gate2[:, :, :]).then_inc(gate_out, 16)
            sp.wait_ge(gate_out, 16)

        @block.gpsimd
        def _(pool):
            pool.memset(keep["half"][:, :], -0.5)

        @block.scalar
        def _(act):
            act.wait_ge(small_in, 80)
            act.activation(cexp[:, :, :], cvec[:, :, :], ACT.Exp, scale=-1.0).then_inc(c_exp, 1)

        @block.tensor
        def _(pe):
            pe.wait_ge(c_silu, 1)
            pe.wait_ge(small_in, 80)

            def mul(n, j, first):
                pe.wait_ge(w_in[j], n * 4 + 16 - 4 * j)
                if not first:
                    pe.wait_ge(row_done, n - 3)
                for k in range(KT):
                    mm = pe.matmul(acc[j][0:2, :], csilu[:, k, :], ring[j][:, k, :], start=(k == 0), stop=(k == KT - 1))
                mm.then_inc(acc_done, 1)

            for j in range(4):
                mul(j, j, True)
            with pe.Fori(1, NB // 4) as u:
                for j in range(4):
                    mul(u * 4 + j, j, False)
            pe.wait_ge(row_done, NB)
            for j in range(MOD // P):
                mm = pe.transpose(cols[:, 2 * j:2 * j + 2], row[:, j * P:(j + 1) * P], keep["ident"][0:2, 0:2])
            mm.then_inc(cols_done, 1)
            for i, (r, v, h) in enumerate(GATES):
                if i >= 2:
                    pe.wait_ge(gate_read, i - 1)
                pe.matmul(gate[h][:, :], sel[:, v, :], row[:, r * D + h * BLK:r * D + (h + 1) * BLK],
                          start=True, stop=True).then_inc(gate_done, 1)

        @block.vector
        def _(dve):
            link = Links(dve, vec_link)
            dve.wait_ge(c_exp, 1)
            link.wait(dve.tensor_scalar(cexp[:, :, :], cexp[:, :, :], 1.0, None, ALU.add))
            link.wait(dve.reciprocal(cexp[:, :, :], cexp[:, :, :]))
            dve.tensor_tensor(csilu[:, :, :], cvec[:, :, :], cexp[:, :, :], ALU.mult).then_inc(c_silu, 1)

            def add_bias(n, j):
                dve.wait_ge(acc_done, n + 1)
                at = bass.ds(n * BLK, BLK)
                dve.tensor_tensor(row[:, at], acc[j][0:2, :], brow[:, at], ALU.add).then_inc(row_done, 1)

            with dve.Fori(0, NB // 4) as u:
                for j in range(4):
                    add_bias(u * 4 + j, j)
            dve.wait_ge(cols_done, 1)
            link.wait(dve.tensor_copy(keep["mod"][:, :, :], cols[:, 0:2 * (MOD // P)].rearrange("p (j v) -> p j v", v=2)))
            for norm in range(2):
                sc = keep["mod"][:, (3 * norm + 1) * KT:(3 * norm + 2) * KT, :]
                link.wait(dve.tensor_scalar(keep["gain"][:, norm, :, :], sc, 1.0, None, ALU.add))
                for v in range(2):
                    dve.tensor_tensor(keep["gain"][:, norm, :, v], keep["gain"][:, norm, :, v], gains[:, norm, :], ALU.mult)
            for i, (r, v, h) in enumerate(GATES):
                dve.wait_ge(gate_done, i + 1)
                to = gate2 if r == 5 else keep["gate"]
                dve.tensor_copy(to[:, v, h * BLK:(h + 1) * BLK], gate[h][:, :]).then_inc(gate_read, 1)


def projection(nc, io, keep):
    ORDER = [AV, MV, MO, AQ, AK, MQ, MK]
    NB = len(ORDER)
    S = 3
    with ExitStack() as ctx:
        def sb(name, shape, dt=F32):
            return ctx.enter_context(nc.sbuf_tensor(name, shape, dt))

        def ps(name, shape):
            return ctx.enter_context(nc.psum_tensor(name, shape, F32))

        def sem(name):
            return ctx.enter_context(nc.semaphore(name))

        w = [sb(f"pj_w{i}", [P, BLK]) for i in range(S)]
        wh = [sb(f"pj_wh{j}", [P, KT, BLK], F32R) for j in range(2)]
        wl = [sb(f"pj_wl{j}", [P, KT, BLK], F32R) for j in range(2)]
        wg = sb("pj_wg", [P, KT, NG])
        wgh = sb("pj_wgh", [P, KT, NG], F32R)
        wgl = sb("pj_wgl", [P, KT, NG], F32R)
        hh = sb("pj_hh", [P, KT, NT * P], F32R)
        hl = sb("pj_hl", [P, KT, NT * P], F32R)
        xt = [sb(f"pj_x{j}", [P, D]) for j in range(2)]
        xn = sb("pj_xn", [P, D])
        h = [sb(f"pj_h{g}", [P, 4, P]) for g in range(2)]
        stat = sb("pj_stat", [P, NT, 2])
        out = [sb(f"pj_out{i}", [P, BLK]) for i in range(S)]
        raw = sb("pj_raw", [P, BLK])
        tmp = sb("pj_tmp", [P, BLK])
        hs = sb("pj_hs", [P, AH])
        half = keep["half"][:, 0:AH]
        qkg = sb("pj_qkg", [P, 2, AD])
        bg = sb("pj_bg", [P, NG])
        cos = sb("pj_cos", [P, NT, P])
        sin = sb("pj_sin", [P, NT, P])
        acc = [ps(f"pj_acc{i}", [P, BLK]) for i in range(S)]
        tp = [ps(f"pj_tp{g}", [P, 4, P]) for g in range(2)]
        junk = ps("pj_junk", [P, D])
        small_in = sem("pj_small_in")
        w_in = [sem(f"pj_w_in{i}") for i in range(S)]
        x_in = [sem(f"pj_x_in{j}") for j in range(2)]
        squares = sem("pj_squares")
        mean_sq = sem("pj_mean_sq")
        rstd = sem("pj_rstd")
        xn_done = sem("pj_xn_done")
        tp_done = sem("pj_tp_done")
        h_done = sem("pj_h_done")
        h_hi = sem("pj_h_hi")
        h_lo = sem("pj_h_lo")
        w_hi = sem("pj_w_hi")
        w_lo = sem("pj_w_lo")
        acc_done = sem("pj_acc_done")
        acc_read = sem("pj_acc_read")
        head_sq = sem("pj_head_sq")
        head_rstd = sem("pj_head_rstd")
        vec_out = sem("pj_vec_out")
        rows_out = [sem(f"pj_rows_out{i}") for i in range(S)]
        cache_out = sem("pj_cache_out")
        spread = sem("pj_spread")
        raw_read = sem("pj_raw_read")
        vec_link = sem("pj_vec_link")
        block = ctx.enter_context(nc.Block())

        def tiles(eng, unit):
            with eng.Fori(0, 2) as u:
                for i in range(S):
                    unit(u * S + i, i, u)
            for i in range(S):
                unit(2 * S + i, i, 2)

        @block.sync
        def _(sp):
            def load_x(t):
                sp.dma_start(xt[t % 2][:, :], tile_rows(io["x"], t)).then_inc(x_in[t % 2], 16)

            def load_w(m, k):
                r = KT * m + k
                if r >= S:
                    sp.wait_ge(w_lo, r - 1 if k == 0 or k == 1 else r - 2)
                sp.dma_start(w[k % S][:, :], io["w_in"][r]).then_inc(w_in[k % S], 16)

            load_x(0)
            for k in range(S):
                load_w(0, k)
            load_x(1)
            for k in range(S, KT):
                load_w(0, k)
            sp.dma_start(qkg[:, :, :], io["qkg"]).then_inc(small_in, 16)
            sp.dma_start(bg[:, :], io["bg"]).then_inc(small_in, 16)
            sp.dma_start(cos[:, :, :], io["cos"]).then_inc(small_in, 16)
            sp.dma_start(sin[:, :, :], io["sin"]).then_inc(small_in, 16)
            sp.dma_start(wg[:, :, :], io["w_gate"]).then_inc(small_in, 16)
            for k in range(KT):
                if k + 2 < NT:
                    sp.wait_ge(xn_done, k + 1)
                    load_x(k + 2)
                load_w(1, k)
            for a in range(AH):
                sp.dma_start(io["bias_rows"][a], io["toeplitz"][a:a + 1, :].to_broadcast([GRID_W, 15 * 127])).then_inc(spread, 16)
            for m in range(2, NB):
                for k in range(KT):
                    load_w(m, k)
            sp.wait_ge(spread, 16 * AH)

        @block.gpsimd
        def _(pool):
            def norm(t):
                pool.wait_ge(mean_sq, t + 1)
                pool.tensor_tensor(stat[:, t, 1:2], stat[:, t, 1:2], keep["half"][:, 0:1], ALU.pow).then_inc(rstd, 1)

            def store(m, t, i):
                at = ORDER[m] * BLK
                if m < 2:
                    pool.wait_ge(acc_read, t + NT * m + 1)
                else:
                    pool.wait_ge(vec_out, t + NT * (m - 2) + 1)
                pool.dma_start(tile_rows(io["proj"], t)[:, at:at + BLK], out[i][:, :]).then_inc(rows_out[i], 16)

            def cache(m, name, count):
                if m < 2:
                    pool.wait_ge(acc_read, NT * m + 1)
                else:
                    pool.wait_ge(vec_out, NT * (m - 2) + 1)
                pool.dma_start(io[name], out[0][:, :]).then_inc(cache_out, 16)
                pool.wait_ge(cache_out, count)

            def heads(m, t):
                pool.wait_ge(head_sq, t + NT * (m - 3) + 1)
                pool.tensor_tensor(hs[:, :], hs[:, :], half, ALU.pow).then_inc(head_rstd, 1)

            norm(0)
            norm(1)
            for t in range(NT):
                if t + 2 < NT:
                    norm(t + 2)
                if t == 0:
                    cache(0, "new_v", 16)
                store(0, t, t % S)
            for m in range(1, NB):
                n = ORDER[m]
                if n == AK:
                    for t in range(S):
                        heads(m, t)
                        if t == 0:
                            cache(m, "new_k", 32)
                        store(m, t, t)
                    with pool.Fori(1, 3) as u:
                        for i in range(S):
                            t = u * S + i
                            heads(m, t)
                            store(m, t, i)
                else:
                    with pool.Fori(0, 3) as u:
                        for i in range(S):
                            t = u * S + i
                            if n == AQ:
                                heads(m, t)
                            store(m, t, i)
            for i in range(S):
                pool.wait_ge(rows_out[i], 16 * S * NB)

        @block.scalar
        def _(act):
            def square(t):
                act.wait_ge(x_in[t % 2], 16 * (t // 2 + 1))
                if t:
                    act.wait_ge(squares, t)
                act.activation(junk[:, :], xt[t % 2][:, :], ACT.Square, accum_out=stat[:, t, 0:1]).then_inc(squares, 1)

            def high(t):
                for g in range(2):
                    act.wait_ge(h_done, 2 * t + g + 1)
                    act.activation(hh[:, 4 * g:4 * g + 4, t * P:(t + 1) * P], h[g][:, :, :], ACT.Copy).then_inc(h_hi, 1)

            def high_w(m, k, i, u):
                act.wait_ge(w_in[i], u * 16 + 16 * (m * (2 if i == 2 else 3) + 1))
                at = bass.ds(k, 1)
                act.activation(wh[m % 2][:, at, :].rearrange("p a n -> p (a n)"), w[i][:, :], ACT.Copy).then_inc(w_hi, 1)

            def evict(m, t, i, u):
                n = ORDER[m]
                act.wait_ge(acc_done, t + NT * m + 1)
                if n in (MQ, MK):
                    if m > 5 or not isinstance(t, int) or t > 0:
                        act.wait_ge(raw_read, t + NT * (m - 5))
                    act.activation(raw[:, :], acc[i][:, :], ACT.Copy, scale=1.0 if n == MQ else MD ** -0.5).then_inc(acc_read, 1)
                    return
                if not (m == 0 and isinstance(u, int) and u == 0):
                    act.wait_ge(rows_out[i], u * 16 + 16 * 3 * m)
                if n == MO:
                    act.activation(out[i][:, :], acc[i][:, :], ACT.Exp, scale=-1.0).then_inc(acc_read, 1)
                else:
                    act.activation(out[i][:, :], acc[i][:, :], ACT.Copy).then_inc(acc_read, 1)

            square(0)
            for k in range(4):
                high_w(0, k, k % S, k // S)
            square(1)
            high(0)
            for k in range(4, KT):
                high_w(0, k, k % S, k // S)
            for t in range(NT):
                if t + 1 < NT:
                    high(t + 1)
                if t + 2 < NT:
                    square(t + 2)
                if t < KT:
                    high_w(1, t, t % S, t // S)
                evict(0, t, t % S, t // S)
            for m in range(1, NB):
                def unit(t, i, u):
                    evict(m, t, i, u)
                    if m + 1 < NB and not (isinstance(t, int) and t == KT):
                        high_w(m + 1, t, i, u)

                if ORDER[m] == MQ:
                    for t in range(S):
                        unit(t, t, 0)
                    with act.Fori(1, 2) as u:
                        for i in range(S):
                            unit(u * S + i, i, u)
                    for i in range(S):
                        unit(2 * S + i, i, 2)
                else:
                    tiles(act, unit)

        @block.tensor
        def _(pe):
            def turn(t):
                pe.wait_ge(xn_done, t + 1)
                for g in range(2):
                    if t:
                        pe.wait_ge(h_done, 2 * t + g - 1)
                    for k in range(4):
                        at = (4 * g + k) * P
                        mm = pe.transpose(tp[g][:, k, :], xn[:, at:at + P], keep["ident"][:, :])
                    mm.then_inc(tp_done, 1)

            def unit(m, t, j):
                if not isinstance(m, int) or m or t >= S:
                    pe.wait_ge(acc_read, m * NT + t - 2)
                if isinstance(m, int) and m == 0:
                    pe.wait_ge(h_lo, 2 * t + 2)
                elif t == 0 and j is not None:
                    pe.wait_ge(w_lo, m * KT + KT)
                hi, lo = (wgh, wgl) if j is None else (wh[j], wl[j])
                cols = NG if j is None else BLK
                at = slice(t * P, (t + 1) * P)
                for k in range(KT):
                    if isinstance(m, int) and m == 0 and t == 0:
                        pe.wait_ge(w_lo, k + 1)
                    for part, (a, b) in enumerate(((hh, hi), (hh, lo), (hl, hi))):
                        mm = pe.matmul(acc[t % S][:, 0:cols], a[:, k, at], b[:, k, :],
                                       start=(k == 0 and part == 0), stop=(k == KT - 1 and part == 2))
                mm.then_inc(acc_done, 1)

            turn(0)
            turn(1)
            for t in range(NT):
                unit(0, t, 0)
                if t + 2 < NT:
                    turn(t + 2)
            with pe.Fori(0, (NB - 1) // 2) as u:
                for i in range(2):
                    for t in range(NT):
                        unit(u * 2 + 1 + i, t, 1 - i)
            for t in range(NT):
                unit(NB, t, None)

        @block.vector
        def _(dve):
            link = Links(dve, vec_link)

            def normalise(t):
                dve.wait_ge(squares, t + 1)
                dve.tensor_scalar(stat[:, t, 1:2], stat[:, t, 0:1], 1.0 / D, EPS, ALU.mult, ALU.add).then_inc(mean_sq, 1)
                dve.wait_ge(rstd, t + 1)
                if t:
                    dve.wait_ge(tp_done, 2 * t)
                dve.tensor_scalar(xn[:, :], xt[t % 2][:, :], stat[:, t, 1:2], None, ALU.mult).then_inc(xn_done, 1)

            def modulate(t):
                v = 1 if t else 0
                for g in range(2):
                    if t:
                        dve.wait_ge(h_lo, 2 * t + g - 1)
                    dve.wait_ge(tp_done, 2 * t + g + 1)
                    for k in range(4):
                        n = 4 * g + k
                        op = dve.tensor_scalar(h[g][:, k, :], tp[g][:, k, :], keep["gain"][:, 0, n, v:v + 1],
                                               keep["mod"][:, n, v:v + 1], ALU.mult, ALU.add)
                    op.then_inc(h_done, 1)
                for g in range(2):
                    dve.wait_ge(h_hi, 2 * t + g + 1)
                    at = slice(t * P, (t + 1) * P)
                    dve.tensor_tensor(hl[:, 4 * g:4 * g + 4, at], h[g][:, :, :], hh[:, 4 * g:4 * g + 4, at].bitcast(F32),
                                      ALU.subtract).then_inc(h_lo, 1)

            def low_w(m, k, i):
                dve.wait_ge(w_hi, k + KT * m + 1)
                at = bass.ds(k, 1)
                dve.tensor_tensor(wl[m % 2][:, at, :].rearrange("p a n -> p (a n)"), w[i][:, :],
                                  wh[m % 2][:, at, :].rearrange("p a n -> p (a n)").bitcast(F32), ALU.subtract).then_inc(w_lo, 1)

            def sigmoid(m, t, i, u):
                dve.wait_ge(acc_read, t + NT * m + 1)
                link.wait(dve.tensor_scalar(out[i][:, :], out[i][:, :], 1.0, None, ALU.add))
                dve.reciprocal(out[i][:, :], out[i][:, :]).then_inc(vec_out, 1)

            def heads(m, t, i, u):
                dve.wait_ge(acc_read, t + NT * m + 1)
                q = out[i][:, :]
                link.wait(dve.tensor_tensor(tmp[:, :], q, q, ALU.mult))
                link.wait(dve.tensor_reduce(hs[:, :], tmp[:, :].rearrange("p (h d) -> p h d", h=AH), AX.X, ALU.add))
                dve.tensor_scalar(hs[:, :], hs[:, :], 1.0 / AD, EPS, ALU.mult, ALU.add).then_inc(head_sq, 1)
                dve.wait_ge(head_rstd, t + NT * (m - 3) + 1)
                q = out[i][:, :].rearrange("p (h d) -> p h d", h=AH)
                link.wait(dve.tensor_tensor(q, q, hs[:, :].rearrange("p (h a) -> p h a", a=1).to_broadcast([P, AH, AD]), ALU.mult))
                g = ORDER[m]
                dve.tensor_tensor(q, q, qkg[:, g:g + 1, :].to_broadcast([P, AH, AD]), ALU.mult).then_inc(vec_out, 1)

            def rotary(m, t, i, u):
                dve.wait_ge(acc_read, t + NT * m + 1)
                dve.wait_ge(rows_out[i], u * 16 + 16 * 3 * m)
                dve.wait_ge(vec_out, t + NT * (m - 2))
                x = raw[:, :].rearrange("p (h d) -> p h d", h=MH)
                at = bass.ds(t, 1)
                dve.tensor_tensor(out[i][:, :].rearrange("p (h d) -> p h d", h=MH), x, cos[:, at, :].to_broadcast([P, MH, P]), ALU.mult)
                xs = raw[:, :].rearrange("p (h g a f) -> p h g a f", h=MH, g=2, a=2)
                ss = sin[:, at, :].rearrange("p t (g a f) -> p t g a f", g=2, a=2)
                ts = tmp[:, :].rearrange("p (h g a f) -> p h g a f", h=MH, g=2, a=2)
                for a in range(2):
                    for g in range(2):
                        op = dve.tensor_tensor(ts[:, :, g, a, :], xs[:, :, g, 1 - a, :],
                                               ss[:, :, g, a, :].to_broadcast([P, MH, 32]), ALU.mult)
                op.then_inc(raw_read, 1)
                dve.wait_ge(raw_read, t + NT * (m - 5) + 1)
                dve.tensor_tensor(out[i][:, :], out[i][:, :], tmp[:, :], ALU.add).then_inc(vec_out, 1)

            WORK = {AV: (None, 0), MV: (None, 0), MO: (sigmoid, 1), AQ: (heads, 3), AK: (heads, 3), MQ: (rotary, 0), MK: (rotary, 0)}
            normalise(0)
            for k in range(4):
                low_w(0, k, k % S)
            modulate(0)
            normalise(1)
            for k in range(4, KT):
                low_w(0, k, k % S)
            for t in range(NT):
                if t + 1 < NT:
                    modulate(t + 1)
                if t + 2 < NT:
                    normalise(t + 2)
                if t < KT:
                    low_w(1, t, t % S)
            dve.wait_ge(small_in, 80)
            link.wait(dve.tensor_copy(wgh[:, :, :], wg[:, :, :]))
            dve.tensor_tensor(wgl[:, :, :], wg[:, :, :], wgh[:, :, :].bitcast(F32), ALU.subtract)
            links = link.k
            for m in range(1, NB):
                work, per = WORK[ORDER[m]]

                def unit(t, i, u):
                    if work is not None:
                        link.start(t * per + links)
                        work(m, t, i, u)
                        assert link.k == per
                    if m + 1 < NB and not (isinstance(t, int) and t == KT):
                        low_w(m + 1, t, i)

                tiles(dve, unit)
                links += per * NT
            for t in range(NT):
                dve.wait_ge(acc_done, NT * NB + t + 1)
                dve.tensor_tensor(keep["gates"][:, t, :], acc[t % S][:, 0:NG], bg[:, :], ALU.add).then_inc(acc_read, 1)



def mlstm(nc, io, keep):
    L = P - 1
    HD = MD + 1
    with ExitStack() as ctx:
        def sb(name, shape):
            return ctx.enter_context(nc.sbuf_tensor(name, shape, F32))

        def ps(name, shape):
            return ctx.enter_context(nc.psum_tensor(name, shape, F32))

        def sem(name):
            return ctx.enter_context(nc.semaphore(name))

        causal = sb("ml_causal", [P, 2, P])
        gsrc = sb("ml_gsrc", [P, 2, P])
        lf = sb("ml_lf", [P, P])
        ones = sb("ml_ones", [P, P])
        zeros = sb("ml_zeros", [P, P])
        scan_in = sb("ml_scan_in", [P, 2, P])
        bsum = sb("ml_bsum", [P, P])
        asc = sb("ml_asc", [P, P])
        mloc = sb("ml_mloc", [P, P])
        nat = sb("ml_nat", [P, 3, P])
        rows = sb("ml_rows", [1, 4, P])
        stm = sb("ml_stm", [1, 2 * MH])
        m0 = sb("ml_m0", [P, 1])
        mb = sb("ml_mb", [P, P])
        absf = sb("ml_absf", [P, P])
        nml = sb("ml_nml", [P, 1])
        quant = sb("ml_quant", [P, 4, P])
        negm = sb("ml_negm", [P, P])
        decay = sb("ml_decay", [P, 1])
        ddiag = sb("ml_ddiag", [P, P])
        cols = sb("ml_cols", [P, 3, P])
        decays = sb("ml_decays", [P, P])
        mlg = sb("ml_gain", [P, MW])
        nat_in = [sb(f"ml_nat_in{j}", [P, 3, NT, MD]) for j in range(2)]
        v_in = [sb(f"ml_v_in{j}", [P, NT, HD]) for j in range(2)]
        bc_in = [sb(f"ml_bc_in{j}", [P, 2, 2, NT, P]) for j in range(2)]
        st = [sb(f"ml_st{j}", [P, 2, 2, HD]) for j in range(2)]
        qkT = sb("ml_qkT", [P, 2, NT, P])
        s_raw = sb("ml_s_raw", [P, NT, P])
        qTw = [sb(f"ml_qTw{j}", [P, 2, NT, P]) for j in range(2)]
        kw = [sb(f"ml_kw{j}", [P, 2, NT, MD]) for j in range(2)]
        st_ctx = [sb(f"ml_st_ctx{j}", [P, 2, HD]) for j in range(2)]
        den = sb("ml_den", [P, NT, 2])
        hid = [sb(f"ml_hid{j}", [P, 2, NT, MD]) for j in range(2)]
        sq = sb("ml_sq", [P, NT, MD])
        rs = sb("ml_rs", [P, NT])
        tq = [ps(f"ml_tq{j}", [P, 4, P]) for j in range(2)]
        num = [ps(f"ml_num{j}", [P, 2, HD]) for j in range(4)]
        upd = [ps(f"ml_upd{j}", [P, 2, HD]) for j in range(2)]

        const_in = sem("ml_const_in")
        gv = sem("ml_gate_vec")
        ga = sem("ml_gate_act")
        gp = sem("ml_gate_pe")
        rows_out = sem("ml_rows_out")
        m_out = sem("ml_m_out")
        consts = sem("ml_consts")
        qk_in = [sem(f"ml_qk_in{j}") for j in range(2)]
        rest_in = [sem(f"ml_rest_in{j}") for j in range(2)]
        bc_landed = [sem(f"ml_bc_landed{j}") for j in range(2)]
        turned = sem("ml_turned")
        turned_read = sem("ml_turned_read")
        shifted = sem("ml_shifted")
        masked = sem("ml_masked")
        weights = sem("ml_weights")
        scores = sem("ml_scores")
        keyw = sem("ml_keyw")
        qw = sem("ml_qw")
        upd_done = sem("ml_upd_done")
        st_new = sem("ml_st_new")
        num_done = sem("ml_num_done")
        den_done = sem("ml_den_done")
        num_read = sem("ml_num_read")
        added = sem("ml_added")
        squared = sem("ml_squared")
        mean_sq = sem("ml_mean_sq")
        rstd = sem("ml_rstd")
        scaled = sem("ml_scaled")
        gated = sem("ml_gated")
        head_out = [sem(f"ml_head_out{j}") for j in range(2)]
        state_out = [sem(f"ml_state_out{j}") for j in range(2)]
        vec_link = sem("ml_vec_link")
        block = ctx.enter_context(nc.Block())

        ident = keep["ident"]
        UPDATES = NT - 1
        GROUPS = [(i, t) for i in range(3) for t in range(0, NT, 4)]

        def tiles_of(s):
            return (s, NT - s if s else 0)

        def row_of(r, t, h):
            return 64 * r + MH * t + h

        @block.sync
        def _(sp):
            sp.dma_start(causal[:, :, :], io["causal"]).then_inc(const_in, 16)
            sp.dma_start(stm[:, :], io["stm"]).then_inc(const_in, 16)
            sp.dma_start(mlg[:, :], io["mlg"]).then_inc(const_in, 16)

            def load_tiles(to, b, h):
                at = b * BLK + h * MD
                return sp.dma_start(to, io["proj"][:, :, at:at + MD].rearrange("t p d -> p t d"))

            def load_qk(h, j):
                load_tiles(nat_in[j][:, 0, :, :], MQ, h).then_inc(qk_in[j], 16)
                load_tiles(nat_in[j][:, 1, :, :], MK, h).then_inc(qk_in[j], 16)

            def load_rest(h, j):
                load_tiles(nat_in[j][:, 2, :, :], MO, h).then_inc(rest_in[j], 16)
                load_tiles(v_in[j][:, :, 0:MD], MV, h).then_inc(rest_in[j], 16)
                sp.dma_start(st[j][:, 0, :, :], io["stC"][:, h].rearrange("r d e -> d r e")).then_inc(rest_in[j], 16)

            def load_bc(h, j):
                for k in range(2):
                    for r in range(2):
                        src = io["mrows"][k:k + 1, r, 0:NT, h, :].to_broadcast([P, NT, P])
                        sp.dma_start(bc_in[j][:, k, r, :, :], src).then_inc(bc_landed[j], 16)

            load_qk(0, 0)
            load_rest(0, 0)
            sp.wait_ge(ga, 6)
            sp.wait_ge(gv, 4)
            sp.dma_start(io["mrows"][0].rearrange("r t h n -> (r t h) n"), negm[:, :]).then_inc(rows_out, 16)
            sp.dma_start(io["mrows"][1].rearrange("r t h n -> (r t h) n"), quant[:, 3, :]).then_inc(rows_out, 16)
            for r in range(2):
                sp.dma_start(io["new_m"][r:r + 1, :], rows[:, 2, 64 * r:64 * r + MH]).then_inc(m_out, 16)
            sp.wait_ge(rows_out, 32)
            load_bc(0, 0)
            load_qk(1, 1)
            load_bc(1, 1)
            load_rest(1, 1)
            for h in range(2, MH):
                j = h % 2
                sp.wait_ge(keyw, h - 1)
                sp.wait_ge(turned, len(GROUPS) * (h - 2) + 6)
                load_qk(h, j)
                sp.wait_ge(num_done, NT * (h - 1))
                load_bc(h, j)
                sp.wait_ge(head_out[j], 16 * (h // 2))
                load_rest(h, j)
            sp.wait_ge(m_out, 32)

        @block.tensor
        def _(pe):
            pe.wait_ge(gv, 1)
            pe.transpose(tq[0][:, 0, :], gsrc[:, 0, :], ident[:, :])
            pe.transpose(tq[0][:, 1, :], lf[:, :], ident[:, :]).then_inc(gp, 1)
            pe.wait_ge(gv, 2)
            pe.matmul(tq[1][0:1, 0, :], bsum[:, L:P], ident[:, :], start=True, stop=True)
            pe.matmul(tq[1][0:1, 1, :], mloc[:, L:P], ident[:, :], start=True, stop=True).then_inc(gp, 1)
            pe.wait_ge(gv, 3)
            pe.matmul(tq[0][:, 0, 0:1], rows[:, 3, :], ident[0:1, 0:1], start=True, stop=True).then_inc(gp, 1)
            pe.wait_ge(gv, 5)
            pe.wait_ge(ga, 6)
            for i in range(3):
                pe.transpose(tq[1][:, i, :], quant[:, i, :], ident[:, :])
            pe.matmul(tq[0][:, 0, :], ones[:, :], ddiag[:, :], start=True, stop=True).then_inc(gp, 1)
            pe.wait_ge(gv, 6)

            def group(h, g):
                j, (i, t0) = h % 2, GROUPS[g]
                n = len(GROUPS) * h + g
                if g == 0:
                    pe.wait_ge(qk_in[j], 32 * (h // 2 + 1))
                if n >= 2:
                    pe.wait_ge(turned_read, n - 1)
                if i == 2:
                    pe.wait_ge(turned_read, len(GROUPS) * h + 6)
                for t in range(t0, min(t0 + 4, NT)):
                    if i < 2:
                        mm = pe.transpose(tq[n % 2][:, t - t0, :], nat_in[j][:, i, t, :], ident[:, :])
                    else:
                        mm = pe.matmul(tq[n % 2][:, t - t0, :], qkT[:, 1, t, :], qkT[:, 0, t, :], start=True, stop=True)
                mm.then_inc(turned, 1)

            def step(h, s):
                j = h % 2
                if s == 0:
                    pe.wait_ge(rest_in[j], 48 * (h // 2 + 1))
                    pe.wait_ge(keyw, h + 1)
                if s < UPDATES:
                    u = UPDATES * h + s
                    if u >= 2:
                        pe.wait_ge(st_new, u - 1)
                    for r, t in enumerate(tiles_of(s)):
                        mm = pe.matmul(upd[s % 2][:, r, :], kw[j][:, r, t, :], v_in[j][:, t, :], start=True, stop=True)
                    mm.then_inc(upd_done, 1)
                if s == 0:
                    pe.wait_ge(scores, h + 1)
                    pe.wait_ge(qw, h + 1)
                n = NT * h + s
                if n >= 4:
                    pe.wait_ge(num_read, n - 3)
                if s > 1:
                    pe.wait_ge(st_new, UPDATES * h + s)
                for r, t in enumerate(tiles_of(s)):
                    mm = pe.matmul(num[n % 4][:, r, :], bc_in[j][:, 0, r, t, :], v_in[j][:, t, :], start=True, stop=(s == 0))
                    if s:
                        mm = pe.matmul(num[n % 4][:, r, :], qTw[j][:, r, t, :], st[j][:, (s - 1) % 2, r, :], start=False, stop=True)
                mm.then_inc(num_done, 1)

            for g in range(len(GROUPS)):
                group(0, g)
            for h in range(MH):
                for s in range(NT):
                    step(h, s)
                    if h + 1 < MH:
                        group(h + 1, s)

        @block.scalar
        def _(act):
            act.wait_ge(consts, 1)
            act.activation(lf[:, :], absf[:, :], ACT.Exp, scale=-1.0).then_inc(ga, 1)
            act.wait_ge(ga, 1)
            act.activation(lf[:, :], lf[:, :], ACT.Ln, bias=1.0).then_inc(ga, 1)
            act.wait_ge(gv, 4)
            act.activation(quant[:, 1, :], nat[:, 0, :], ACT.Exp, bias=nml[:, 0:1]).then_inc(ga, 1)
            act.activation(quant[:, 2, :], mb[:, :], ACT.Exp, scale=-1.0).then_inc(ga, 1)
            act.activation(quant[:, 3, :], nat[:, 1, :], ACT.Exp, scale=-1.0, bias=m0[:, 0:1]).then_inc(ga, 1)
            act.activation(decay[:, :], m0[:, :], ACT.Exp, bias=nml[:, 0:1]).then_inc(ga, 1)
            def take(h, g):
                i, t0 = GROUPS[g]
                n = len(GROUPS) * h + g
                nt = min(4, NT - t0)
                act.wait_ge(turned, n + 1)
                if h and g == 0:
                    act.wait_ge(qw, h)
                if h and g == 6:
                    act.wait_ge(scores, h)
                dst = s_raw[:, t0:t0 + nt, :] if i == 2 else qkT[:, i, t0:t0 + nt, :]
                act.activation(dst, tq[n % 2][:, 0:nt, :], ACT.Copy).then_inc(turned_read, 1)

            def exps(h):
                act.wait_ge(masked, h + 1)
                w = bc_in[h % 2][:, 0, :, :, :]
                act.activation(w, w, ACT.Exp).then_inc(weights, 1)

            def square(h):
                act.wait_ge(added, h + 1)
                act.activation(sq[:, :, :], hid[h % 2][:, 0, :, :], ACT.Square).then_inc(squared, 1)

            def step(h, s):
                j, n = h % 2, NT * h + s
                if h >= 2 and s == 0:
                    act.wait_ge(head_out[j], 16 * (h // 2))
                act.wait_ge(den_done, n + 1)
                for r, t in enumerate(tiles_of(s)):
                    op = act.activation(hid[j][:, r, t, :], num[n % 4][:, r, 0:MD], ACT.Copy, scale=den[:, s, r:r + 1])
                op.then_inc(num_read, 1)

            for g in range(len(GROUPS)):
                take(0, g)
            exps(0)
            for h in range(MH):
                for s in range(NT):
                    step(h, s)
                    if h and s == 1:
                        square(h - 1)
                    if h + 1 < MH:
                        take(h + 1, s)
                if h + 1 < MH:
                    exps(h + 1)
            square(MH - 1)

        @block.gpsimd
        def _(pool):
            pool.wait_ge(const_in, 48)

            def mask(h):
                pool.wait_ge(shifted, h + 1)
                for r in range(2):
                    w = bc_in[h % 2][:, 0, r, :, :]
                    op = pool.tensor_tensor(w, w, causal[:, r:r + 1, :].to_broadcast([P, NT, P]), ALU.add)
                op.then_inc(masked, 1)

            def finish(h):
                j, last = h % 2, h == MH - 1
                if not last:
                    pool.wait_ge(num_read, NT * (h + 1))
                    pool.tensor_tensor(hid[j][:, 0, :, :], hid[j][:, 0, :, :], hid[j][:, 1, :, :], ALU.add).then_inc(added, 1)
                pool.wait_ge(mean_sq, h + 1)
                pool.tensor_tensor(rs[:, :], rs[:, :], keep["half"][:, :], ALU.pow).then_inc(rstd, 1)
                if not last:
                    pool.wait_ge(scaled, h + 1)
                    pool.tensor_tensor(hid[j][:, 0, :, :], hid[j][:, 0, :, :], nat_in[j][:, 2, :, :], ALU.mult).then_inc(gated, 1)
                pool.wait_ge(gated, h + 1)
                at = AW + h * MD
                pool.dma_start(io["mix"][:, :, at:at + MD].rearrange("t p d -> p t d"), hid[j][:, 0, :, :]).then_inc(head_out[j], 16)
                pool.wait_ge(st_new, UPDATES * h + 1)
                pool.dma_start(io["new_st"][:, h].rearrange("r d e -> d r e"), st_ctx[j][:, :, :]).then_inc(state_out[j], 16)

            mask(0)
            for h in range(MH):
                if h:
                    finish(h - 1)
                if h + 1 < MH:
                    mask(h + 1)
            finish(MH - 1)
            for j in range(2):
                pool.wait_ge(head_out[j], 16 * MH // 2)
                pool.wait_ge(state_out[j], 16 * MH // 2)

        @block.vector
        def _(dve):
            link = Links(dve, vec_link)
            dve.wait_ge(const_in, 48)
            for x in (gsrc, zeros, rows):
                dve.memset(x[:], 0.0)
            for j in range(2):
                dve.memset(v_in[j][:, :, MD:HD], 1.0)
            link.wait(dve.memset(ones[:, :], 1.0))
            for r in range(2):
                for i in range(2):
                    op = dve.tensor_copy(gsrc[:, i, 64 * r:64 * r + NT * MH].rearrange("p (t h) -> p t h", h=MH),
                                         keep["gates"][:, :, 8 * r + 4 * i:8 * r + 4 * i + 4])
            link.wait(op)
            f = gsrc[:, 1, :]
            link.wait(dve.tensor_scalar(absf[:, :], f, -1.0, None, ALU.mult))
            dve.tensor_tensor(absf[:, :], absf[:, :], f, ALU.max).then_inc(consts, 1)
            dve.wait_ge(ga, 2)
            dve.scalar_tensor_tensor(out=lf[:, :], in0=f, scalar=0.0, in1=lf[:, :], op0=ALU.min, op1=ALU.subtract).then_inc(gv, 1)
            dve.wait_ge(gp, 1)
            dve.tensor_copy(scan_in[0:64, :, :], tq[0][0:64, 0:2, :])
            link.wait(dve.tensor_copy(scan_in[64:P, :, :], tq[0][64:P, 0:2, ::-1]))
            link.wait(dve.tensor_tensor_scan(bsum[:, :], scan_in[:, 1, :], zeros[:, :], 0.0, ALU.add, ALU.add))
            link.wait(dve.tensor_tensor(asc[:, :], scan_in[:, 0, :], bsum[:, :], ALU.subtract))
            dve.tensor_tensor_scan(mloc[:, :], asc[:, :], asc[:, :], -3e38, ALU.max, ALU.max).then_inc(gv, 1)
            dve.wait_ge(gp, 2)
            link.wait(dve.tensor_copy(rows[:, 0:2, :], tq[1][0:1, 0:2, :]))
            for r in range(2):
                for h in range(MH):
                    a = 64 * r + MH + h
                    cut = slice(a, a + MH * 7 + 1, MH) if r == 0 else slice(a + MH * 7, a - 1, -MH)
                    dve.tensor_tensor_scan(rows[:, 2, cut], rows[:, 1, cut], rows[:, 0, cut], stm[:, MH * r + h:MH * r + h + 1],
                                           ALU.max, ALU.add)
                c = slice(64 * r, 64 * r + MH)
                op = dve.scalar_tensor_tensor(out=rows[:, 2, c], in0=rows[:, 1, c], scalar=0.0, in1=rows[:, 0, c],
                                              op0=ALU.max, op1=ALU.add)
            link.wait(op)
            dve.tensor_copy(rows[:, 3, 8:36], rows[:, 2, 4:32])
            dve.tensor_copy(rows[:, 3, 68:96], rows[:, 2, 72:100])
            dve.tensor_copy(rows[:, 3, 4:8], stm[:, 0:MH])
            dve.tensor_copy(rows[:, 3, 96:100], stm[:, MH:2 * MH]).then_inc(gv, 1)
            dve.wait_ge(gp, 3)
            link.wait(dve.tensor_copy(m0[:, :], tq[0][:, 0, 0:1]))
            link.wait(dve.tensor_scalar(mloc[:, :], mloc[:, :], m0[:, 0:1], None, ALU.max))
            dve.tensor_scalar(nml[:, :], mloc[:, L:P], -1.0, None, ALU.mult)
            for i, x in enumerate((asc, mloc, bsum)):
                dve.tensor_copy(nat[0:64, i, :], x[0:64, :])
                op = dve.tensor_copy(nat[64:P, i, :], x[64:P, ::-1])
            link.wait(op)
            dve.tensor_tensor(mb[:, :], nat[:, 1, :], nat[:, 2, :], ALU.add)
            dve.tensor_scalar(negm[:, :], nat[:, 1, :], -1.0, None, ALU.mult).then_inc(gv, 1)
            dve.tensor_copy(quant[:, 0, :], nat[:, 0, :])
            dve.wait_ge(ga, 6)
            dve.tensor_scalar(ddiag[:, :], ident[:, :], decay[:, 0:1], None, ALU.mult).then_inc(gv, 1)
            dve.wait_ge(gp, 4)
            dve.tensor_copy(cols[:, :, :], tq[1][:, 0:3, :])
            dve.tensor_copy(decays[:, :], tq[0][:, 0, :]).then_inc(gv, 1)
            dve.wait_ge(gv, 6)

            def by_tile(i, h, n):
                c = cols[:, i, :].rearrange("p (r t h) -> p r t h", r=2, h=MH)[:, :, 0:NT, h:h + 1]
                return c.to_broadcast([P, 2, NT, n])

            def shift(h):
                dve.wait_ge(bc_landed[h % 2], 64 * (h // 2 + 1))
                w = bc_in[h % 2][:, 0, :, :, :]
                dve.tensor_tensor(w, w, by_tile(0, h, P), ALU.add).then_inc(shifted, 1)

            def keys(h, r):
                j = h % 2
                if r == 0:
                    dve.wait_ge(qk_in[j], 32 * (h // 2 + 1))
                    if h >= 2:
                        dve.wait_ge(upd_done, UPDATES * (h - 1))
                c = cols[:, 1, :].rearrange("p (r t h) -> p r t h", r=2, h=MH)[:, r, 0:NT, h:h + 1]
                op = dve.tensor_tensor(kw[j][:, r, :, :], nat_in[j][:, 1, :, :], c.to_broadcast([P, NT, MD]), ALU.mult)
                if r:
                    op.then_inc(keyw, 1)

            def queries(h, r):
                j = h % 2
                if r == 0:
                    dve.wait_ge(turned_read, len(GROUPS) * h + 3)
                    if h >= 2:
                        dve.wait_ge(num_done, NT * (h - 1))
                op = dve.tensor_tensor(qTw[j][:, r, :, :], qkT[:, 0, :, :], bc_in[j][:, 1, r, :, :], ALU.mult)
                if r:
                    op.then_inc(qw, 1)

            def weigh(h):
                dve.wait_ge(turned_read, len(GROUPS) * (h + 1))
                dve.wait_ge(weights, h + 1)
                for r in range(2):
                    w = bc_in[h % 2][:, 0, r, :, :]
                    op = dve.tensor_tensor(w, w, s_raw[:, :, :], ALU.mult)
                op.then_inc(scores, 1)

            def step(h, s):
                j, n = h % 2, NT * h + s
                if s < UPDATES:
                    dve.wait_ge(upd_done, UPDATES * h + s + 1)
                    if s == 0:
                        if h >= 2:
                            dve.wait_ge(state_out[j], 16 * (h // 2))
                        dve.tensor_copy(st_ctx[j][:, :, :], upd[0][:, :, :]).then_inc(st_new, 1)
                    else:
                        if s > 1:
                            dve.wait_ge(num_done, n)
                        dve.wait_ge(st_new, UPDATES * h + s)
                        for r, t in enumerate(tiles_of(s)):
                            c = row_of(r, t, h)
                            op = dve.scalar_tensor_tensor(out=st[j][:, s % 2, r, :], in0=st[j][:, (s - 1) % 2, r, :],
                                                          scalar=decays[:, c:c + 1], in1=upd[s % 2][:, r, :],
                                                          op0=ALU.mult, op1=ALU.add)
                        op.then_inc(st_new, 1)
                dve.wait_ge(num_done, n + 1)
                if s == 0 and h:
                    dve.wait_ge(num_read, n)
                for r, t in enumerate(tiles_of(s)):
                    c = row_of(r, t, h)
                    op = dve.tensor_scalar(den[:, s, r:r + 1], num[n % 4][:, r, MD:HD], -1.0, cols[:, 2, c:c + 1],
                                           ALU.mult, ALU.max)
                link.wait(op)
                link.wait(dve.tensor_tensor(den[:, s, :], den[:, s, :], num[n % 4][:, :, MD], ALU.max))
                dve.reciprocal(den[:, s, :], den[:, s, :]).then_inc(den_done, 1)

            def mean_square(h):
                dve.wait_ge(squared, h + 1)
                link.wait(dve.tensor_reduce(rs[:, :], sq[:, :, :], AX.X, ALU.add))
                dve.tensor_scalar(rs[:, :], rs[:, :], 1.0 / MD, EPS, ALU.mult, ALU.add).then_inc(mean_sq, 1)

            def normalise(h):
                dve.wait_ge(rstd, h + 1)
                y = hid[h % 2][:, 0, :, :]
                link.wait(dve.tensor_tensor(y, y, rs[:, :].rearrange("p (t a) -> p t a", a=1).to_broadcast([P, NT, MD]), ALU.mult))
                dve.tensor_tensor(y, y, mlg[:, h * MD:(h + 1) * MD].rearrange("p (a d) -> p a d", a=1).to_broadcast([P, NT, MD]),
                                  ALU.mult).then_inc(scaled, 1)

            shift(0)
            keys(0, 0)
            keys(0, 1)
            queries(0, 0)
            queries(0, 1)
            weigh(0)
            for h in range(MH):
                for s in range(NT):
                    step(h, s)
                    if h and s == 2:
                        mean_square(h - 1)
                    if h and s == 3:
                        normalise(h - 1)
                    if h + 1 < MH:
                        if s == 0 and h == 0 or s == 4 and h:
                            shift(h + 1)
                        if s in (1, 2):
                            keys(h + 1, s - 1)
                        if s in (5, 6):
                            queries(h + 1, s - 5)
                if h + 1 < MH:
                    weigh(h + 1)
            y, back, gate = hid[(MH - 1) % 2][:, 0, :, :], hid[(MH - 1) % 2][:, 1, :, :], nat_in[(MH - 1) % 2][:, 2, :, :]
            dve.wait_ge(num_read, NT * MH)
            dve.tensor_tensor(y, y, back, ALU.add).then_inc(added, 1)
            mean_square(MH - 1)
            normalise(MH - 1)
            dve.wait_ge(scaled, MH)
            dve.tensor_tensor(y, y, gate, ALU.mult).then_inc(gated, 1)



def attention(nc, io, keep):
    SCALE = AD ** -0.5
    WR = 8
    JR = 14
    HP = AH // 2
    LT = NT - 1
    WINDOWS = []
    for i in range(LT):
        first = [min(max(r - WR // 2, 0), LAT // GRID_W - WR) for r in (2 * i, 2 * i + 1)]
        WINDOWS.append((first[0], first[1] + WR - first[0], first[0] - 2 * i + 7 - 1, first[1] != first[0]))
    with ExitStack() as ctx:
        def sb(name, shape):
            return ctx.enter_context(nc.sbuf_tensor(name, shape, F32))

        def ps(name, shape):
            return ctx.enter_context(nc.psum_tensor(name, shape, F32))

        def sem(name):
            return ctx.enter_context(nc.semaphore(name))

        qk_nat = keep["space"][:, :].rearrange("p (t b n) -> p t b n", b=2, n=AW)
        w_out = keep["space"][:, 0:KT * D].rearrange("p (k n) -> p k n", k=KT)
        v_nat = sb("at_v_nat", [P, NT + 1, AW])
        qT = sb("at_qT", [P, 2, HP, NT, P])
        kT = sb("at_kT", [P, HP, NT + 1, P])
        window = sb("at_window", [P, GRID_W])
        rowmask = sb("at_rowmask", [P, WR + 1])
        zeros = sb("at_zeros", [P, P])
        table = [sb(f"at_table{j}", [P, JR, GRID_W]) for j in range(2)]
        inner = [sb(f"at_inner{j}", [P, WR + 1, GRID_W]) for j in range(2)]
        prob = [sb(f"at_prob{j}", [P, 11 * GRID_W]) for j in range(3)]
        probT = [sb(f"at_probT{j}", [P, 6, P]) for j in range(2)]
        low = sb("at_low", [P, 9 * AH, 2])
        total = sb("at_total", [P, 9 * AH])
        heads = [sb(f"at_heads{j}", [P, LT, 2, AD]) for j in range(2)]
        first_rows = sb("at_first_rows", [P, AH, AD])
        score = [ps(f"at_score{j}", [P, 2 * BLK]) for j in range(2)]
        turn = [ps(f"at_turn{j}", [P, 4, P]) for j in range(2)]
        outp = [ps(f"at_out{j}", [P, 8, AD]) for j in range(2)]

        const_in = sem("at_const_in")
        tile_in = [sem(f"at_tile_in{j}") for j in range((NT + 1) // 2)]
        table_in = [sem(f"at_table_in{j}") for j in range(2)]
        table_ready = sem("at_table_ready")
        laid = sem("at_laid")
        laid_vec = sem("at_laid_vec")
        laid_act = sem("at_laid_act")
        scored = sem("at_scored")
        biased = sem("at_biased")
        expd = sem("at_expd")
        turned = [sem(f"at_turned{j}") for j in range(2)]
        taken = [sem(f"at_taken{j}") for j in range(2)]
        summed = sem("at_summed")
        scaled = sem("at_scaled")
        out_free = sem("at_out_free")
        pair_out = [sem(f"at_pair_out{j}") for j in range(2)]
        first_out = sem("at_first_out")
        w_out_in = sem("at_w_out_in")
        vec_link = sem("at_vec_link")
        pool_link = sem("at_pool_link")
        block = ctx.enter_context(nc.Block())

        units = []
        for h in range(AH):
            units.append((h, 0))
        for h in range(AH):
            for i in range(LT):
                units.append((h, i + 1))
        N = len(units)

        def local_cols(t):
            return GRID_W * WINDOWS[t - 1][1] if t else 0

        def pieces(h, t):
            if t == 0:
                return [(0, P, kT[:, h // 2, 0, :])]
            u0, nr, _, _ = WINDOWS[t - 1]
            keys = kT[:, h // 2, 1:, :].rearrange("p t n -> p (t n)")
            out = [(0, BLK, keys[:, GRID_W * u0:GRID_W * u0 + BLK])]
            n = GRID_W * nr
            if n > BLK:
                out.append((BLK, n - BLK, keys[:, GRID_W * u0 + BLK:GRID_W * u0 + n]))
            return out + [(n, P, kT[:, h // 2, NT, :])]

        def blocks(h, t):
            cols = slice(AD * h, AD * h + AD)
            if t == 0:
                return [(0, P, v_nat[:, 0, cols])]
            u0, nr, _, _ = WINDOWS[t - 1]
            n, out = GRID_W * nr, []
            for c in range(0, n, P):
                k = min(P, n - c)
                out.append((c, k, v_nat[0:k, 1 + (GRID_W * u0 + c) // P, cols]))
            return out + [(n, P, v_nat[:, NT, cols])]

        GROUPS = [(i, t) for t in range(NT) for i in range(2)] + [(1, NT)]

        def lay(copy, g):
            i, t = GROUPS[g]
            src = score[g % 4 // 2][:, g % 2 * BLK:g % 2 * BLK + BLK].rearrange("p (m n) -> p m n", n=P)
            if i:
                return copy(kT[:, :, t, :], src)
            for b in range(2):
                rows = slice(AD * b, AD * b + AD)
                op = copy(qT[rows, b, :, t, :], src[rows])
            return op

        def store(eng, hp):
            eng.wait_ge(scaled, 2 * hp + 3)
            eng.dma_start(io["mix"][1:NT, :, hp * P:(hp + 1) * P].rearrange("t p d -> p t d"),
                          heads[hp % 2][:, :, :, :].rearrange("p t b d -> p t (b d)")).then_inc(pair_out[hp % 2], 16)

        @block.sync
        def _(sp):
            sp.dma_start(window[:, :], io["window"]).then_inc(const_in, 16)
            sp.dma_start(rowmask[:, :], io["rowmask"]).then_inc(const_in, 16)
            for t in range(NT):
                sp.dma_start(qk_nat[:, t, :, :], io["proj"][t, :, 0:2 * AW].rearrange("p (b n) -> p b n", b=2)).then_inc(tile_in[t // 2], 16)
                sp.dma_start(v_nat[:, t, :], io["proj"][t, :, 2 * AW:3 * AW]).then_inc(tile_in[t // 2], 16)
            sp.dma_start(qk_nat[:, NT, 1, :], io["ck"]).then_inc(tile_in[NT // 2], 16)
            sp.dma_start(v_nat[:, NT, :], io["cv"]).then_inc(tile_in[NT // 2], 16)
            for h in range(AH):
                if h >= 2:
                    sp.wait_ge(biased, AH + LT * (h - 1))
                rows = io["bias_rows"]
                for half in range(2):
                    src = bass.AP(tensor=rows.tensor, offset=h * GRID_W * 15 * 127 + (1 - half) * 127 + GRID_W - 1,
                                  ap=[[15 * 127 - 1, GRID_W], [127, JR], [1, GRID_W]])
                    sp.dma_start(table[h % 2][GRID_W * half:GRID_W * (half + 1), :, :], src).then_inc(table_in[h % 2], 16)
                if h == 1:
                    sp.wait_ge(laid, len(GROUPS))
                    sp.dma_start(w_out, io["w_out"]).then_inc(w_out_in, 16)
            sp.wait_ge(w_out_in, 16)

        @block.gpsimd
        def _(pool):
            pool.wait_ge(const_in, 32)
            link = Links(pool, pool_link)
            for h in range(AH):
                b, s = table[h % 2], inner[h % 2]
                pool.wait_ge(table_in[h % 2], 32 * (h // 2 + 1))
                link.wait(pool.tensor_scalar(b[:, :, :], b[:, :, :], 1 / SCALE, None, ALU.mult))
                link.wait(pool.tensor_tensor(b[:, :, :], b[:, :, :],
                                             window[:, :].rearrange("p (a n) -> p a n", a=1).to_broadcast([P, JR, GRID_W]), ALU.add))
                pool.tensor_tensor(s[:, :, :], b[:, 2:2 + WR + 1, :],
                                   rowmask[:, :].rearrange("p (r a) -> p r a", a=1).to_broadcast([P, WR + 1, GRID_W]), ALU.add)\
                    .then_inc(table_ready, 1)
                if h == 0:
                    pool.wait_ge(scaled, 1)
                    pool.dma_start(io["mix"][0, :, 0:AW], first_rows[:, :, :].rearrange("p h d -> p (h d)")).then_inc(first_out, 16)
                elif h % 2 == 1 and h >= 3:
                    store(pool, (h - 3) // 2)
            store(pool, 3)
            pool.wait_ge(first_out, 16)
            pool.wait_ge(pair_out[0], 32)
            pool.wait_ge(pair_out[1], 32)

        @block.tensor
        def _(pe):
            ident = keep["ident"]
            for g, (i, t) in enumerate(GROUPS):
                bank = score[g % 4 // 2][:, (g % 2) * BLK:(g % 2 + 1) * BLK]
                if g >= 4:
                    pe.wait_ge((laid_vec, laid_act)[g % 2], g // 2 - 1)
                pe.wait_ge(tile_in[t // 2], 64)
                for hp in range(HP):
                    mm = pe.transpose(bank[:, hp * P:(hp + 1) * P], qk_nat[:, t, i, hp * P:(hp + 1) * P], ident[:, :])
                mm.then_inc(laid, 1)
            pe.wait_ge(laid_vec, (len(GROUPS) + 1) // 2)
            pe.wait_ge(laid_act, len(GROUPS) // 2)

            def raw_scores(n):
                h, t = units[n]
                if n >= 2:
                    pe.wait_ge(biased, n - 1)
                q = qT[:, h % 2, h // 2, t, :]
                for c, k, keys in pieces(h, t):
                    mm = pe.matmul(score[n % 2][:, c:c + k], q, keys, start=True, stop=True)
                mm.then_inc(scored, 1)

            def turn_probs(n):
                h, t = units[n]
                pe.wait_ge(expd, n + 1)
                if n >= 1:
                    pe.wait_ge(taken[0], n)
                bl = blocks(h, t)
                for b, (c, k, _) in enumerate(bl):
                    if b == 4:
                        pe.wait_ge(taken[1], n)
                    mm = pe.transpose(turn[b // 4][0:k, b % 4, :], prob[n % 3][:, c:c + k], ident[:, :])
                    if b == min(3, len(bl) - 1):
                        mm.then_inc(turned[0], 1)
                if len(bl) > 4:
                    mm.then_inc(turned[1], 1)

            def values(n):
                h, t = units[n]
                bank = 0 if n < AH else (h + 1) % 2
                slot = h if n < AH else t - 1
                if n >= AH and slot == 0 and h >= 1:
                    pe.wait_ge(scaled, h)
                pe.wait_ge(taken[0], n + 1)
                pe.wait_ge(taken[1], n + 1)
                bl = blocks(h, t)
                for b, (c, k, v) in enumerate(bl):
                    mm = pe.matmul(outp[bank][:, slot, :], probT[n % 2][0:k, b, :], v, start=(b == 0), stop=(b == len(bl) - 1))
                mm.then_inc(summed, 1)

            for n in range(N + 2):
                if n < N:
                    raw_scores(n)
                if 1 <= n <= N:
                    turn_probs(n - 1)
                if n >= 2:
                    values(n - 2)

        @block.scalar
        def _(act):
            for g in range(1, len(GROUPS), 2):
                act.wait_ge(laid, g + 1)
                lay(lambda to, src: act.activation(to, src, ACT.Copy), g).then_inc(laid_act, 1)

            def exps(n):
                h, t = units[n]
                w = local_cols(t) + P
                act.wait_ge(biased, n + 1)
                p = prob[n % 3][:, 0:w]
                act.activation(p, p, ACT.Exp, scale=-1.0, bias=low[:, n, 1:2], accum_out=total[:, n:n + 1]).then_inc(expd, 1)

            def take(n):
                h, t = units[n]
                if t == 0:
                    act.wait_ge(expd, n + 1)
                    act.activation(low[0:1, n, 0:1], low[0:1, n, 1:2], ACT.Copy).then_inc(taken[1], 1)
                    return
                act.wait_ge(turned[1], n - AH + 1)
                if n >= 2:
                    act.wait_ge(summed, n - 1)
                bl = blocks(h, t)[4:]
                for b, (c, k, _) in enumerate(bl):
                    if len(bl) == 1 or k < P:
                        op = act.activation(probT[n % 2][0:k, 4 + b, :], turn[1][0:k, b, :], ACT.Copy)
                    else:
                        op = act.activation(probT[n % 2][:, 4 + b, :], turn[1][:, b, :], ACT.Copy)
                op.then_inc(taken[1], 1)

            for n in range(N + 1):
                if n < N:
                    exps(n)
                if n >= 1:
                    take(n - 1)

        @block.vector
        def _(dve):
            link = Links(dve, vec_link)
            link.wait(dve.memset(zeros[:, :], 0.0))
            dve.memset(qT[AD:P, 0, :, :, :], 0.0)
            dve.memset(qT[0:AD, 1, :, :, :], 0.0)
            for g in range(0, len(GROUPS), 2):
                dve.wait_ge(laid, g + 1)
                lay(dve.tensor_copy, g).then_inc(laid_vec, 1)

            def bias(n):
                h, t = units[n]
                dve.wait_ge(scored, n + 1)
                if n >= 3:
                    dve.wait_ge(turned[0], n - 2)
                    if n - 3 >= AH:
                        dve.wait_ge(turned[1], n - 2 - AH)
                w = local_cols(t)
                s, p = score[n % 2], prob[n % 3]
                start = 3e38
                if t:
                    _, nr, j0, differ = WINDOWS[t - 1]
                    if t == 1:
                        dve.wait_ge(table_ready, h + 1)
                    tab = inner[h % 2][:, 0:nr, :] if differ else table[h % 2][:, j0:j0 + nr, :]
                    link.wait(dve.tensor_tensor_reduce(p[:, 0:w], s[:, 0:w], tab.rearrange("p r n -> p (r n)"), -SCALE, start,
                                                       ALU.add, ALU.min, low[:, n, 0:1]))
                    start = low[:, n, 0:1]
                dve.tensor_tensor_reduce(p[:, w:w + P], s[:, w:w + P], zeros[:, :], -SCALE, start,
                                         ALU.add, ALU.min, low[:, n, 1:2]).then_inc(biased, 1)

            def take(n):
                h, t = units[n]
                dve.wait_ge(turned[0], n + 1)
                if n >= 2:
                    dve.wait_ge(summed, n - 1)
                nb = 4 if t else 1
                dve.tensor_copy(probT[n % 2][:, 0:nb, :], turn[0][:, 0:nb, :]).then_inc(taken[0], 1)

            def scale(g):
                c = slice(8 * g, 8 * g + 8)
                link.wait(dve.reciprocal(total[:, c], total[:, c]))
                dve.wait_ge(summed, 8 * g + 8)
                h = g - 1
                dst = first_rows[:, :, :] if g == 0 else heads[h // 2 % 2][:, :, h % 2, :]
                if g and h // 2 >= 2:
                    dve.wait_ge(pair_out[h // 2 % 2], 16)
                dve.tensor_tensor(dst, outp[g % 2][:, :, :], total[:, c].rearrange("p (t a) -> p t a", a=1).to_broadcast([P, 8, AD]),
                                  ALU.mult).then_inc(scaled, 1)

            for n in range(N + 2):
                if n < N:
                    bias(n)
                if 1 <= n <= N:
                    take(n - 1)
                if n >= 9 and (n - 9) % 8 == 1:
                    scale((n - 10) // 8)
            if (N + 1 - 9) % 8 != 1:
                scale(N // 8 - 1)



GAP = 2
TW = CTX + GAP + LAT
CUTS = [(0, CTX + GAP + 2 * P), (CTX + GAP + 2 * P, 3 * P), (CTX + GAP + 5 * P, 3 * P)]


def column_of(t):
    return t * P + (GAP if t else 0)


def output_projection(nc, io, keep):
    with ExitStack() as ctx:
        def sb(name, shape):
            return ctx.enter_context(nc.sbuf_tensor(name, shape, F32))

        def ps(name, shape):
            return ctx.enter_context(nc.psum_tensor(name, shape, F32))

        def sem(name):
            return ctx.enter_context(nc.semaphore(name))

        w = keep["space"][:, 0:KT * D].rearrange("p (k n) -> p k n", k=KT)
        mt = [sb(f"op_mix{j}", [P, MIX]) for j in range(3)]
        xt = [sb(f"op_x{j}", [P, D]) for j in range(3)]
        mT = [sb(f"op_mixT{j}", [P, KT, P]) for j in range(2)]
        x1 = [sb(f"op_x1{j}", [P, D]) for j in range(2)]
        xn = [sb(f"op_xn{j}", [P, D]) for j in range(2)]
        junk = sb("op_junk", [P, D])
        h2 = [sb(f"op_h2{g}", [P, 4, P]) for g in range(2)]
        stat = sb("op_stat", [P, NT, 2])
        zeros = sb("op_zeros", [P, KT * GAP])
        tp = [ps(f"op_tp{j}", [P, 4, P]) for j in range(4)]
        acc = [ps(f"op_acc{j}", [P, BLK]) for j in range(4)]
        w_up_in = sem("op_w_up_in")
        t_in = [sem(f"op_t_in{j}") for j in range(3)]
        turned = sem("op_turned")
        turned_read = sem("op_turned_read")
        acc_done = sem("op_acc_done")
        gated = sem("op_gated")
        x1_done = sem("op_x1_done")
        squares = sem("op_squares")
        mean_sq = sem("op_mean_sq")
        rstd = sem("op_rstd")
        xn_done = sem("op_xn_done")
        xn_turned = sem("op_xn_turned")
        xn_read = sem("op_xn_read")
        h2_hi = sem("op_h2_hi")
        h2_lo = sem("op_h2_lo")
        x1_out = [sem(f"op_x1_out{j}") for j in range(2)]
        block = ctx.enter_context(nc.Block())

        @block.sync
        def _(sp):
            for t in range(NT):
                if t >= 3:
                    sp.wait_ge(x1_done, t - 2)
                    sp.wait_ge(turned, 2 * t - 4)
                sp.dma_start(mt[t % 3][:, :], io["mix"][t]).then_inc(t_in[t % 3], 16)
                sp.dma_start(xt[t % 3][:, :], io["x"][t]).then_inc(t_in[t % 3], 16)
            sp.dma_start(keep["w_up"][:, :, :, :], io["w_up"][0]).then_inc(w_up_in, 16)
            sp.wait_ge(w_up_in, 16)

        @block.gpsimd
        def _(pool):
            for t in range(NT):
                pool.wait_ge(x1_done, t + 1)
                pool.dma_start(io["x1"][t], x1[t % 2][:, :]).then_inc(x1_out[t % 2], 16)
                pool.wait_ge(mean_sq, t + 1)
                pool.tensor_tensor(stat[:, t, 1:2], stat[:, t, 1:2], keep["half"][:, 0:1], ALU.pow).then_inc(rstd, 1)
            pool.wait_ge(x1_out[0], 16 * ((NT + 1) // 2))
            pool.wait_ge(x1_out[1], 16 * (NT // 2))

        @block.tensor
        def _(pe):
            def turn(t):
                pe.wait_ge(t_in[t % 3], 32 * (t // 3 + 1))
                for g in range(2):
                    if t:
                        pe.wait_ge(turned_read, 2 * (t - 1) + g + 1)
                    for k in range(4):
                        mm = pe.transpose(tp[g][:, k, :], mt[t % 3][:, (4 * g + k) * P:(4 * g + k + 1) * P], keep["ident"][:, :])
                    mm.then_inc(turned, 1)

            def turn_xn(t):
                pe.wait_ge(xn_done, t + 1)
                for g in range(2):
                    if t:
                        pe.wait_ge(xn_read, 2 * (t - 1) + g + 1)
                    for k in range(4):
                        mm = pe.transpose(tp[2 + g][:, k, :], xn[t % 2][:, (4 * g + k) * P:(4 * g + k + 1) * P], keep["ident"][:, :])
                    mm.then_inc(xn_turned, 1)

            turn(0)
            for t in range(NT):
                if t + 1 < NT:
                    turn(t + 1)
                pe.wait_ge(turned_read, 2 * t + 2)
                for b in range(2):
                    n = 2 * t + b
                    if n >= 4:
                        pe.wait_ge(gated, n - 3)
                    for k in range(KT):
                        mm = pe.matmul(acc[n % 4][:, :], mT[t % 2][:, k, :], w[:, k, b * BLK:(b + 1) * BLK], start=(k == 0), stop=(k == KT - 1))
                    mm.then_inc(acc_done, 1)
                if t:
                    turn_xn(t - 1)
            turn_xn(NT - 1)

        @block.scalar
        def _(act):
            def square(t):
                act.wait_ge(x1_done, t + 1)
                act.activation(junk[:, :], x1[t % 2][:, :], ACT.Square, accum_out=stat[:, t, 0:1]).then_inc(squares, 1)

            def high(t):
                for g in range(2):
                    act.wait_ge(xn_read, 2 * t + g + 1)
                    act.activation(keep["h2h"][:, 4 * g:4 * g + 4, column_of(t):column_of(t) + P], h2[g][:, :, :], ACT.Copy)\
                       .then_inc(h2_hi, 1)

            for t in range(NT):
                for g in range(2):
                    act.wait_ge(turned, 2 * t + g + 1)
                    if t >= 2:
                        act.wait_ge(acc_done, 2 * t - 2)
                    act.activation(mT[t % 2][:, 4 * g:4 * g + 4, :], tp[g][:, :, :], ACT.Copy).then_inc(turned_read, 1)
                if t:
                    square(t - 1)
                if t >= 2:
                    high(t - 2)
            square(NT - 1)
            high(NT - 2)
            high(NT - 1)

        @block.vector
        def _(dve):
            dve.memset(zeros[:, :], 0.0).then_inc(h2_lo, 1)
            dve.wait_ge(h2_lo, 1)
            z = zeros[:, :].rearrange("p (k n) -> p k n", k=KT)
            dve.tensor_copy(keep["h2h"][:, :, CTX:CTX + GAP], z)
            dve.tensor_copy(keep["h2l"][:, :, CTX:CTX + GAP], z)

            def modulate(t):
                v = 1 if t else 0
                for k in range(KT):
                    if k % 4 == 0:
                        if t:
                            dve.wait_ge(h2_lo, 2 * (t - 1) + k // 4 + 2)
                        dve.wait_ge(xn_turned, 2 * t + k // 4 + 1)
                    op = dve.tensor_scalar(h2[k // 4][:, k % 4, :], tp[2 + k // 4][:, k % 4, :],
                                           keep["gain"][:, 1, k, v:v + 1], keep["mod"][:, 3 * KT + k, v:v + 1], ALU.mult, ALU.add)
                    if k % 4 == 3:
                        op.then_inc(xn_read, 1)

            def low(t):
                for g in range(2):
                    dve.wait_ge(h2_hi, 2 * t + g + 1)
                    at = slice(column_of(t), column_of(t) + P)
                    dve.tensor_tensor(keep["h2l"][:, 4 * g:4 * g + 4, at], h2[g][:, :, :],
                                      keep["h2h"][:, 4 * g:4 * g + 4, at].bitcast(F32), ALU.subtract).then_inc(h2_lo, 1)

            for t in range(NT):
                j, v = t % 2, 1 if t else 0
                dve.wait_ge(t_in[t % 3], 32 * (t // 3 + 1))
                if t >= 2:
                    dve.wait_ge(x1_out[j], 16 * (t // 2))
                    dve.wait_ge(squares, t - 1)
                for b in range(2):
                    n, at = 2 * t + b, slice(b * BLK, (b + 1) * BLK)
                    dve.wait_ge(acc_done, n + 1)
                    dve.tensor_tensor(x1[j][:, at], acc[n % 4][:, :], keep["gate"][:, v, at], ALU.mult).then_inc(gated, 1)
                dve.wait_ge(gated, 2 * t + 2)
                dve.tensor_tensor(x1[j][:, :], x1[j][:, :], xt[t % 3][:, :], ALU.add).then_inc(x1_done, 1)
                if t >= 2:
                    low(t - 2)
                if t:
                    modulate(t - 1)
                dve.wait_ge(squares, t + 1)
                dve.tensor_scalar(stat[:, t, 1:2], stat[:, t, 0:1], 1.0 / D, EPS, ALU.mult, ALU.add).then_inc(mean_sq, 1)
                dve.wait_ge(rstd, t + 1)
                if t >= 2:
                    dve.wait_ge(xn_turned, 2 * t - 2)
                dve.tensor_scalar(xn[j][:, :], x1[j][:, :], stat[:, t, 1:2], None, ALU.mult).then_inc(xn_done, 1)
            low(NT - 2)
            modulate(NT - 1)
            low(NT - 1)


def mlp_up(nc, io, keep):
    with ExitStack() as ctx:
        def sb(name, shape, dt=F32):
            return ctx.enter_context(nc.sbuf_tensor(name, shape, dt))

        def ps(name, shape):
            return ctx.enter_context(nc.psum_tensor(name, shape, F32))

        def sem(name):
            return ctx.enter_context(nc.semaphore(name))

        space, used = keep["space"], [0]

        def piece(n):
            used[0] += n
            return space[:, used[0] - n:used[0]]

        w = [keep["w_up"], piece(KT * 2 * P).rearrange("p (k b n) -> p k b n", k=KT, b=2)]
        wh = [sb(f"up_wh{j}", [P, KT, 2, P], F32R) for j in range(2)]
        wl = [sb(f"up_wl{j}", [P, KT, 2, P], F32R) for j in range(2)]
        cw = sb("up_convw", [P, FT, 2, 3])
        cb = sb("up_convb", [P, FT, 2])
        u = [piece(TW + 2) for j in range(2)]
        conv = [piece(TW) for j in range(2)]
        assert used[0] <= KT * D
        g = [sb(f"up_g{j}", [P, TW]) for j in range(2)]
        acc = [[ps(f"up_acc{i}_{c}", [P, BLK]) for c in range(3)] for i in range(2)]
        const_in = sem("up_const_in")
        w_in = [sem(f"up_w_in{j}") for j in range(2)]
        w_hi = sem("up_w_hi")
        w_lo = sem("up_w_lo")
        acc_done = sem("up_acc_done")
        acc_read = sem("up_acc_read")
        conv_done = sem("up_conv_done")
        silu_done = sem("up_silu_done")
        g_done = sem("up_g_done")
        g_out = [sem(f"up_g_out{j}") for j in range(2)]
        edges = sem("up_edges")
        vec_link = sem("up_vec_link")
        block = ctx.enter_context(nc.Block())
        h2h, h2l = keep["h2h"], keep["h2l"]

        @block.sync
        def _(sp):
            def load(f, j):
                sp.dma_start(w[j][:, :, :, :], io["w_up"][bass.ds(f, 1)].rearrange("a p k b n -> (a p) k b n")).then_inc(w_in[j], 16)

            def store(f, j):
                sp.wait_ge(g_done, f + 1)
                for t0, nt in ((0, 1), (1, NT - 1)):
                    at = column_of(t0)
                    sp.dma_start(io["g"][t0:t0 + nt, :, bass.ds(f, 1), :].rearrange("t p a n -> (a p) t n"),
                                 g[j][:, at:at + nt * P].rearrange("p (t n) -> p t n", n=P)).then_inc(g_out[j], 16)

            load(1, 1)
            sp.dma_start(cw[:, :, :, :], io["convw"]).then_inc(const_in, 16)
            sp.dma_start(cb[:, :, :], io["convb"]).then_inc(const_in, 16)
            with sp.Fori(1, FT // 2) as v:
                for j in range(2):
                    f = v * 2 + j
                    sp.wait_ge(w_lo, f - 1)
                    load(f, j)
                    store(f - 2, j)
            for j in range(2):
                store(FT - 2 + j, j)
            for j in range(2):
                sp.wait_ge(g_out[j], 16 * FT)

        @block.tensor
        def _(pe):
            def tile(f, j, warm):
                pe.wait_ge(w_lo, f + 1)
                for i in range(2):
                    for c, (c0, cn) in enumerate(CUTS):
                        if warm:
                            pe.wait_ge(acc_read, 6 * f - 6 + 3 * i + c + 1)
                        for k in range(KT):
                            for part, (a, b) in enumerate(((wh, h2h), (wh, h2l), (wl, h2h))):
                                mm = pe.matmul(acc[i][c][:, 0:cn], a[j][:, k, i, :], b[:, k, c0:c0 + cn],
                                               start=(k == 0 and part == 0), stop=(k == KT - 1 and part == 2))
                        mm.then_inc(acc_done, 1)

            tile(0, 0, False)
            tile(1, 1, True)
            with pe.Fori(1, FT // 2) as v:
                for j in range(2):
                    tile(v * 2 + j, j, True)

        @block.scalar
        def _(act):
            act.wait_ge(edges, 1)

            def high(f, j, warm):
                if warm or j:
                    act.wait_ge(w_in[j], f * 8 + 8 * j)
                if warm:
                    act.wait_ge(acc_done, 6 * f - 6)
                act.activation(wh[j][:, :, :, :], w[j][:, :, :, :], ACT.Copy).then_inc(w_hi, 1)

            def half_tile(f, i, warm):
                for c, (c0, cn) in enumerate(CUTS):
                    act.wait_ge(acc_done, 6 * f + 3 * i + c + 1)
                    if warm and c == 0:
                        act.wait_ge(conv_done, 2 * f - 1 + i)
                    act.activation(u[i][:, 1 + c0:1 + c0 + cn], acc[i][c][:, 0:cn], ACT.Copy).then_inc(acc_read, 1)

            def silu(f):
                act.wait_ge(conv_done, 2 * f + 1)
                act.activation(conv[0][:, :], conv[0][:, :], ACT.Silu).then_inc(silu_done, 1)

            def tile(f, j, warm, more):
                half_tile(f, 0, warm)
                if more:
                    high(f + 1, 1 - j, True)
                half_tile(f, 1, warm)
                silu(f)

            high(0, 0, False)
            high(1, 1, False)
            half_tile(0, 0, False)
            half_tile(0, 1, False)
            silu(0)
            with act.Fori(0, FT // 2 - 1) as v:
                for j in range(2):
                    f = v * 2 + 1 + j
                    tile(f, 1 - j, True, True)
            tile(FT - 1, 1, True, False)

        @block.vector
        def _(dve):
            for i in range(2):
                dve.memset(u[i][:, 0:1], 0.0)
                op = dve.memset(u[i][:, TW + 1:TW + 2], 0.0)
            op.then_inc(edges, 1)
            link = Links(dve, vec_link)
            PER = 4

            def low(f, j):
                dve.wait_ge(w_hi, f + 1)
                dve.tensor_tensor(wl[j][:, :, :, :], w[j][:, :, :, :], wh[j][:, :, :, :].bitcast(F32), ALU.subtract).then_inc(w_lo, 1)

            def tile(f, j, warm, more):
                link.start(PER * f)
                for i in range(2):
                    dve.wait_ge(acc_read, 6 * f + 3 * i + 3)
                    if warm:
                        dve.wait_ge(g_done, f)
                    at = bass.ds(f, 1)

                    def tap(n):
                        return cw[:, at, i, n:n + 1].rearrange("p a n -> p (a n)")

                    link.wait(dve.tensor_scalar(conv[i][:, :], u[i][:, 1:TW + 1], tap(1), cb[:, at, i], ALU.mult, ALU.add))
                    link.wait(dve.scalar_tensor_tensor(out=conv[i][:, :], in0=u[i][:, 0:TW], scalar=tap(0), in1=conv[i][:, :],
                                                       op0=ALU.mult, op1=ALU.add))
                    dve.scalar_tensor_tensor(out=conv[i][:, :], in0=u[i][:, 2:TW + 2], scalar=tap(2), in1=conv[i][:, :],
                                             op0=ALU.mult, op1=ALU.add).then_inc(conv_done, 1)
                    if i == 0 and more:
                        low(f + 1, 1 - j)
                assert link.k == PER
                dve.wait_ge(silu_done, f + 1)
                dve.wait_ge(conv_done, 2 * f + 2)
                if not isinstance(f, int) or f >= 2:
                    dve.wait_ge(g_out[j], 16 * (f - j))
                dve.tensor_tensor(g[j][:, :], conv[0][:, :], conv[1][:, :], ALU.mult).then_inc(g_done, 1)

            low(0, 0)
            low(1, 1)
            dve.wait_ge(const_in, 32)
            tile(0, 0, False, False)
            tile(1, 1, True, True)
            with dve.Fori(1, FT // 2 - 1) as v:
                for j in range(2):
                    tile(v * 2 + j, j, True, True)
            tile(FT - 2, 0, True, True)
            tile(FT - 1, 1, True, False)


def mlp_down(nc, io, keep):
    FS = 2
    PC = FT // FS
    with ExitStack() as ctx:
        def sb(name, shape, dt=F32):
            return ctx.enter_context(nc.sbuf_tensor(name, shape, dt))

        def sem(name):
            return ctx.enter_context(nc.semaphore(name))

        w = [sb(f"dn_w{j}", [P, FS, BLK]) for j in range(3)]
        wh = sb("dn_wh", [P, FT, BLK], F32R)
        wl = sb("dn_wl", [P, FT, BLK], F32R)
        g = [sb(f"dn_g{j}", [P, FT, P]) for j in range(2)]
        gh = [sb(f"dn_gh{j}", [P, FT, P], F32R) for j in range(2)]
        gl = [sb(f"dn_gl{j}", [P, FT, P], F32R) for j in range(2)]
        x1 = [sb(f"dn_x1{j}", [P, BLK]) for j in range(2)]
        tmp = sb("dn_tmp", [P, BLK])
        acc = [ctx.enter_context(nc.psum_tensor(f"dn_acc{j}", [P, BLK], F32)) for j in range(2)]
        gate_in = sem("dn_gate_in")
        w_in = [sem(f"dn_w_in{j}") for j in range(3)]
        g_in = [sem(f"dn_g_in{j}") for j in range(2)]
        w_hi = sem("dn_w_hi")
        w_lo = sem("dn_w_lo")
        g_hi = sem("dn_g_hi")
        g_lo = sem("dn_g_lo")
        multiplied = sem("dn_multiplied")
        gated = sem("dn_gated")
        added = sem("dn_added")
        x_in = [sem(f"dn_x_in{j}") for j in range(2)]
        y_out = [sem(f"dn_y_out{j}") for j in range(2)]
        block = ctx.enter_context(nc.Block())

        def units(eng, unit):
            for h in range(2):
                for t in range(3):
                    unit(h, t, (h + t) % 2, h == 1 or t == 2)
                with eng.Fori(1, NT // 2) as u:
                    for i in range(2):
                        unit(h, u * 2 + 1 + i, (h + 1 + i) % 2, True)

        def number(h, t):
            return t + NT * h

        def columns(h):
            return slice(h * BLK, (h + 1) * BLK)

        @block.sync
        def _(sp):
            def store(q, h, t, j):
                sp.wait_ge(added, q + 1)
                sp.dma_start(tile_rows(io["y"], t)[:, columns(h)], x1[j][:, :]).then_inc(y_out[j], 16)

            def load_w(first, last):
                for r in range(first, last):
                    i = r % PC
                    if r >= 3:
                        sp.wait_ge(w_lo, r - 2)
                    sp.dma_start(w[r % 3][:, :, :], io["w_down"][r // PC, :, FS * i:FS * i + FS]).then_inc(w_in[r % 3], 16)

            def load_g(q, t, j, warm):
                if warm:
                    sp.wait_ge(g_lo, q - 1)
                sp.dma_start(g[j][:, :, :], io["g"][bass.ds(t, 1)].rearrange("a p f n -> (a p) f n")).then_inc(g_in[j], 16)

            def unit(h, t, j, warm):
                q = number(h, t)
                if not isinstance(t, int) or t != 1:
                    load_g(q, t, j, warm)
                if warm:
                    if isinstance(t, int) and t < 2:
                        store(q - 2, 0, NT - 2 + t, j)
                    else:
                        store(q - 2, h, t - 2, j)
                    sp.wait_ge(y_out[j], q * 8 - 8 * j)
                if isinstance(t, int) and t == 0:
                    first, cut, last = (PC + 3, PC + 3, 2 * PC) if h else (1, 5, PC + 3)
                    load_w(first, cut)
                    load_g(q + 1, 1, 1 - j, warm)
                    load_w(cut, last)
                sp.dma_start(x1[j][:, :], tile_rows(io["x1"], t)[:, columns(h)]).then_inc(x_in[j], 16)

            load_w(0, 1)
            units(sp, unit)
            for t in range(NT - 2, NT):
                store(NT + t, 1, t, (NT + t) % 2)
            for j in range(2):
                sp.wait_ge(y_out[j], 16 * NT)

        @block.gpsimd
        def _(pool):
            pool.dma_start(keep["gate"][:, :, :], io["gate2"]).then_inc(gate_in, 16)

        @block.tensor
        def _(pe):
            def unit(h, t, j, warm):
                q = number(h, t)
                pe.wait_ge(g_lo, q + 1)
                if warm:
                    pe.wait_ge(gated, q - 1)
                for f in range(FT):
                    if f % FS == 0 and isinstance(t, int) and t == 0:
                        pe.wait_ge(w_lo, PC * h + f // FS + 1)
                    for part, (a, b) in enumerate(((gh, wh), (gh, wl), (gl, wh))):
                        mm = pe.matmul(acc[j][:, :], a[j][:, f, :], b[:, f, :],
                                       start=(f == 0 and part == 0), stop=(f == FT - 1 and part == 2))
                    if f % FS == FS - 1:
                        mm.then_inc(multiplied, 1)

            units(pe, unit)

        @block.scalar
        def _(act):
            def high_w(h, first, last):
                for i in range(first, last):
                    r = PC * h + i
                    act.wait_ge(w_in[r % 3], 16 * (r // 3 + 1))
                    if h:
                        act.wait_ge(multiplied, PC * (NT - 1) + i + 1)
                    act.activation(wh[:, FS * i:FS * i + FS, :], w[r % 3][:, :, :], ACT.Copy).then_inc(w_hi, 1)

            def unit(h, t, j, warm):
                q = number(h, t)
                act.wait_ge(g_in[j], q * 8 - 8 * j + 16)
                if warm:
                    act.wait_ge(multiplied, q * PC - PC)
                act.activation(gh[j][:, :, :], g[j][:, :, :], ACT.Copy).then_inc(g_hi, 1)
                if isinstance(t, int) and t == 0:
                    high_w(h, 0 if h else 1, PC)

            high_w(0, 0, 1)
            units(act, unit)

        @block.vector
        def _(dve):
            def low_w(h, first, last):
                for i in range(first, last):
                    r = PC * h + i
                    dve.wait_ge(w_hi, r + 1)
                    at = slice(FS * i, FS * i + FS)
                    dve.tensor_tensor(wl[:, at, :], w[r % 3][:, :, :], wh[:, at, :].bitcast(F32), ALU.subtract).then_inc(w_lo, 1)

            def finish(q, h, v, j):
                if not isinstance(q, int) or q:
                    dve.wait_ge(added, q)
                dve.wait_ge(gate_in, 16)
                dve.wait_ge(multiplied, q * PC + PC)
                dve.tensor_tensor(tmp[:, :], acc[j][:, :], keep["gate"][:, v, columns(h)], ALU.mult).then_inc(gated, 1)
                dve.wait_ge(gated, q + 1)
                dve.wait_ge(x_in[j], q * 8 - 8 * j + 16)
                dve.tensor_tensor(x1[j][:, :], x1[j][:, :], tmp[:, :], ALU.add).then_inc(added, 1)

            def unit(h, t, j, warm):
                q = number(h, t)
                dve.wait_ge(g_hi, q + 1)
                dve.tensor_tensor(gl[j][:, :, :], g[j][:, :, :], gh[j][:, :, :].bitcast(F32), ALU.subtract).then_inc(g_lo, 1)
                if isinstance(t, int) and t == 0:
                    low_w(h, 0 if h else 1, PC)
                if not isinstance(t, int) or t:
                    finish(q - 1, h, 0 if isinstance(t, int) and t == 1 else 1, 1 - j)
                elif h:
                    finish(q - 1, 0, 1, 1 - j)

            low_w(0, 0, 1)
            units(dve, unit)
            finish(2 * NT - 1, 1, 1, 1)



def shape_constants():
    import numpy as np
    f = np.float32
    tri = np.tril(np.ones((P, P), bool))
    pos = np.arange(LAT)
    quarter = MD // 4
    freq = (10000.0 ** (-np.arange(quarter, dtype=f) / f(quarter))).astype(f)
    cos = np.ones((P, NT, 2, 2, quarter), f)
    sin = np.zeros((P, NT, 2, 2, quarter), f)
    for g, p in enumerate((pos // GRID_W, pos % GRID_W)):
        ang = (p.astype(f)[:, None] * freq[None, :]).reshape(NT - 1, P, quarter).transpose(1, 0, 2)
        for a in range(2):
            cos[:, 1:, g, a] = np.cos(ang)
            sin[:, 1:, g, a] = np.sin(ang) * (1 if a else -1)
    sel = np.zeros((2, 2, P), f)
    sel[0, 0] = sel[1, 1] = 1
    col = np.arange(GRID_W)
    cs = np.clip(col - 8, 0, GRID_W - 16)
    inside = (col[None, :] >= cs[:, None]) & (col[None, :] < cs[:, None] + 16)
    window = np.tile(np.where(inside, f(0), f(NEG)), (2, 1))
    rowmask = np.zeros((P, 9), f)
    rowmask[:GRID_W, 8] = NEG
    rowmask[GRID_W:, 0] = NEG
    return {"ident": np.eye(P, dtype=f), "flip": np.eye(P, dtype=f)[::-1].copy(),
            "cos": cos.reshape(P, NT, MD), "sin": sin.reshape(P, NT, MD), "sel": sel,
            "causal": np.stack([np.where(tri.T, f(0), f(NEG)), np.where(tri, f(0), f(NEG))], axis=1),
            "window": window, "rowmask": rowmask}


def lay_out(inp):
    import numpy as np
    a = {k: np.asarray(v) for k, v in inp.items()}
    w_in = a["w_in"][0].reshape(KT, P, -1).transpose(1, 0, 2)
    rep = lambda v: np.broadcast_to(v, (P,) + v.shape)
    toe = np.zeros((AH, 15, 127), np.float32)
    toe[:, :, 48:79] = a["rpb"][0]
    out = dict(shape_constants())
    out.update({
        "x": np.concatenate([a["x_prompt"][0], a["x_sample"][0]]).reshape(NT, P, D),
        "cT": np.stack([a["c_ctx"], a["c"][0]], -1).reshape(KT, P, 2).transpose(1, 0, 2),
        "w_mod": a["w_mod"][0].reshape(KT, P, MOD // BLK, BLK).transpose(2, 1, 0, 3),
        "b_mod2": np.broadcast_to(a["b_mod"], (2, MOD)),
        "gains": np.stack([a["norm1_g"][0].reshape(KT, P).T, a["norm2_g"][0].reshape(KT, P).T], 1),
        "w_in": w_in[:, :, :7 * BLK].reshape(P, KT, 7, BLK)[:, :, [AV, MV, MO, AQ, AK, MQ, MK]].transpose(2, 1, 0, 3).reshape(7 * KT, P, BLK),
        "w_gate": w_in[:, :, 7 * BLK:],
        "bg": rep(a["b_gate"][0]),
        "qkg": rep(np.stack([a["q_norm_g"][0], a["k_norm_g"][0]])),
        "ck": a["cache_k"][0, 0].reshape(P, AW), "cv": a["cache_v"][0, 0].reshape(P, AW),
        "toeplitz": toe.reshape(AH, 15 * 127),
        "stC": np.concatenate([a["state_C"][0, 0], a["state_n"][0, 0][..., None]], -1),
        "stm": a["state_m"][0, 0].reshape(1, 2 * MH),
        "mlg": rep(a["ml_norm_g"][0]),
        "w_out": a["w_out"][0].reshape(KT, P, D).transpose(1, 0, 2),
        "w_up": a["w_up"][0].reshape(KT, P, 2, FT, P).transpose(3, 1, 0, 2, 4),
        "convw": a["conv_w"][0].reshape(3, 2, FT, P).transpose(3, 2, 1, 0),
        "convb": a["conv_b"][0].reshape(2, FT, P).transpose(2, 1, 0),
        "w_down": a["w_down"][0].reshape(FT, P, 2, BLK).transpose(2, 1, 0, 3),
    })
    return out



_OUTS = {"y": (NT, P, D), "new_k": (P, AW), "new_v": (P, AW), "new_st": (2, MH, MD, MD + 1), "new_m": (2, MH)}
_SCRATCH = {"proj": (NT, P, 7 * BLK), "mix": (NT, P, MIX), "x1": (NT, P, D), "g": (NT, P, FT, P), "gate2": (P, 2, D), "mrows": (2, 2, 16, MH, P),
            "bias_rows": (AH, GRID_W, 15 * 127)}


def program(nc, io):
    with ExitStack() as ctx:
        def keeping(name, shape):
            keep[name] = ctx.enter_context(nc.sbuf_tensor("keep_" + name, shape, F32))

        keep = {}
        keeping("ident", [P, P])
        keeping("mod", [P, MOD // P, 2])
        keeping("gain", [P, 2, KT, 2])
        keeping("gate", [P, 2, D])
        keeping("half", [P, NT])
        keeping("gates", [P, NT, NG])
        modulation(nc, io, keep)
        projection(nc, io, keep)
        mlstm(nc, io, keep)
        with ExitStack() as mixer:
            keep["space"] = mixer.enter_context(nc.sbuf_tensor("keep_space", [P, (NT + 1) * 2 * AW], F32))
            keep["w_up"] = keep["space"][:, KT * D:].rearrange("p (k b n) -> p k b n", k=KT, b=2)
            attention(nc, io, keep)
            for part in ("h2h", "h2l"):
                keep[part] = mixer.enter_context(nc.sbuf_tensor("keep_" + part, [P, KT, TW], F32R))
            output_projection(nc, io, keep)
            mlp_up(nc, io, keep)
        mlp_down(nc, io, keep)


def kernel(**inputs):
    import numpy as _np
    import concourse.bacc as _bacc
    from concourse import mybir as _mybir
    from concourse.bass_utils import run_bass_kernel_spmd as _run

    nc = _bacc.Bacc("TRN2", target_bir_lowering=False, num_devices=1)
    arrays, io = {}, {}
    for name, a in lay_out(inputs).items():
        a = _np.ascontiguousarray(a)
        arrays[f"in_{name}"] = a
        io[name] = nc.dram_tensor(f"in_{name}", a.shape, _mybir.dt.from_np(a.dtype), kind="ExternalInput").ap()
    for name, shape in _OUTS.items():
        io[name] = nc.dram_tensor(f"out_{name}", shape, _mybir.dt.float32, kind="ExternalOutput").ap()
    for name, shape in _SCRATCH.items():
        io[name] = nc.dram_tensor(f"scratch_{name}", shape, _mybir.dt.float32, kind="Internal").ap()
    program(nc, io)
    got = _run(nc, [arrays], core_ids=[0]).results[0]
    y = got["out_y"].reshape(CTX + LAT, D)
    st = got["out_new_st"]
    return (y[None, :CTX], y[None, CTX:], got["out_new_k"].reshape(1, 1, CTX, AH, AD), got["out_new_v"].reshape(1, 1, CTX, AH, AD),
            st[None, None, ..., :MD], st[None, None, ..., MD], got["out_new_m"].reshape(1, 1, 2, MH))
```
